# Optimizing a Trainium2 kernel written in Bass

```python
import jax, jax.numpy as jnp
from jax import lax
import numpy as np

D_MODEL = 2048
BATCH = 1
SEQ = 512
DEPTH = 1

GRID_W = 64
CTX_LEN = 256
HEAD_DIM = 128
A_Q_HEADS = 6
A_KV_HEADS = 2
B_Q_HEADS = 6
B_KV_HEADS = 2
CONV_CH = D_MODEL - (A_Q_HEADS + B_Q_HEADS) * HEAD_DIM
CONV_WIDTH = 3
WINDOW = 128
Q_BLOCK = 128
ROPE_BASE = 10000.0
ROPE_PAIRS = HEAD_DIM // 4
NORM_EPS = 1e-6
NEG_INF = -1e30
ATTN_SCALE = HEAD_DIM ** -0.5
FFN_HIDDEN = ((8 * D_MODEL + 3 * 256 - 1) // (3 * 256)) * 256

KV_W_A = A_KV_HEADS * HEAD_DIM
KV_W_B = B_KV_HEADS * HEAD_DIM
OFF_AK = 0
OFF_AV = OFF_AK + KV_W_A
OFF_BK = OFF_AV + KV_W_A
OFF_BV = OFF_BK + KV_W_B
KV_COLS = OFF_BV + KV_W_B
OFF_AQ = KV_COLS
OFF_BQ = OFF_AQ + A_Q_HEADS * HEAD_DIM
OFF_CONV = OFF_BQ + B_Q_HEADS * HEAD_DIM
IN_COLS = OFF_CONV + 3 * CONV_CH
N_MOD = 6

kernel_name = "hybrid_parallel_groups_dit_block"

def rms_norm(x, g):
    xf = x.astype(jnp.float32)
    y = xf * lax.rsqrt(jnp.mean(xf * xf, axis=-1, keepdims=True) + NORM_EPS)
    return (y * g.astype(jnp.float32)).astype(x.dtype)

def cols(t, start, width):
    return t[..., start:start + width]

def split_heads(t, n_heads):
    return t.reshape(*t.shape[:-1], n_heads, HEAD_DIM)

def axial_rope_tables(rows):
    row = jnp.repeat(jnp.arange(rows, dtype=jnp.int32), GRID_W)
    col = jnp.tile(jnp.arange(GRID_W, dtype=jnp.int32), rows)
    inv_freq = jnp.power(ROPE_BASE, -jnp.arange(ROPE_PAIRS, dtype=jnp.float32) / ROPE_PAIRS)
    ang = jnp.stack([row, col], axis=1).astype(jnp.float32)[:, :, None] * inv_freq
    return jnp.cos(ang), jnp.sin(ang)

def apply_axial_rope(x, cos, sin):
    xs = x.astype(jnp.float32).reshape(*x.shape[:-1], 2, 2, ROPE_PAIRS)
    x1, x2 = xs[..., 0, :], xs[..., 1, :]
    c, s = cos[:, None], sin[:, None]
    out = jnp.stack([x1 * c - x2 * s, x2 * c + x1 * s], axis=-2)
    return out.reshape(x.shape).astype(x.dtype)

def dense_gqa(q, k, v, sink=None):
    b, lq, h, dh = q.shape
    hkv = k.shape[2]
    g = h // hkv
    qg = q.reshape(b, lq, hkv, g, dh)
    s = jnp.einsum('bqhgd,bkhd->bhgqk', qg, k).astype(jnp.float32) * ATTN_SCALE
    if sink is not None:
        sink_col = jnp.broadcast_to(sink.astype(jnp.float32).reshape(hkv, g, 1, 1), s.shape[:-1] + (1,))
        p = jax.nn.softmax(jnp.concatenate([s, sink_col], axis=-1), axis=-1)[..., :-1]
    else:
        p = jax.nn.softmax(s, axis=-1)
    o = jnp.einsum('bhgqk,bkhd->bqhgd', p.astype(v.dtype), v)
    return o.reshape(b, lq, h * dh)

def global_attention_latent(q, k, v, kc, vc):
    b, s, h, dh = q.shape
    nblk = s // Q_BLOCK
    keys = jnp.concatenate([kc, k], axis=1)
    vals = jnp.concatenate([vc, v], axis=1)
    qb = q.reshape(b, nblk, Q_BLOCK, h, dh).transpose(1, 0, 2, 3, 4)
    o = lax.map(lambda qblk: dense_gqa(qblk, keys, vals), qb)
    return o.transpose(1, 0, 2, 3).reshape(b, s, h * dh)

def window_attention_latent(q, k, v, kc, vc, sink):
    b, s, h, dh = q.shape
    hkv = k.shape[2]
    g = h // hkv
    nblk = s // Q_BLOCK

    def band(t):
        tp = jnp.pad(t, ((0, 0), (Q_BLOCK, Q_BLOCK), (0, 0), (0, 0))).reshape(b, nblk + 2, Q_BLOCK, hkv, dh)
        return jnp.concatenate([tp[:, :-2], tp[:, 1:-1], tp[:, 2:]], axis=2)

    kb, vb = band(k), band(v)
    qg = q.reshape(b, nblk, Q_BLOCK, hkv, g, dh)
    s_win = jnp.einsum('bnqhgd,bnkhd->bnhgqk', qg, kb).astype(jnp.float32) * ATTN_SCALE
    blk = jnp.arange(nblk, dtype=jnp.int32)[:, None] * Q_BLOCK
    qpos = blk + jnp.arange(Q_BLOCK, dtype=jnp.int32)[None]
    kpos = blk - Q_BLOCK + jnp.arange(3 * Q_BLOCK, dtype=jnp.int32)[None]
    valid = ((jnp.abs(qpos[:, :, None] - kpos[:, None, :]) <= WINDOW)
             & (kpos[:, None, :] >= 0) & (kpos[:, None, :] < s))
    s_win = jnp.where(valid[None, :, None, None], s_win, NEG_INF)
    s_ctx = jnp.einsum('bnqhgd,bchd->bnhgqc', qg, kc).astype(jnp.float32) * ATTN_SCALE
    sink_col = jnp.broadcast_to(sink.astype(jnp.float32).reshape(1, 1, hkv, g, 1, 1), s_ctx.shape[:-1] + (1,))
    p = jax.nn.softmax(jnp.concatenate([s_win, s_ctx, sink_col], axis=-1), axis=-1)
    n_win = 3 * Q_BLOCK
    n_ctx = kc.shape[1]
    p_win = p[..., :n_win].astype(v.dtype)
    p_ctx = p[..., n_win:n_win + n_ctx].astype(v.dtype)
    o = (jnp.einsum('bnhgqk,bnkhd->bnqhgd', p_win, vb)
         + jnp.einsum('bnhgqc,bchd->bnqhgd', p_ctx, vc))
    return o.reshape(b, s, h * dh)

def short_conv(u, conv_w):
    g_pre, g_post, val = jnp.split(u, 3, axis=-1)
    z = g_pre * val
    w = conv_w.astype(z.dtype)[:, None, :]
    y = lax.conv_general_dilated(z, w, window_strides=(1,),
                                 padding=[(CONV_WIDTH // 2, CONV_WIDTH // 2)],
                                 dimension_numbers=('NWC', 'WIO', 'NWC'),
                                 feature_group_count=CONV_CH)
    return g_post * y

def swiglu(h, w_gate, w_up, w_down):
    return (jax.nn.silu(h @ w_gate) * (h @ w_up)) @ w_down

def hybrid_layer(x, xc, mod, mod_c, g_mix_pre, g_mix_post, g_ffn_pre, g_ffn_post, w_in, q_norm, k_norm,
                 sink, conv_w, w_out, w_gate, w_up, w_down, cos, sin, update_ctx):
    sh1, sc1, gt1, sh2, sc2, gt2 = jnp.split(mod, N_MOD, axis=-1)
    csh1, csc1, cgt1, csh2, csc2, cgt2 = jnp.split(mod_c, N_MOD, axis=-1)

    h = rms_norm(x, g_mix_pre) * (1 + sc1) + sh1
    hc = rms_norm(xc, g_mix_pre) * (1 + csc1) + csh1
    p = h @ w_in
    pc = hc @ w_in if update_ctx else hc @ w_in[:, :KV_COLS]

    kac = rms_norm(split_heads(cols(pc, OFF_AK, KV_W_A), A_KV_HEADS), k_norm)
    vac = split_heads(cols(pc, OFF_AV, KV_W_A), A_KV_HEADS)
    kbc = split_heads(cols(pc, OFF_BK, KV_W_B), B_KV_HEADS)
    vbc = split_heads(cols(pc, OFF_BV, KV_W_B), B_KV_HEADS)

    qa = apply_axial_rope(rms_norm(split_heads(cols(p, OFF_AQ, A_Q_HEADS * HEAD_DIM), A_Q_HEADS), q_norm), cos, sin)
    ka = apply_axial_rope(rms_norm(split_heads(cols(p, OFF_AK, KV_W_A), A_KV_HEADS), k_norm), cos, sin)
    va = split_heads(cols(p, OFF_AV, KV_W_A), A_KV_HEADS)
    oa = global_attention_latent(qa, ka, va, kac, vac)

    qb = apply_axial_rope(split_heads(cols(p, OFF_BQ, B_Q_HEADS * HEAD_DIM), B_Q_HEADS), cos, sin)
    kb = apply_axial_rope(split_heads(cols(p, OFF_BK, KV_W_B), B_KV_HEADS), cos, sin)
    vb = split_heads(cols(p, OFF_BV, KV_W_B), B_KV_HEADS)
    ob = window_attention_latent(qb, kb, vb, kbc, vbc, sink)

    oc = short_conv(cols(p, OFF_CONV, 3 * CONV_CH), conv_w)

    y = jnp.concatenate([oa, ob, oc], axis=-1) @ w_out
    x = x + gt1 * rms_norm(y, g_mix_post)
    h2 = rms_norm(x, g_ffn_pre) * (1 + sc2) + sh2
    x = x + gt2 * rms_norm(swiglu(h2, w_gate, w_up, w_down), g_ffn_post)

    if update_ctx:
        qac = rms_norm(split_heads(cols(pc, OFF_AQ, A_Q_HEADS * HEAD_DIM), A_Q_HEADS), q_norm)
        qbc = split_heads(cols(pc, OFF_BQ, B_Q_HEADS * HEAD_DIM), B_Q_HEADS)
        oac = dense_gqa(qac, kac, vac)
        obc = dense_gqa(qbc, kbc, vbc, sink)
        occ = short_conv(cols(pc, OFF_CONV, 3 * CONV_CH), conv_w)
        yc = jnp.concatenate([oac, obc, occ], axis=-1) @ w_out
        xc = xc + cgt1 * rms_norm(yc, g_mix_post)
        h2c = rms_norm(xc, g_ffn_pre) * (1 + csc2) + csh2
        xc = xc + cgt2 * rms_norm(swiglu(h2c, w_gate, w_up, w_down), g_ffn_post)
    return x, xc

def setup_inputs(seed: int = 0) -> dict:
    key = jax.random.key(seed)
    ks = jax.random.split(key, 20)
    f32 = jnp.float32
    D, F, L = D_MODEL, FFN_HIDDEN, DEPTH

    def nrm(k, shape, scale):
        return jax.random.normal(k, shape, f32) * scale

    return {
        "x": nrm(ks[0], (BATCH, SEQ, D), 1.0),
        "c": nrm(ks[1], (BATCH, D), 1.0),
        "ctx": nrm(ks[2], (BATCH, CTX_LEN, D), 1.0),
        "c_ctx": nrm(ks[3], (D,), 1.0),
        "w_ada": nrm(ks[4], (L, D, N_MOD * D), D ** -0.5),
        "b_ada": nrm(ks[5], (L, N_MOD * D), 0.01),
        "g_mix_pre": 1.0 + nrm(ks[6], (L, D), 0.02),
        "g_mix_post": 1.0 + nrm(ks[7], (L, D), 0.02),
        "g_ffn_pre": 1.0 + nrm(ks[8], (L, D), 0.02),
        "g_ffn_post": 1.0 + nrm(ks[9], (L, D), 0.02),
        "w_in": nrm(ks[10], (L, D, IN_COLS), D ** -0.5),
        "q_norm": 1.0 + nrm(ks[11], (L, HEAD_DIM), 0.02),
        "k_norm": 1.0 + nrm(ks[12], (L, HEAD_DIM), 0.02),
        "sink": nrm(ks[13], (L, B_Q_HEADS), 1.0),
        "conv_w": nrm(ks[14], (L, CONV_WIDTH, CONV_CH), CONV_WIDTH ** -0.5),
        "w_out": nrm(ks[15], (L, D, D), D ** -0.5),
        "w_gate": nrm(ks[16], (L, D, F), D ** -0.5),
        "w_up": nrm(ks[17], (L, D, F), D ** -0.5),
        "w_down": nrm(ks[18], (L, F, D), F ** -0.5),
    }

def reference(x, c, ctx, c_ctx, w_ada, b_ada, g_mix_pre, g_mix_post, g_ffn_pre, g_ffn_post, w_in,
              q_norm, k_norm, sink, conv_w, w_out, w_gate, w_up, w_down):
    rows = x.shape[1] // GRID_W
    cos, sin = axial_rope_tables(rows)
    xc = ctx
    silu_c = jax.nn.silu(c)
    silu_cc = jax.nn.silu(c_ctx)
    for l in range(DEPTH):
        mod = (silu_c @ w_ada[l] + b_ada[l])[:, None, :]
        mod_c = silu_cc @ w_ada[l] + b_ada[l]
        x, xc = hybrid_layer(x, xc, mod, mod_c, g_mix_pre[l], g_mix_post[l], g_ffn_pre[l], g_ffn_post[l],
                             w_in[l], q_norm[l], k_norm[l], sink[l], conv_w[l], w_out[l],
                             w_gate[l], w_up[l], w_down[l], cos, sin, update_ctx=(l < DEPTH - 1))
    return x


_drawn_inputs = setup_inputs


def setup_inputs(seed=0):
    import zlib

    import numpy as np

    out = dict(_drawn_inputs(seed))
    spreads = {}
    factors = {'b_ada': 3.278,
     'g_mix_pre': 3.392,
     'g_mix_post': 4.75,
     'g_ffn_pre': 4.723,
     'g_ffn_post': 58.927,
     'q_norm': 35.022,
     'k_norm': 102.883,
     'sink': 8.0}
    for name, (base, spread) in spreads.items():
        noise = np.random.default_rng([zlib.crc32(name.encode()), seed]).standard_normal(out[name].shape)
        drawn = base * np.exp(spread * noise) if base else spread * noise
        out[name] = __import__('jax').numpy.asarray(drawn.astype(out[name].dtype))
    for name, factor in factors.items():
        out[name] = (out[name] * factor).astype(out[name].dtype)
    return out
```

```python
from contextlib import ExitStack

import concourse.bass as bass
from concourse import mybir

ALU = mybir.AluOpType
ACT = mybir.ActivationFunctionType
AX = mybir.AxisListType
F32 = mybir.dt.float32
F32R = mybir.dt.float32r

P = 128
D = 2048
KC = D // P
SEQ = 512
CTX = 256
TOK = SEQ + CTX
NQB = SEQ // P
HEADS = 12
A_HEADS = 6
GROUP = 3
FFN = 5632
EPS = 1e-6
NEG = -1e30
SCALE = float(P) ** -0.5

UCOLS = 256
UCH = 4
UNIT = UCH * UCOLS
RING = 4
ADA0_UNITS = 64
IN_JOBS = 16
OUT_JOBS = 8
GROUPS = FFN // (4 * P)
GROUP_UNITS = 24
U_IN = ADA0_UNITS
U_OUT = U_IN + 4 * IN_JOBS
U_FFN = U_OUT + 4 * OUT_JOBS
U_END = U_FFN + GROUPS * GROUP_UNITS
U_Q = U_IN + 16
RSQRT_STEPS = 7
LAG = 2
H2_BUF = (6, 7, 1)

BASE = 16512
R_H = BASE
R_C = R_H + 65536
R_QKV = R_C + 32768
R_STAGE = R_QKV + 49152
R_WHI = R_STAGE + 16384
R_WLO = R_WHI + 16384
R_ACC = R_WLO + 16384
R_SMALL = R_ACC + 4096


def slot_in(u):
    v = u - U_IN
    return v % 2, ADA0_UNITS // 4 + v // 2 + 1


def ada_steps(u):
    if u < U_Q:
        return (3, 3, 2)[(u - U_IN - RING) % 3]
    if u < U_OUT:
        return (2, 1, 1, 1, 2, 1, 1, 1, 2, 1, 1, 2)[(u - U_Q) % 12]
    return int(u < U_FFN)


def ffn_fills(slot):
    return ADA0_UNITS // 4 + (2 * (IN_JOBS + OUT_JOBS) if slot < 2 else 0)


def key_window(i):
    h, n = divmod(i, NQB)
    if h < A_HEADS:
        return 0, SEQ
    lo, hi = max(n - 1, 0), min(n + 2, NQB)
    return P * lo, P * (hi - lo)


def hybrid_block(nc, a, out):
    ctx = ExitStack()

    def sb(name, shape, at, dt=F32):
        return nc.alloc_sbuf_tensor_at(name, shape, dt, offset=at)

    def sem(name):
        return ctx.enter_context(nc.semaphore(name))

    with ctx:
        PS = ctx.enter_context(nc.psum_tensor("PS", [P, 8, 512], F32))
        psf = PS[:, :, :].rearrange("p b n -> p (b n)")

        xtok = sb("xtok", [P, 6, D], R_H)
        junk = sb("junk", [P, D], R_H + 49152)
        row4 = sb("row4", [4, 1024], R_H + 57344)
        hhi = sb("hhi", [P, KC, SEQ], R_H, F32R)
        hlo = sb("hlo", [P, KC, SEQ], R_H + 32768, F32R)
        tsq = sb("tsq", [P, 2, SEQ], R_H)
        tst = sb("tst", [P, 4, SEQ], R_H + 4096)
        ostage = sb("ostage", [P, 2, NQB, 512], R_H + 16384)

        chi = sb("chi", [P, KC, CTX], R_C, F32R)
        clo = sb("clo", [P, KC, CTX], R_C + 16384, F32R)
        qraw = sb("qraw", [P, 2, SEQ], R_C)
        qsq = sb("qsq", [P, 2, SEQ], R_C + 4096)
        qsw = sb("qsw", [P, 2, SEQ], R_C + 8192)
        gpre = sb("gpre", [P, 4, SEQ], R_C)
        gpost = sb("gpost", [P, 4, SEQ], R_C + 8192)
        zpad = sb("zpad", [P, 4, SEQ + 2], R_C + 16384)
        pt = sb("pt", [P, 2, 6, SEQ], R_C)
        prob = [sb(f"prob{n}", [P, TOK], R_C + 24576 + 3072 * n) for n in range(2)]
        yT = sb("yT", [P, KC, SEQ], R_C)

        xT = sb("xT", [P, KC, TOK], R_QKV)
        qT = sb("qT", [P, HEADS, SEQ], R_QKV)
        kT = sb("kT", [P, 4, TOK], R_QKV + 24576)
        vv = sb("vv", [P, 6, 512], R_QKV + 36864)
        ktmp = sb("ktmp", [P, 8, TOK], R_QKV)
        xtok2 = sb("xtok2", [P, NQB, D], R_QKV)
        jst = sb("jst", [P, 8, SEQ], R_QKV + 32768)
        facc = sb("facc", [P, KC, SEQ], R_QKV)
        hidhi = sb("hidhi", [P, 4, SEQ], R_QKV + 32768, F32R)
        hidlo = sb("hidlo", [P, 4, SEQ], R_QKV + 40960, F32R)

        stage = sb("stage", [P, RING, UNIT], R_STAGE)
        whi = sb("whi", [P, RING, UNIT], R_WHI, F32R)
        wlo = sb("wlo", [P, RING, UNIT], R_WLO, F32R)
        rows = sb("rows", [P, 2, P], R_ACC)
        acc = sb("acc", [P, 1024], R_ACC)
        sg = sb("sg", [P, 2, SEQ], R_ACC)

        at = [R_SMALL]

        def small(name, shape, dt=F32):
            n = 4
            for s in shape[1:]:
                n *= s
            t = sb(name, shape, at[0], dt)
            at[0] += (n + 31) // 32 * 32
            return t

        ident = small("ident", [P, P])
        ones = small("ones", [P, P])
        prob.append(sb("prob2", [P, TOK], at[0]))
        cosT = small("cosT", [P, SEQ])
        sinT = small("sinT", [P, SEQ])
        maskl = small("maskl", [P, P])
        maskr = small("maskr", [P, P])
        colA = small("colA", [P, 128])
        colB = small("colB", [P, 80])
        sil = small("sil", [P, 32])
        silp = small("silp", [P, 64 + 124], F32R)
        msum = small("msum", [P, 32, 4])
        modc = small("modc", [P, 96])
        modx = small("modx", [P, 32])
        gain = small("gain", [P, 5, KC])
        xss = small("xss", [P, 4, 6])
        qss = small("qss", [P, 4, 24])
        sinkc = small("sinkc", [P, A_HEADS])
        mx = small("mx", [P, 48])
        nb = small("nb", [P, 48])
        rsum = small("rsum", [P, 48])
        rinv = small("rinv", [P, 48])
        esink = small("esink", [P, 48])
        assert at[0] <= 229368

        bA = colA[:, 0:96]
        cA = colA[:, 96:128]
        g_mix_pre, g_mix_post = colB[:, 0:16], colB[:, 16:32]
        g_ffn_pre, g_ffn_post = colB[:, 32:48], colB[:, 48:64]

        def tap(t, c):
            return colB[:, 64 + 4 * t + c:65 + 4 * t + c]

        qg, kg, qgs, kgs = (colB[:, n:n + 1] for n in (76, 77, 78, 79))

        v_ada = a["w_ada"].rearrange("(k p) n -> p k n", p=P)
        v_in = a["w_in"].rearrange("(k p) n -> p k n", p=P)
        v_out = a["w_out"].rearrange("(k p) n -> p k n", p=P)
        v_gate = a["w_gate"].rearrange("(k p) n -> p k n", p=P)
        v_up = a["w_up"].rearrange("(k p) n -> p k n", p=P)
        v_down = a["w_down"].rearrange("(k p) n -> p k n", p=P)
        o_tok = out.rearrange("(t p) n -> p t n", p=P)

        const_in = sem("const_in")
        mask_in = sem("mask_in")
        x_in = [sem(f"x_in{t}") for t in range(6)]
        x2_in = sem("x2_in")
        stage_in = [sem(f"stage_in{s}") for s in range(RING)]
        ada_in = [sem(f"ada_in{s}") for s in range(2)]
        setup = sem("setup")
        rows_turned = sem("rows_turned")
        cols_ready = sem("cols_ready")
        silu_ready = sem("silu_ready")
        silp_ready = sem("silp_ready")
        hi_ready = sem("hi_ready")
        lo_ready = sem("lo_ready")
        unit_used = sem("unit_used")
        rms = sem("rms")
        xsq = sem("xsq")
        xhat = sem("xhat")
        x_turned = sem("x_turned")
        x_kept = sem("x_kept")
        row_kept = sem("row_kept")
        row_turned = sem("row_turned")
        mods = sem("mods")
        h_t = sem("h_t")
        h_hi = sem("h_hi")
        h_lo = sem("h_lo")
        ada_used = sem("ada_used")
        ada_sum = sem("ada_sum")
        mod_add = sem("mod_add")
        bank_act = sem("bank_act")
        bank_dve = sem("bank_dve")
        ksq = sem("ksq")
        kstat = sem("kstat")
        kswap = sem("kswap")
        kdone = sem("kdone")
        qswap = sem("qswap")
        qsq_made = sem("qsq_made")
        qsum = sem("qsum")
        qdone = sem("qdone")
        zdone = sem("zdone")
        conv_y = sem("conv_y")
        dchain = sem("dchain")
        s_done = sem("s_done")
        nb_done = sem("nb_done")
        p_done = sem("p_done")
        es_done = sem("es_done")
        pn_done = sem("pn_done")
        pt_turned = sem("pt_turned")
        pt_lat = sem("pt_lat")
        pt_ctx = sem("pt_ctx")
        o_done = sem("o_done")
        o_hi = sem("o_hi")
        o_lo = sem("o_lo")
        y_sq = sem("y_sq")
        y_sqsum = sem("y_sqsum")
        y_stat = sem("y_stat")
        x2_turned = sem("x2_turned")
        x1_u = sem("x1_u")
        x1_done = sem("x1_done")
        x1_sq = sem("x1_sq")
        x1_sum = sem("x1_sum")
        h2_t = sem("h2_t")
        h2_hi = sem("h2_hi")
        h2_lo = sem("h2_lo")
        gate_done = sem("gate_done")
        hid_done = sem("hid_done")
        hid_hi = sem("hid_hi")
        hid_lo = sem("hid_lo")
        facc_done = sem("facc_done")
        f_sq = sem("f_sq")
        f_sqsum = sem("f_sqsum")
        f_stat = sem("f_stat")
        f_out = sem("f_out")
        o_turned = sem("o_turned")
        o_act = sem("o_act")
        o_dve = sem("o_dve")
        stored = [sem(f"stored{s}") for s in range(2)]

        block = ctx.enter_context(nc.Block())
        N_CONST = 3 + 4 + 4 + 3 + 4

        @block.sync
        def _(sp):
            def w_load(slot, src):
                sp.dma_start(stage[:, slot, :].rearrange("p (k n) -> p k n", k=UCH), src).then_inc(stage_in[slot], 16)

            for b in range(4):
                for k in range(KC):
                    u = 16 * b + k
                    if u >= RING:
                        sp.wait_ge(lo_ready, u - RING + 1)
                    sp.dma_start(stage[:, u % RING, :], v_ada[:, k, 1024 * b:1024 * b + 1024])\
                        .then_inc(stage_in[u % RING], 16)
            for q in range(2):
                sp.wait_ge(lo_ready, U_IN - 3 + q)
                w_load(q, v_in[:, 4 * q:4 * q + 4, 0:UCOLS])
            for q in (2, 3):
                sp.wait_ge(lo_ready, U_IN + q - 1)
                w_load(q % 2, v_in[:, 4 * q:4 * q + 4, 0:UCOLS])
            with sp.Fori(1, IN_JOBS) as j:
                for q in range(4):
                    sp.wait_ge(lo_ready, U_IN - 1 + q + 4 * j)
                    w_load(q % 2, v_in[:, 4 * q:4 * q + 4, bass.ds(j * UCOLS, UCOLS)])
            with sp.Fori(0, OUT_JOBS) as j:
                for q in range(4):
                    sp.wait_ge(lo_ready, U_OUT - 1 + q + 4 * j)
                    w_load(q % 2, v_out[:, 4 * q:4 * q + 4, bass.ds(j * UCOLS, UCOLS)])
            sp.wait_ge(lo_ready, U_FFN)
            sp.wait_ge(ada_used, 128)

            def ffn_loads(g):
                r = 0
                for pair in range(2):
                    for w in (v_gate, v_up):
                        for q in range(4):
                            sp.wait_ge(lo_ready, U_FFN - 3 + r + GROUP_UNITS * g)
                            w_load(r % RING, w[:, 4 * q:4 * q + 4, bass.ds(512 * g + UCOLS * pair, UCOLS)])
                            r += 1
                for d in range(8):
                    sp.wait_ge(lo_ready, U_FFN - 3 + r + GROUP_UNITS * g)
                    w_load(r % RING, v_down[:, bass.ds(4 * g, 4), UCOLS * d:UCOLS * d + UCOLS])
                    r += 1

            with sp.Fori(0, GROUPS) as g:
                ffn_loads(g)
            for c in range(4):
                sp.wait_ge(o_act, 2 * c + 2)
                sp.wait_ge(o_dve, 2 * c + 2)
                sp.dma_start(o_tok[:, :, 512 * c:512 * c + 512], ostage[:, c % 2]).then_inc(stored[c % 2], 16)
            sp.wait_ge(stored[0], 32)
            sp.wait_ge(stored[1], 32)

        @block.gpsimd
        def _(pool):
            nc.gpsimd.memset(ones[:], 1.0).then_inc(setup, 1)
            nc.gpsimd.memset(silp[:, :].bitcast(F32), 0.0).then_inc(setup, 1)
            pool.wait_ge(lo_ready, ADA0_UNITS)
            for k in range(KC):
                if k >= 2:
                    pool.wait_ge(ada_used, k - 1)
                pool.dma_start(stage[:, 2 + k % 2, :], v_ada[:, k, 4096:5120]).then_inc(ada_in[k % 2], 16)
            with pool.Fori(1, 8) as b:
                for k in range(KC):
                    pool.wait_ge(ada_used, k - 1 + 16 * b)
                    pool.dma_start(stage[:, 2 + k % 2, :], v_ada[:, k, bass.ds(4096 + 1024 * b, 1024)])\
                        .then_inc(ada_in[k % 2], 16)

        @block.scalar
        def _(act):
            def copy_(dst, src):
                return nc.scalar.activation(dst, src, ACT.Copy)

            def split_hi(u, slot, count):
                act.wait_ge(stage_in[slot], 16 * count)
                act.wait_ge(unit_used, u - RING + 1)
                copy_(whi[:, u % RING, :], stage[:, slot, :]).then_inc(hi_ready, 1)

            def sqrt_(use, dst, src):
                act.wait_ge(rms, RSQRT_STEPS * use + 1)
                nc.scalar.activation(dst, src, ACT.Sqrt).then_inc(rms, 1)

            ld = lambda dst, src: act.dma_start(dst, src).then_inc(const_in, 16)
            ld(rows[0:96, 0, :], a["b_ada"].rearrange("(r n) -> r n", n=P))
            ld(rows[96:112, 0, :], a["c"].rearrange("o (r n) -> (o r) n", n=P))
            ld(rows[112:128, 0, :], a["c_ctx"].rearrange("(r n) -> r n", n=P))
            for n, name in enumerate(("g_mix_pre", "g_mix_post", "g_ffn_pre", "g_ffn_post")):
                ld(rows[16 * n:16 * n + 16, 1, :], a[name].rearrange("(r n) -> r n", n=P))
            ld(rows[64:76, 1, :], a["conv_w"].rearrange("t (c n) -> (t c) n", n=P))
            ld(rows[76:77, 1, :], a["q_norm"].rearrange("(o n) -> o n", o=1))
            ld(rows[77:78, 1, :], a["k_norm"].rearrange("(o n) -> o n", o=1))
            ld(ident[:], a["ident"])
            for r, name in ((78, "q_norm"), (79, "k_norm")):
                w = a[name].rearrange("(o a h i) -> o a h i", o=1, a=2, h=2)
                d = rows[r:r + 1, 1, :].rearrange("p (a h i) -> p a h i", a=2, h=2)
                for h in range(2):
                    ld(d[:, :, h, :], w[:, :, 1 - h, :])
            ld(cosT[:], a["rope_cos"])
            ld(sinT[:], a["rope_sin"])
            ld(sinkc[:], a["sink"].rearrange("(o h) -> o h", o=1).broadcast_to([P, A_HEADS]))
            for t in range(6):
                src = a["x"][P * t:P * t + P, :] if t < 4 else a["ctx"][P * (t - 4):P * (t - 4) + P, :]
                act.dma_start(xtok[:, t, :], src).then_inc(x_in[t], 16)
            act.dma_start(maskl[:], a["mask_left"]).then_inc(mask_in, 16)
            act.dma_start(maskr[:], a["mask_right"]).then_inc(mask_in, 16)

            act.wait_ge(cols_ready, 1)
            nc.scalar.activation(sil[:], cA, ACT.Silu).then_inc(silu_ready, 1)

            def keep_row(b):
                act.wait_ge(unit_used, 16 * b + 16)
                if b:
                    act.wait_ge(row_turned, b)
                copy_(row4[:, :], psf[0:4, 1024 * (b % 2):1024 * (b % 2) + 1024]).then_inc(row_kept, 1)

            def keep_x(g):
                t, c = g // 4, g % 4
                act.wait_ge(x_turned, g + 1)
                copy_(xT[:, 4 * c:4 * c + 4, P * t:P * t + P],
                      PS[:, 4 + g % 2, :].rearrange("p (c n) -> p c n", c=4)).then_inc(x_kept, 1)

            for u in range(ADA0_UNITS):
                act.wait_ge(stage_in[u % RING], 16 * (u // RING + 1))
                if u >= RING:
                    act.wait_ge(unit_used, u - RING + 1)
                copy_(whi[:, u % RING, :], stage[:, u % RING, :]).then_inc(hi_ready, 1)
                if 4 <= u < 16 and u % 2 == 0:
                    t = (u - 4) // 2
                    act.wait_ge(x_in[t], 16)
                    if t:
                        act.wait_ge(xsq, t)
                    nc.scalar.activation(junk[:], xtok[:, t, :], ACT.Square, accum_out=xss[:, 0, t:t + 1])\
                        .then_inc(xsq, 1)
                if u == 18:
                    sqrt_(0, xss[:, 2, :], xss[:, 1, :])
                if 27 <= u < 51:
                    keep_x(u - 27)
                if u in (19, 35, 51):
                    keep_row((u - 19) // 16)
            keep_row(3)
            for u in range(U_IN, U_IN + 4):
                split_hi(u, *slot_in(u))

            act.wait_ge(x_turned, 24)
            for j in range(KC):
                act.wait_ge(h_t, 2 * j + 1)
                copy_(hhi[:, j, :], xT[:, j, 0:SEQ]).then_inc(h_hi, 1)
                act.wait_ge(h_t, 2 * j + 2)
                copy_(chi[:, j, :], xT[:, j, SEQ:TOK]).then_inc(h_hi, 1)

            def swap(dst, src, done):
                for s in range(4):
                    act.dma_start(dst[32 * (s ^ 1):32 * (s ^ 1) + 32, :], src[32 * s:32 * s + 32, :])\
                        .then_inc(done, 16)

            def k_job(b):
                act.wait_ge(unit_used, U_IN + 8 * b + 4)
                if b:
                    act.wait_ge(kdone, 2)
                else:
                    act.wait_ge(h_lo, 2 * KC)
                copy_(ktmp[:, 0, 0:SEQ], PS[:, 0, :]).then_inc(bank_act, 1)
                copy_(ktmp[:, 0:2, SEQ:TOK], PS[:, 2, :].rearrange("p (s n) -> p s n", s=2)).then_inc(bank_act, 1)
                act.wait_ge(bank_act, 4 * b + 2)
                swap(ktmp[:, 7, 0:SEQ], ktmp[:, 0, 0:SEQ], kswap)
                if b == 0:
                    nc.scalar.activation(ktmp[:, 2, :], ktmp[:, 0, :], ACT.Square).then_inc(ksq, 1)
                    act.wait_ge(bank_dve, 1)
                    nc.scalar.activation(ktmp[:, 3, :], ktmp[:, 1, :], ACT.Square).then_inc(ksq, 1)

            def k_swap_second(b):
                act.wait_ge(bank_dve, 2 * b + 1)
                act.wait_ge(kdone, 2 * b + 1)
                swap(ktmp[:, 7, 0:SEQ], ktmp[:, 1, 0:SEQ], kswap)

            def v_job(b):
                act.wait_ge(unit_used, U_IN + 8 * b + 8)
                for t in (0, 4):
                    copy_(vv[:, t:t + 2, UCOLS * b:UCOLS * b + UCOLS],
                          PS[:, 3 + t // 2, :].rearrange("p (t n) -> p t n", t=2)).then_inc(bank_act, 1)

            def q_job(j):
                act.wait_ge(unit_used, U_Q + 4 * j + 4)
                if j == 0:
                    act.wait_ge(kdone, 4)
                if 0 < j <= 6:
                    act.wait_ge(qdone, 2 * j)
                if j <= 5:
                    for s in range(2):
                        copy_(qraw[:, s, :], PS[:, 2 * (j % 3) + s, :]).then_inc(bank_act, 1)
                    act.wait_ge(bank_act, 8 + 2 * j + 2)
                    for s in range(2):
                        swap(qsw[:, s, :], qraw[:, s, :], qswap)
                    if j < 3:
                        if j:
                            act.wait_ge(qsum, j)
                        for s in range(2):
                            nc.scalar.activation(qsq[:, s, :], qraw[:, s, :], ACT.Square).then_inc(qsq_made, 1)
                else:
                    dst = gpre if j < 8 else gpost
                    for s in range(2):
                        copy_(dst[:, 2 * (j % 2) + s, :], PS[:, 2 * (j % 3) + s, :]).then_inc(bank_act, 1)

            for u in range(U_IN + 4, U_OUT + 4):
                e = u - 3
                if e == U_IN + 4:
                    k_job(0)
                if e == U_IN + 6:
                    sqrt_(1, ktmp[:, 5, :], ktmp[:, 4, :])
                if e == U_IN + 7:
                    k_swap_second(0)
                if e == U_IN + 8:
                    v_job(0)
                    sqrt_(2, ktmp[:, 5, :], ktmp[:, 4, :])
                if e == U_IN + 12:
                    k_job(1)
                if e == U_IN + 14:
                    k_swap_second(1)
                if e == U_IN + 16:
                    v_job(1)
                if e > U_Q and (e - U_Q) % 4 == 0 and (e - U_Q) // 4 - 1 < 10:
                    q_job((e - U_Q) // 4 - 1)
                if e == U_Q + 16:
                    sqrt_(3, qss[:, 1, :], qss[:, 0, :])
                split_hi(u, *slot_in(u))

            act.wait_ge(unit_used, U_OUT)
            for c in range(4):
                act.wait_ge(conv_y, c + 1)
                copy_(hhi[:, 12 + c, :], gpre[:, c, :]).then_inc(o_hi, 1)

            def exp_item(i):
                h = i // NQB
                s0 = 1024 * (i % 2)
                lo, w = key_window(i)
                act.wait_ge(nb_done, i + 1)
                if i == 2:
                    act.wait_ge(qdone, HEADS)
                if i >= 3:
                    act.wait_ge(pt_turned, i - 2)
                sc = qss[:, 3, i:i + 1] if h < A_HEADS else SCALE
                nc.scalar.activation(prob[i % 3][:, 512 - w:TOK], psf[:, s0 + 512 - w:s0 + TOK], ACT.Exp,
                                     bias=nb[:, i:i + 1], scale=sc, accum_out=rsum[:, i:i + 1]).then_inc(p_done, 1)
                if h >= A_HEADS:
                    nc.scalar.activation(esink[:, i:i + 1], sinkc[:, h - A_HEADS:h - A_HEADS + 1], ACT.Exp,
                                         bias=nb[:, i:i + 1]).then_inc(es_done, 1)

            def keep_pt(i):
                h, n = divmod(i, NQB)
                lo, w = key_window(i)
                act.wait_ge(pt_turned, i + 1)
                if h >= 2:
                    act.wait_ge(o_done, h - 1)
                copy_(pt[:, h % 2, lo // P:(lo + w) // P, P * n:P * n + P],
                      psf[:, 2048 + lo:2048 + lo + w].rearrange("p (k n) -> p k n", n=P)).then_inc(pt_lat, 1)

            def keep_o_hi(h):
                act.wait_ge(o_done, h + 1)
                copy_(hhi[:, h, :], PS[:, 6 + h % 2, :]).then_inc(o_hi, 1)

            for i in range(4 * HEADS + LAG):
                if i < 4 * HEADS:
                    exp_item(i)
                if i >= LAG:
                    keep_pt(i - LAG)
                if i % 4 == 3 and i > 4:
                    keep_o_hi(i // 4 - 1)
            keep_o_hi(HEADS - 1)

            for t in range(NQB):
                act.dma_start(xtok2[:, t, :], a["x"][P * t:P * t + P, :]).then_inc(x2_in, 16)

            def y_squares(j):
                for s in range(2):
                    n = 2 * j + s
                    act.wait_ge(bank_dve, 4 + n + 1)
                    if n >= 2:
                        act.wait_ge(y_sqsum, n - 1)
                    nc.scalar.activation(jst[:, s, :], yT[:, n, :], ACT.Square).then_inc(y_sq, 1)

            for u in range(U_OUT + 4, U_FFN + 4):
                e = u - 3
                if u < U_FFN:
                    split_hi(u, *slot_in(u))
                else:
                    act.wait_ge(stage_in[u - U_FFN], 16 * (ffn_fills(u - U_FFN) + 1))
                    act.wait_ge(unit_used, e)
                    copy_(whi[:, u % RING, :], stage[:, u - U_FFN, :]).then_inc(hi_ready, 1)
                if (e - U_OUT) % 4 == 0:
                    y_squares((e - U_OUT) // 4 - 1)

            sqrt_(4, jst[:, 4, :], jst[:, 3, :])
            for j in range(KC):
                act.wait_ge(x1_done, j + 1)
                if j >= 2:
                    act.wait_ge(x1_sum, j - 1)
                nc.scalar.activation(jst[:, j % 2, :], yT[:, j, :], ACT.Square).then_inc(x1_sq, 1)
            sqrt_(5, jst[:, 4, :], jst[:, 3, :])
            for j in range(KC):
                act.wait_ge(h2_t, j + 1)
                nc.scalar.activation(hhi[:, j, :], jst[:, H2_BUF[j % 3], :], ACT.Identity, bias=modc[:, 48 + j:49 + j])\
                    .then_inc(h2_hi, 1)

            def ffn(g, last):
                for r in range(GROUP_UNITS):
                    def silu(half):
                        act.wait_ge(unit_used, U_FFN + 1 + r + GROUP_UNITS * g)
                        act.wait_ge(hid_lo, 4 * g + 2 * half)
                        for s in range(2):
                            nc.scalar.activation(sg[:, s, :], PS[:, s, :], ACT.Silu).then_inc(gate_done, 1)

                    def upper(half):
                        for s in range(2):
                            act.wait_ge(hid_done, 4 * g + 2 * half + s + 1)
                            copy_(hidhi[:, 2 * half + s, :], sg[:, s, :]).then_inc(hid_hi, 1)

                    if r in (3, 11):
                        silu(r // 8)
                    if r in (7, 15):
                        upper(r // 8)
                    if not (last and r >= GROUP_UNITS - RING):
                        act.wait_ge(stage_in[r % RING], 16 * (ffn_fills(r % RING) + r // RING + 2) + 96 * g)
                        act.wait_ge(unit_used, U_FFN + 1 + r + GROUP_UNITS * g)
                        copy_(whi[:, r % RING, :], stage[:, r % RING, :]).then_inc(hi_ready, 1)

            with act.Fori(0, GROUPS - 1) as g:
                ffn(g, False)
            ffn(GROUPS - 1, True)

            act.wait_ge(unit_used, U_END - 8)
            for j in range(KC):
                act.wait_ge(facc_done, 16 * GROUPS + j + 1)
                if j >= 2:
                    act.wait_ge(f_sqsum, j - 1)
                nc.scalar.activation(tsq[:, j % 2, :], facc[:, j, :], ACT.Square).then_inc(f_sq, 1)
            sqrt_(6, tst[:, 1, :], tst[:, 0, :])
            for c in range(4):
                act.wait_ge(o_turned, c + 1)
                if c >= 2:
                    act.wait_ge(stored[c % 2], 16)
                for t in range(2):
                    copy_(ostage[:, c % 2, t, :], PS[:, 4 * (c % 2) + t, :]).then_inc(o_act, 1)

        @block.vector
        def _(dve):
            own = [0]

            def link(ins):
                own[0] += 1
                ins.then_inc(dchain, 1)
                dve.wait_ge(dchain, own[0])

            def split_lo(u, slot):
                dve.wait_ge(hi_ready, u + 1)
                nc.vector.tensor_tensor(wlo[:, u % RING, :], stage[:, slot, :], whi[:, u % RING, :].bitcast(F32),
                                        ALU.subtract).then_inc(lo_ready, 1)

            def rsqrt_head(use, dst, sums, n):
                nc.vector.tensor_scalar(dst, sums, 1.0 / n, EPS, ALU.mult, ALU.add).then_inc(rms, 1)

            def rsqrt_tail(use, mean, root, tmp):
                n = RSQRT_STEPS * use + 2
                steps = (
                    lambda: nc.vector.reciprocal(root, root),
                    lambda: nc.vector.tensor_tensor(tmp, root, root, ALU.mult),
                    lambda: nc.vector.tensor_tensor(tmp, tmp, mean, ALU.mult),
                    lambda: nc.vector.tensor_scalar(tmp, tmp, -0.5, 1.5, ALU.mult, ALU.add),
                    lambda: nc.vector.tensor_tensor(root, root, tmp, ALU.mult),
                )
                for step in steps:
                    dve.wait_ge(rms, n)
                    step().then_inc(rms, 1)
                    n += 1
                dve.wait_ge(rms, n)

            dve.wait_ge(rows_turned, 2)
            nc.vector.tensor_copy(colA[:], PS[:, 7, 0:128]).then_inc(cols_ready, 1)
            nc.vector.tensor_copy(colB[:], PS[:, 7, 128:208]).then_inc(cols_ready, 1)
            dve.wait_ge(cols_ready, 2)
            dve.wait_ge(silu_ready, 1)
            dve.wait_ge(setup, 2)
            silv = sil[:, :].rearrange("p (v k) -> p k v", v=2)
            parts = silp[:, 0:64].rearrange("p (k v) -> p k v", v=4)
            nc.vector.tensor_copy(parts[:, :, 0:2], silv).then_inc(silp_ready, 1)
            dve.wait_ge(silp_ready, 1)
            nc.vector.tensor_tensor(parts[:, :, 2:4], silv, parts[:, :, 0:2].bitcast(F32), ALU.subtract)\
                .then_inc(silp_ready, 1)

            for u in range(ADA0_UNITS):
                split_lo(u, u % RING)
                if u == 16:
                    dve.wait_ge(xsq, 6)
                    rsqrt_head(0, xss[:, 1, :], xss[:, 0, :], D)
                if u == 20:
                    rsqrt_tail(0, xss[:, 1, :], xss[:, 2, :], xss[:, 3, :])
                if 21 <= u < 45 and (u - 21) % 4 == 0:
                    t = (u - 21) // 4
                    nc.vector.tensor_scalar(xtok[:, t, :], xtok[:, t, :], xss[:, 2, t:t + 1], None, ALU.mult)\
                        .then_inc(xhat, 1)
            split_lo(U_IN, 0)
            split_lo(U_IN + 1, 1)
            dve.wait_ge(row_turned, 4)
            link(nc.vector.tensor_copy(msum[:, :, :].rearrange("p c v -> p (c v)"), PS[:, 6, 0:128]))
            link(nc.vector.tensor_tensor(msum[:, :, 0:2], msum[:, :, 0:2], msum[:, :, 2:4], ALU.add))
            nc.vector.tensor_tensor(modc[:, 0:32], msum[:, :, 0], bA[:, 0:32], ALU.add).then_inc(mods, 1)
            nc.vector.tensor_tensor(modx[:, :], msum[:, :, 1], bA[:, 0:32], ALU.add).then_inc(mods, 1)
            dve.wait_ge(mods, 2)
            nc.vector.scalar_tensor_tensor(gain[:, 0, :], modc[:, 16:32], 1.0, g_mix_pre, ALU.add, ALU.mult)\
                .then_inc(mods, 1)
            nc.vector.scalar_tensor_tensor(gain[:, 1, :], modx[:, 16:32], 1.0, g_mix_pre, ALU.add, ALU.mult)\
                .then_inc(mods, 1)
            dve.wait_ge(mods, 4)
            dve.wait_ge(x_kept, 24)

            def h_full(j):
                nc.vector.tensor_scalar(xT[:, j, 0:SEQ], xT[:, j, 0:SEQ], gain[:, 0, j:j + 1], modc[:, j:j + 1],
                                        ALU.mult, ALU.add).then_inc(h_t, 1)
                nc.vector.tensor_scalar(xT[:, j, SEQ:TOK], xT[:, j, SEQ:TOK], gain[:, 1, j:j + 1],
                                        modx[:, j:j + 1], ALU.mult, ALU.add).then_inc(h_t, 1)

            h_full(0)
            h_full(1)
            split_lo(U_IN + 2, 0)
            split_lo(U_IN + 3, 1)
            for j in range(KC):
                if j + 2 < KC:
                    h_full(j + 2)
                dve.wait_ge(h_hi, 2 * j + 1)
                nc.vector.tensor_tensor(hlo[:, j, :], xT[:, j, 0:SEQ], hhi[:, j, :].bitcast(F32), ALU.subtract)\
                    .then_inc(h_lo, 1)
                dve.wait_ge(h_hi, 2 * j + 2)
                nc.vector.tensor_tensor(clo[:, j, :], xT[:, j, SEQ:TOK], chi[:, j, :].bitcast(F32), ALU.subtract)\
                    .then_inc(h_lo, 1)

            seen = [0]

            def ada_step():
                n = seen[0]
                b, k = divmod(n, KC)
                seen[0] += 1
                w = stage[:, 2 + n % 2, :]
                if k == 0 and b:
                    mod_block(b - 1)
                dve.wait_ge(ada_in[n % 2], 16 * (n // 2 + 1))
                if n:
                    dve.wait_ge(ada_used, n)
                if k == 0:
                    nc.vector.tensor_scalar(acc[:], w, sil[:, k:k + 1], None, ALU.mult).then_inc(ada_used, 1)
                else:
                    nc.vector.scalar_tensor_tensor(acc[:], w, sil[:, k:k + 1], acc[:], ALU.mult, ALU.add)\
                        .then_inc(ada_used, 1)

            def mod_block(b):
                dve.wait_ge(ada_sum, b + 1)
                nc.vector.tensor_tensor(modc[:, 32 + 8 * b:40 + 8 * b], PS[:, 6, 0:8],
                                        bA[:, 32 + 8 * b:40 + 8 * b], ALU.add).then_inc(mod_add, 1)

            def k_job(b):
                dve.wait_ge(unit_used, U_IN + 8 * b + 4)
                nc.vector.tensor_copy(ktmp[:, 1, 0:SEQ], PS[:, 1, :]).then_inc(bank_dve, 1)

            def k_mean(s):
                dve.wait_ge(kstat, s + 1)
                rsqrt_head(1 + s, ktmp[:, 4, :], psf[:, 3072:3072 + TOK], P)

            def k_finish(b, s):
                raw, part, res = ktmp[:, s, :], ktmp[:, 7, 0:SEQ], kT[:, 2 * b + s, :]
                dve.wait_ge(bank_dve, 2 * b + 1)
                dve.wait_ge(bank_act, 4 * b + 2)
                if b == 0:
                    rsqrt_tail(1 + s, ktmp[:, 4, :], ktmp[:, 5, :], ktmp[:, 6, :])
                    t = ktmp[:, 2 + s, :]
                    dve.wait_ge(kswap, 64 * (s + 1))
                    link(nc.vector.scalar_tensor_tensor(part, part, kgs, sinT[:], ALU.mult, ALU.mult))
                    link(nc.vector.scalar_tensor_tensor(t[:, 0:SEQ], raw[:, 0:SEQ], kg, cosT[:], ALU.mult, ALU.mult))
                    link(nc.vector.tensor_scalar(t[:, SEQ:TOK], raw[:, SEQ:TOK], kg, None, ALU.mult))
                    link(nc.vector.tensor_tensor(t[:, 0:SEQ], t[:, 0:SEQ], part, ALU.add))
                    nc.vector.tensor_tensor(res, t, ktmp[:, 5, :], ALU.mult).then_inc(kdone, 1)
                else:
                    dve.wait_ge(kswap, 64 * (s + 3))
                    link(nc.vector.tensor_tensor(part, part, sinT[:], ALU.mult))
                    link(nc.vector.tensor_tensor(res[:, 0:SEQ], raw[:, 0:SEQ], cosT[:], ALU.mult))
                    link(nc.vector.tensor_copy(res[:, SEQ:TOK], raw[:, SEQ:TOK]))
                    nc.vector.tensor_tensor(res[:, 0:SEQ], res[:, 0:SEQ], part, ALU.add).then_inc(kdone, 1)

            def v_job(b):
                dve.wait_ge(unit_used, U_IN + 8 * b + 8)
                nc.vector.tensor_copy(vv[:, 2:4, UCOLS * b:UCOLS * b + UCOLS],
                                      PS[:, 4, :].rearrange("p (t n) -> p t n", t=2)).then_inc(bank_dve, 1)

            def q_finish(j):
                for s in range(2):
                    h = 2 * j + s
                    dve.wait_ge(bank_act, 8 + 2 * j + 2)
                    dve.wait_ge(qswap, 128 * j + 128)
                    part, res, raw = qsw[:, s, :], qT[:, h, :], qraw[:, s, :]
                    if h < A_HEADS:
                        link(nc.vector.scalar_tensor_tensor(part, part, qgs, sinT[:], ALU.mult, ALU.mult))
                        link(nc.vector.scalar_tensor_tensor(res, raw, qg, cosT[:], ALU.mult, ALU.mult))
                    else:
                        link(nc.vector.tensor_tensor(part, part, sinT[:], ALU.mult))
                        link(nc.vector.tensor_tensor(res, raw, cosT[:], ALU.mult))
                    nc.vector.tensor_tensor(res, res, part, ALU.add).then_inc(qdone, 1)

            def z_job(j):
                dve.wait_ge(unit_used, U_Q + 4 * j + 4)
                if j == 10:
                    dve.wait_ge(bank_act, 8 + 20)
                    for s in (0, SEQ + 1):
                        nc.vector.memset(zpad[:, :, s:s + 1], 0.0).then_inc(zdone, 1)
                for s in range(2):
                    c = 2 * (j - 10) + s
                    nc.vector.tensor_tensor(zpad[:, c, 1:SEQ + 1], PS[:, 2 * (j % 3) + s, :], gpre[:, c, :],
                                            ALU.mult).then_inc(zdone, 1)

            def conv(c):
                dve.wait_ge(zdone, 3 + c)
                y = gpre[:, c, :]
                link(nc.vector.tensor_scalar(y, zpad[:, c, 0:SEQ], tap(0, c), None, ALU.mult))
                link(nc.vector.scalar_tensor_tensor(y, zpad[:, c, 1:SEQ + 1], tap(1, c), y, ALU.mult, ALU.add))
                link(nc.vector.scalar_tensor_tensor(y, zpad[:, c, 2:SEQ + 2], tap(2, c), y, ALU.mult, ALU.add))
                nc.vector.tensor_tensor(y, y, gpost[:, c, :], ALU.mult).then_inc(conv_y, 1)

            for u in range(U_IN + 4, U_OUT + 4):
                e = u - 3
                if e == U_IN + 4:
                    k_job(0)
                if e == U_IN + 6:
                    k_mean(0)
                if e == U_IN + 7:
                    k_finish(0, 0)
                    k_mean(1)
                if e == U_IN + 8:
                    v_job(0)
                if e == U_IN + 9:
                    k_finish(0, 1)
                if e == U_IN + 12:
                    k_job(1)
                if e == U_IN + 14:
                    k_finish(1, 0)
                if e == U_IN + 15:
                    k_finish(1, 1)
                if e == U_IN + 16:
                    v_job(1)
                if (e - U_Q) % 4 == 1 and 0 <= (e - U_Q) // 4 - 1 < 6:
                    q_finish((e - U_Q) // 4 - 1)
                if e == U_Q + 15:
                    dve.wait_ge(qsum, 3)
                    rsqrt_head(3, qss[:, 0, :], PS[:, 7, 0:24], P)
                if e == U_Q + 18:
                    rsqrt_tail(3, qss[:, 0, :], qss[:, 1, :], qss[:, 2, :])
                    link(nc.vector.tensor_scalar(qss[:, 3, :], qss[:, 1, :], SCALE, None, ALU.mult))
                if e == U_Q + 44:
                    z_job(10)
                if e == U_Q + 46:
                    conv(0)
                if e == U_Q + 47:
                    conv(1)
                if e == U_Q + 48:
                    z_job(11)
                for _ in range(ada_steps(u)):
                    ada_step()
                split_lo(u, slot_in(u)[0])
            conv(2)
            conv(3)
            for c in range(4):
                dve.wait_ge(o_hi, c + 1)
                dve.wait_ge(conv_y, c + 1)
                nc.vector.tensor_tensor(hlo[:, 12 + c, :], gpre[:, c, :], hhi[:, 12 + c, :].bitcast(F32),
                                        ALU.subtract).then_inc(o_lo, 1)

            dve.wait_ge(mask_in, 32)

            def row_max(i):
                h, n = divmod(i, NQB)
                s0 = 1024 * (i % 2)
                lo, w = key_window(i)
                dve.wait_ge(s_done, i + 1)
                if h >= A_HEADS:
                    if n > 0:
                        left = psf[:, s0 + 512 - w:s0 + 512 - w + P]
                        link(nc.vector.tensor_tensor(left, left, maskl[:], ALU.add))
                    if n < NQB - 1:
                        right = psf[:, s0 + 512 - P:s0 + 512]
                        link(nc.vector.tensor_tensor(right, right, maskr[:], ALU.add))
                link(nc.vector.tensor_reduce(mx[:, i:i + 1], psf[:, s0 + 512 - w:s0 + TOK], AX.X, ALU.max))
                if h < A_HEADS:
                    nc.vector.tensor_scalar(nb[:, i:i + 1], mx[:, i:i + 1], qss[:, 3, i:i + 1], -1.0,
                                            ALU.mult, ALU.mult).then_inc(nb_done, 1)
                else:
                    link(nc.vector.tensor_scalar(mx[:, i:i + 1], mx[:, i:i + 1], SCALE,
                                                 sinkc[:, h - A_HEADS:h - A_HEADS + 1], ALU.mult, ALU.max))
                    nc.vector.tensor_scalar(nb[:, i:i + 1], mx[:, i:i + 1], -1.0, None, ALU.mult)\
                        .then_inc(nb_done, 1)

            def normalise(i):
                h = i // NQB
                lo, w = key_window(i)
                dve.wait_ge(p_done, i + 1)
                if h >= A_HEADS:
                    dve.wait_ge(es_done, i - NQB * A_HEADS + 1)
                    link(nc.vector.tensor_tensor(rsum[:, i:i + 1], rsum[:, i:i + 1], esink[:, i:i + 1], ALU.add))
                link(nc.vector.reciprocal(rinv[:, i:i + 1], rsum[:, i:i + 1]))
                p = prob[i % 3][:, 512 - w:TOK]
                nc.vector.tensor_scalar(p, p, rinv[:, i:i + 1], None, ALU.mult).then_inc(pn_done, 1)

            def keep_pt(i):
                h, n = divmod(i, NQB)
                dve.wait_ge(pt_turned, i + 1)
                if h >= 2:
                    dve.wait_ge(o_done, h - 1)
                nc.vector.tensor_copy(pt[:, h % 2, 4:6, P * n:P * n + P],
                                      PS[:, 5, 0:CTX].rearrange("p (k n) -> p k n", n=P)).then_inc(pt_ctx, 1)

            def keep_o_lo(h):
                dve.wait_ge(o_hi, 4 + h + 1)
                nc.vector.tensor_tensor(hlo[:, h, :], PS[:, 6 + h % 2, :], hhi[:, h, :].bitcast(F32), ALU.subtract)\
                    .then_inc(o_lo, 1)

            for i in range(4 * HEADS + LAG):
                if i < 4 * HEADS:
                    row_max(i)
                if 1 <= i <= 4 * HEADS:
                    normalise(i - 1)
                if i >= LAG:
                    keep_pt(i - LAG)
                if i % 4 == 0 and i > 4:
                    keep_o_lo(i // 4 - 2)
            keep_o_lo(HEADS - 1)

            def y_job(j):
                dve.wait_ge(unit_used, U_OUT + 4 * j + 4)
                for s in range(2):
                    nc.vector.tensor_copy(yT[:, 2 * j + s, :], PS[:, 2 * (j % 2) + s, :]).then_inc(bank_dve, 1)

            def y_sums(j):
                for s in range(2):
                    n = 2 * j + s
                    dve.wait_ge(y_sq, n + 1)
                    if n == 0:
                        nc.vector.tensor_copy(jst[:, 2, :], jst[:, 0, :]).then_inc(y_sqsum, 1)
                    else:
                        dve.wait_ge(y_sqsum, n)
                        nc.vector.tensor_tensor(jst[:, 2, :], jst[:, 2, :], jst[:, s, :], ALU.add)\
                            .then_inc(y_sqsum, 1)

            for u in range(U_OUT + 4, U_FFN + 4):
                e = u - 3
                if (e - U_OUT) % 4 == 0:
                    y_job((e - U_OUT) // 4 - 1)
                if (e - U_OUT) % 4 == 1 and e > U_OUT + 4:
                    y_sums((e - U_OUT) // 4 - 1)
                for _ in range(ada_steps(u)):
                    ada_step()
                split_lo(u, slot_in(u)[0] if u < U_FFN else u - U_FFN)
            y_sums(OUT_JOBS - 1)
            mod_block(7)
            dve.wait_ge(mod_add, 8)
            nc.vector.tensor_tensor(gain[:, 2, :], modc[:, 32:48], g_mix_post, ALU.mult).then_inc(mods, 1)
            nc.vector.scalar_tensor_tensor(gain[:, 3, :], modc[:, 64:80], 1.0, g_ffn_pre, ALU.add, ALU.mult)\
                .then_inc(mods, 1)
            nc.vector.tensor_tensor(gain[:, 4, :], modc[:, 80:96], g_ffn_post, ALU.mult).then_inc(mods, 1)
            dve.wait_ge(mods, 7)

            dve.wait_ge(y_stat, 1)
            rsqrt_head(4, jst[:, 3, :], PS[:, 6, :], D)
            rsqrt_tail(4, jst[:, 3, :], jst[:, 4, :], jst[:, 5, :])
            for j in range(KC + 1):
                if j < KC:
                    if j >= 2:
                        dve.wait_ge(x1_done, j - 1)
                    nc.vector.scalar_tensor_tensor(jst[:, 6 + j % 2, :], yT[:, j, :], gain[:, 2, j:j + 1],
                                                   jst[:, 4, :], ALU.mult, ALU.mult).then_inc(x1_u, 1)
                if j:
                    dve.wait_ge(x1_u, j)
                    dve.wait_ge(x2_turned, j)
                    nc.vector.tensor_tensor(yT[:, j - 1, :], PS[:, 4 + (j - 1) % 2, :], jst[:, 6 + (j - 1) % 2, :],
                                            ALU.add).then_inc(x1_done, 1)
            dve.wait_ge(x1_sum, KC)
            rsqrt_head(5, jst[:, 3, :], PS[:, 7, :], D)
            for j in range(KC):
                nc.vector.memset(facc[:, j, :], 0.0).then_inc(facc_done, 1)
            rsqrt_tail(5, jst[:, 3, :], jst[:, 4, :], jst[:, 5, :])
            for j in range(KC + 1):
                if j < KC:
                    if j >= 3:
                        dve.wait_ge(h2_lo, j - 2)
                    nc.vector.scalar_tensor_tensor(jst[:, H2_BUF[j % 3], :], yT[:, j, :], gain[:, 3, j:j + 1],
                                                   jst[:, 4, :], ALU.mult, ALU.mult).then_inc(h2_t, 1)
                if j:
                    dve.wait_ge(h2_hi, j)
                    nc.vector.scalar_tensor_tensor(hlo[:, j - 1, :], jst[:, H2_BUF[(j - 1) % 3], :],
                                                   modc[:, 47 + j:48 + j], hhi[:, j - 1, :].bitcast(F32),
                                                   ALU.add, ALU.subtract).then_inc(h2_lo, 1)

            def f_sums(d):
                for s in range(2):
                    n = 2 * d + s
                    dve.wait_ge(f_sq, n + 1)
                    if n == 0:
                        nc.vector.tensor_copy(tst[:, 3, :], tsq[:, 0, :]).then_inc(f_sqsum, 1)
                    else:
                        dve.wait_ge(f_sqsum, n)
                        nc.vector.tensor_tensor(tst[:, 3, :], tst[:, 3, :], tsq[:, s, :], ALU.add)\
                            .then_inc(f_sqsum, 1)

            def ffn(g, last):
                for r in range(GROUP_UNITS):
                    if r in (7, 15):
                        half = r // 8
                        dve.wait_ge(unit_used, U_FFN + 1 + r + GROUP_UNITS * g)
                        for s in range(2):
                            dve.wait_ge(gate_done, 4 * g + 2 * half + s + 1)
                            nc.vector.tensor_tensor(sg[:, s, :], PS[:, 2 + s, :], sg[:, s, :], ALU.mult)\
                                .then_inc(hid_done, 1)
                        for s in range(2):
                            dve.wait_ge(hid_hi, 4 * g + 2 * half + s + 1)
                            nc.vector.tensor_tensor(hidlo[:, 2 * half + s, :], sg[:, s, :],
                                                    hidhi[:, 2 * half + s, :].bitcast(F32), ALU.subtract)\
                                .then_inc(hid_lo, 1)
                    if r >= 16:
                        d = r - 16
                        dve.wait_ge(unit_used, U_FFN + 1 + r + GROUP_UNITS * g)
                        for s in range(2):
                            y = facc[:, 2 * d + s, :]
                            nc.vector.tensor_tensor(y, PS[:, 2 * (d % 2) + s, :], y, ALU.add)\
                                .then_inc(facc_done, 1)
                        if last and d:
                            f_sums(d - 1)
                    if not (last and r >= GROUP_UNITS - RING):
                        dve.wait_ge(hi_ready, U_FFN + RING + 1 + r + GROUP_UNITS * g)
                        nc.vector.tensor_tensor(wlo[:, r % RING, :], stage[:, r % RING, :],
                                                whi[:, r % RING, :].bitcast(F32), ALU.subtract).then_inc(lo_ready, 1)

            with dve.Fori(0, GROUPS - 1) as g:
                ffn(g, False)
            ffn(GROUPS - 1, True)

            f_sums(7)
            dve.wait_ge(f_stat, 1)
            rsqrt_head(6, tst[:, 0, :], PS[:, 4, :], D)
            rsqrt_tail(6, tst[:, 0, :], tst[:, 1, :], tst[:, 2, :])
            def keep_out(c):
                dve.wait_ge(o_turned, c + 1)
                if c >= 2:
                    dve.wait_ge(stored[c % 2], 16)
                for t in (2, 3):
                    nc.vector.tensor_copy(ostage[:, c % 2, t, :], PS[:, 4 * (c % 2) + t, :]).then_inc(o_dve, 1)

            for j in range(KC):
                link(nc.vector.scalar_tensor_tensor(facc[:, j, :], facc[:, j, :], gain[:, 4, j:j + 1], tst[:, 1, :],
                                                    ALU.mult, ALU.mult))
                nc.vector.tensor_tensor(facc[:, j, :], facc[:, j, :], yT[:, j, :], ALU.add).then_inc(f_out, 1)
                if j % 4 == 1 and j > 4:
                    keep_out(j // 4 - 1)
            keep_out(3)

        @block.tensor
        def _(pe):
            mm = nc.tensor.matmul

            def three(dst, w, x, start, stop):
                (w_hi, w_lo), (x_hi, x_lo) = w, x
                mm(dst, w_hi, x_hi, start=start, stop=False)
                mm(dst, w_hi, x_lo, start=False, stop=False)
                return mm(dst, w_lo, x_hi, start=False, stop=stop)

            def wt(slot, k, s):
                n = slot * UNIT + k * UCOLS + s * P
                return (whi[:, :, :].rearrange("p r n -> p (r n)")[:, n:n + P],
                        wlo[:, :, :].rearrange("p r n -> p (r n)")[:, n:n + P])

            pe.wait_ge(const_in, 16 * N_CONST)
            nc.tensor.transpose(PS[:, 7, 0:128], rows[:, 0, :], ident[:]).then_inc(rows_turned, 1)
            nc.tensor.transpose(PS[:, 7, 128:208], rows[0:80, 1, :], ident[0:80, 0:80]).then_inc(rows_turned, 1)

            def turn_rows(b):
                pe.wait_ge(row_kept, b + 1)
                for q in range(8):
                    n = 4 * (8 * b + q)
                    last = nc.tensor.transpose(PS[:, 6, n:n + 4], row4[:, P * q:P * q + P], ident[0:4, 0:4])
                last.then_inc(row_turned, 1)

            pe.wait_ge(silp_ready, 2)
            for u in range(ADA0_UNITS):
                b, k = divmod(u, KC)
                if k == 0 and b >= 2:
                    pe.wait_ge(row_kept, b - 1)
                pe.wait_ge(lo_ready, u + 1)
                c4 = silp[:, 4 * k:4 * k + P]
                for s in range(2):
                    mm(PS[:, 2 * (b % 2) + s, :], c4, whi[:, u % RING, 512 * s:512 * s + 512],
                       start=(k == 0), stop=False)
                    last = mm(PS[:, 2 * (b % 2) + s, :], c4, wlo[:, u % RING, 512 * s:512 * s + 512],
                              start=False, stop=(k == KC - 1))
                last.then_inc(unit_used, 1)
                if 24 <= u < 48:
                    g = u - 24
                    t, c = g // 4, g % 4
                    pe.wait_ge(xhat, t + 1)
                    if g >= 2:
                        pe.wait_ge(x_kept, g - 1)
                    for i in range(4):
                        n = P * (4 * c + i)
                        last = nc.tensor.transpose(PS[:, 4 + g % 2, P * i:P * i + P], xtok[:, t, n:n + P], ident[:])
                    last.then_inc(x_turned, 1)
                if u in (21, 37, 53):
                    turn_rows((u - 21) // 16)
            turn_rows(3)

            def ada_reduce(b):
                pe.wait_ge(ada_used, 16 * b + 16)
                pe.wait_ge(mod_add, b)
                for q in range(8):
                    last = mm(PS[:, 6, q:q + 1], acc[:, P * q:P * q + P], ones[:, 0:1], start=True, stop=True)
                last.then_inc(ada_sum, 1)

            def k_units(b, first):
                for q in range(4):
                    u = U_IN + 8 * b + q
                    pe.wait_ge(lo_ready, u + 1)
                    for i in range(UCH):
                        k = UCH * q + i
                        if first:
                            pe.wait_ge(h_lo, 2 * k + 2)
                        for s in range(2):
                            w = wt(u % RING, i, s)
                            three(PS[:, s, :], w, (hhi[:, k, :], hlo[:, k, :]), k == 0, k == KC - 1)
                            last = three(PS[:, 2, CTX * s:CTX * s + CTX], w, (chi[:, k, :], clo[:, k, :]),
                                         (k, s) == (0, 0), (k, s) == (KC - 1, 1))
                    last.then_inc(unit_used, 1)

            def k_sum(s):
                pe.wait_ge(ksq, s + 1)
                if s:
                    pe.wait_ge(rms, RSQRT_STEPS + 1)
                mm(PS[:, 6, :], ones[:], ktmp[:, 2 + s, 0:SEQ], start=True, stop=True)
                mm(PS[:, 7, 0:CTX], ones[:], ktmp[:, 2 + s, SEQ:TOK], start=True, stop=True).then_inc(kstat, 1)

            def v_units(b):
                for q in range(4):
                    u = U_IN + 8 * b + 4 + q
                    pe.wait_ge(lo_ready, u + 1)
                    for i in range(UCH):
                        k = UCH * q + i
                        w = (whi[:, u % RING, UCOLS * i:UCOLS * i + UCOLS],
                             wlo[:, u % RING, UCOLS * i:UCOLS * i + UCOLS])
                        for t in range(6):
                            if t < 4:
                                x = (hhi[:, k, P * t:P * t + P], hlo[:, k, P * t:P * t + P])
                            else:
                                x = (chi[:, k, P * (t - 4):P * (t - 3)], clo[:, k, P * (t - 4):P * (t - 3)])
                            last = three(PS[:, 3 + t // 2, UCOLS * (t % 2):UCOLS * (t % 2) + UCOLS], x, w,
                                         k == 0 and t % 2 == 0, k == KC - 1 and t % 2 == 1)
                    last.then_inc(unit_used, 1)
                    if b == 0 and q in (1, 2):
                        k_sum(q - 1)
                    if (b, q) == (0, 3):
                        pe.wait_ge(rms, 2 * RSQRT_STEPS + 1)
                        ada_reduce(0)
                    if (b, q) == (1, 1):
                        ada_reduce(1)

            def banks_empty(n_act, n_dve):
                pe.wait_ge(bank_act, n_act)
                pe.wait_ge(bank_dve, n_dve)

            k_units(0, True)
            v_units(0)
            banks_empty(2, 1)
            k_units(1, False)
            banks_empty(4, 2)
            v_units(1)
            banks_empty(8, 4)

            def product(banks, slot, q, first, last_, x=(hhi, hlo), chunk_ready=None):
                for i in range(UCH):
                    k = UCH * q + i
                    if chunk_ready:
                        chunk_ready(i)
                    for s in range(2):
                        last = three(PS[:, banks + s, :], wt(slot, i, s), (x[0][:, k, :], x[1][:, k, :]),
                                     first and i == 0, last_ and i == UCH - 1)
                return last

            def q_sum(j):
                pe.wait_ge(qsq_made, 2 * j + 2)
                for s in range(2):
                    for n in range(NQB):
                        c = NQB * (2 * j + s) + n
                        last = mm(PS[:, 7, c:c + 1], qsq[:, s, P * n:P * n + P], ones[:, 0:1], start=True, stop=True)
                last.then_inc(qsum, 1)

            def q_units(i3, sums):
                for r in range(3):
                    pe.wait_ge(bank_act, 4 + 2 * r + 6 * i3)
                    for q in range(4):
                        n = 4 * r + q
                        pe.wait_ge(lo_ready, U_Q + 1 + n + 12 * i3)
                        product(2 * r, n % RING, q, q == 0, q == 3).then_inc(unit_used, 1)
                        if n == 9:
                            ada_reduce(2 + i3)
                        if n in sums:
                            q_sum(sums[n])

            q_units(0, {6: 0, 10: 1})
            q_units(1, {2: 2})
            with pe.Fori(2, 4) as i3:
                q_units(i3, {})

            pe.wait_ge(bank_act, 28)
            pe.wait_ge(zdone, 6)
            pe.wait_ge(rms, 3 * RSQRT_STEPS + 1)

            def scores(i):
                h, n = divmod(i, NQB)
                kv = h // GROUP
                lo, w = key_window(i)
                if n == 0:
                    pe.wait_ge(qdone, h + 1)
                if i >= 2:
                    pe.wait_ge(p_done, i - 1)
                s0 = 1024 * (i % 2)
                qb = qT[:, h, P * n:P * n + P]
                mm(psf[:, s0 + 512 - w:s0 + 512], qb, kT[:, kv, lo:lo + w], start=True, stop=True)
                mm(psf[:, s0 + 512:s0 + TOK], qb, kT[:, kv, SEQ:TOK], start=True, stop=True).then_inc(s_done, 1)

            def turn(i):
                lo, w = key_window(i)
                pe.wait_ge(pn_done, i + 1)
                if i:
                    pe.wait_ge(pt_lat, i)
                    pe.wait_ge(pt_ctx, i)
                for k in range(w // P):
                    s = 512 - w + P * k
                    nc.tensor.transpose(psf[:, 2048 + lo + P * k:2048 + lo + P * k + P], prob[i % 3][:, s:s + P], ident[:])
                for k in range(2):
                    last = nc.tensor.transpose(PS[:, 5, P * k:P * k + P], prob[i % 3][:, 512 + P * k:640 + P * k], ident[:])
                last.then_inc(pt_turned, 1)

            def values(h):
                kv = h // GROUP
                pe.wait_ge(pt_lat, 4 * h + 4)
                pe.wait_ge(pt_ctx, 4 * h + 4)
                if h == 0:
                    pe.wait_ge(mod_add, 6)
                if h >= 2:
                    pe.wait_ge(o_lo, 4 + h - 1)
                o = PS[:, 6 + h % 2, :]
                mm(o, vv[:, 4, P * kv:P * kv + P], pt[:, h % 2, 4, :], start=True, stop=False)
                mm(o, vv[:, 5, P * kv:P * kv + P], pt[:, h % 2, 5, :], start=False, stop=False)
                for k in range(4):
                    q0, q1 = (0, SEQ) if h < A_HEADS else (P * max(k - 1, 0), P * min(k + 2, NQB))
                    last = mm(o[:, q0:q1], vv[:, k, P * kv:P * kv + P], pt[:, h % 2, k, q0:q1], start=False,
                              stop=(k == 3))
                last.then_inc(o_done, 1)

            for i in range(4 * HEADS + LAG):
                if i < 4 * HEADS:
                    scores(i)
                if i % 4 == 2 and i > 4:
                    values(i // 4 - 1)
                if i >= LAG:
                    turn(i - LAG)
            values(HEADS - 1)

            pe.wait_ge(o_lo, 4 + HEADS)
            pe.wait_ge(p_done, 4 * HEADS)
            with pe.Fori(0, 2) as i4:
                for r in range(4):
                    pe.wait_ge(bank_dve, 2 + 2 * r + 8 * i4)
                    for q in range(4):
                        n = 4 * r + q
                        pe.wait_ge(lo_ready, U_OUT + 1 + n + 16 * i4)
                        product(2 * (r % 2), n % RING, q, q == 0, q == 3).then_inc(unit_used, 1)
                        if n == 13:
                            ada_reduce(6 + i4)

            def turn_x(j):
                if j >= 2:
                    pe.wait_ge(x1_done, j - 1)
                for t in range(NQB):
                    last = nc.tensor.transpose(PS[:, 4 + j % 2, P * t:P * t + P], xtok2[:, t, P * j:P * j + P], ident[:])
                last.then_inc(x2_turned, 1)

            pe.wait_ge(x2_in, 64)
            turn_x(0)
            turn_x(1)
            pe.wait_ge(y_sqsum, KC)
            pe.wait_ge(mod_add, 8)
            mm(PS[:, 6, :], ones[:], jst[:, 2, :], start=True, stop=True).then_inc(y_stat, 1)
            for j in range(KC):
                if j + 2 < KC:
                    turn_x(j + 2)
                pe.wait_ge(x1_sq, j + 1)
                mm(PS[:, 7, :], ones[:], jst[:, j % 2, :], start=(j == 0), stop=(j == KC - 1)).then_inc(x1_sum, 1)

            def ffn(g):
                r = 0
                for job in range(4):
                    if job < 2:
                        pe.wait_ge(facc_done, 14 + 2 * job + 16 * g)
                    elif job == 2:
                        pe.wait_ge(gate_done, 2 + 4 * g)
                    else:
                        pe.wait_ge(hid_done, 2 + 4 * g)
                    for q in range(4):
                        pe.wait_ge(lo_ready, U_FFN + 1 + r + GROUP_UNITS * g)
                        if job == 0:
                            pe.wait_ge(h2_lo, UCH * q + UCH)
                        product(2 * (job % 2), r % RING, q, q == 0, q == 3).then_inc(unit_used, 1)
                        r += 1
                for d in range(8):
                    if d == 0:
                        pe.wait_ge(gate_done, 4 + 4 * g)
                    elif d >= 2:
                        pe.wait_ge(facc_done, 16 + 2 * (d - 1) + 16 * g)
                    pe.wait_ge(lo_ready, U_FFN + 1 + r + GROUP_UNITS * g)
                    product(2 * (d % 2), r % RING, 0, True, True, (hidhi, hidlo),
                            (lambda i: pe.wait_ge(hid_lo, 1 + i + 4 * g)) if d == 0 else None).then_inc(unit_used, 1)
                    r += 1

            with pe.Fori(0, GROUPS) as g:
                ffn(g)

            pe.wait_ge(f_sqsum, KC)
            mm(PS[:, 4, :], ones[:], tst[:, 3, :], start=True, stop=True).then_inc(f_stat, 1)
            for c in range(4):
                pe.wait_ge(f_out, 4 * c + 4)
                if c >= 2:
                    pe.wait_ge(o_act, 2 * (c - 1))
                    pe.wait_ge(o_dve, 2 * (c - 1))
                for t in range(NQB):
                    for i in range(4):
                        last = nc.tensor.transpose(PS[:, 4 * (c % 2) + t, P * i:P * i + P],
                                                   facc[:, 4 * c + i, P * t:P * t + P], ident[:])
                last.then_inc(o_turned, 1)


def shape_constants():
    import numpy as np

    grid_w, pairs = 64, P // 4
    inv = np.power(10000.0, -np.arange(pairs) / pairs).astype(np.float32)
    t = np.arange(SEQ)
    place = (t // grid_w, t % grid_w)
    cos, sin = np.zeros((P, SEQ), np.float32), np.zeros((P, SEQ), np.float32)
    for p in range(P):
        axis, half, i = p // 64, (p // 32) % 2, p % 32
        angle = place[axis].astype(np.float32) * inv[i]
        cos[p] = np.cos(angle.astype(np.float64))
        sin[p] = np.sin(angle.astype(np.float64)) * (1 if half else -1)
    q, k = np.arange(P)[:, None], np.arange(P)[None, :]
    return {
        "ident": np.eye(P, dtype=np.float32), "rope_cos": cos, "rope_sin": sin,
        "mask_left": np.where(k >= q, 0, NEG).astype(np.float32),
        "mask_right": np.where(k <= q, 0, NEG).astype(np.float32),
    }


_INS = ["x", "c", "ctx", "c_ctx", "w_ada", "b_ada", "g_mix_pre", "g_mix_post", "g_ffn_pre", "g_ffn_post",
        "w_in", "q_norm", "k_norm", "sink", "conv_w", "w_out", "w_gate", "w_up", "w_down"]


def kernel(**inputs):
    import concourse.bacc as bacc
    import numpy as np
    from concourse.bass_utils import run_bass_kernel_spmd

    nc = bacc.Bacc("TRN2", target_bir_lowering=False, num_devices=1)
    arrays, args = {}, {}
    given = {name: np.ascontiguousarray(inputs[name]) for name in _INS}
    given.update(shape_constants())
    for name, v in given.items():
        arrays[f"in_{name}"] = v
        ap = nc.dram_tensor(f"in_{name}", v.shape, mybir.dt.from_np(v.dtype), kind="ExternalInput").ap()
        if name in _INS and name not in ("c", "c_ctx"):
            ap = ap[0]
        args[name] = ap
    out = nc.dram_tensor("out", (1, SEQ, D), F32, kind="ExternalOutput").ap()
    hybrid_block(nc, args, out[0])
    r = run_bass_kernel_spmd(nc, [arrays], core_ids=[0])
    return r.results[0]["out"]
```

```python
from contextlib import ExitStack

import concourse.bass as bass
from concourse import mybir

ALU = mybir.AluOpType
ACT = mybir.ActivationFunctionType
AX = mybir.AxisListType
F32 = mybir.dt.float32
F32R = mybir.dt.float32r

P = 128
D = 2048
KC = D // P
SEQ = 512
CTX = 256
TOK = SEQ + CTX
NQB = SEQ // P
HEADS = 12
A_HEADS = 6
GROUP = 3
FFN = 5632
EPS = 1e-6
NEG = -1e30
SCALE = float(P) ** -0.5

UCOLS = 256
UCH = 4
UNIT = UCH * UCOLS
RING = 4
ADA0_UNITS = 64
KV_JOBS = 4
CONV_JOBS = 6
Q_JOBS = 6
IN_JOBS = KV_JOBS + CONV_JOBS + Q_JOBS
OUT_JOBS = 8
GROUPS = FFN // (4 * P)
GROUP_UNITS = 24
U_IN = ADA0_UNITS
U_OUT = U_IN + 4 * IN_JOBS
U_FFN = U_OUT + 4 * OUT_JOBS
U_END = U_FFN + GROUPS * GROUP_UNITS
U_C = U_IN + 4 * KV_JOBS
U_Q = U_C + 4 * CONV_JOBS
RSQRT_STEPS = 7
ADA_ITEM = 4
LAG = 2
OUT_ORDER = (0, 3, 1, 2)

BASE = 16512
R_H = BASE
R_C = R_H + 65536
R_QKV = R_C + 32768
R_STAGE = R_QKV + 49152
R_WHI = R_STAGE + 16384
R_WLO = R_WHI + 16384
R_ACC = R_WLO + 16384
R_SMALL = R_ACC + 4096


def slot_in(u):
    v = u - U_IN
    return v % 2, ADA0_UNITS // 4 + v // 2 + 1


def ada_steps(u):
    if u < U_C:
        return (1, 1, 2)[(u - U_IN - RING) % 3]
    if u < U_OUT:
        return (2, 1, 1, 1, 2, 1, 1, 1, 2, 1, 1, 2)[(u - U_C) % 12]
    if U_OUT + 5 <= u < U_OUT + 29:
        return (2, 1, 1)[(u - U_OUT - 5) % 3]
    return 0


def ffn_fills(slot):
    return ADA0_UNITS // 4 + (2 * (IN_JOBS + OUT_JOBS) if slot < 2 else 0)


def key_window(i):
    h, n = divmod(i, NQB)
    if h < A_HEADS:
        return 0, SEQ
    lo, hi = max(n - 1, 0), min(n + 2, NQB)
    return P * lo, P * (hi - lo)


def hybrid_block(nc, a, out):
    ctx = ExitStack()

    def sb(name, shape, at, dt=F32):
        return nc.alloc_sbuf_tensor_at(name, shape, dt, offset=at)

    def sem(name):
        return ctx.enter_context(nc.semaphore(name))

    with ctx:
        PS = ctx.enter_context(nc.psum_tensor("PS", [P, 8, 512], F32))
        psf = PS[:, :, :].rearrange("p b n -> p (b n)")

        xtok = sb("xtok", [P, 6, D], R_H)
        junk = sb("junk", [P, D], R_H + 49152)
        row4 = sb("row4", [4, 1024], R_H + 57344)
        hhi = sb("hhi", [P, KC, SEQ], R_H, F32R)
        hlo = sb("hlo", [P, KC, SEQ], R_H + 32768, F32R)
        tsq = sb("tsq", [P, 2, SEQ], R_H)
        fsum = sb("fsum", [P, SEQ], R_H + 4096)
        otok = sb("otok", [P, NQB, D], R_H + 32768)

        chi = sb("chi", [P, KC, CTX], R_C, F32R)
        clo = sb("clo", [P, KC, CTX], R_C + 16384, F32R)
        qraw = sb("qraw", [P, 2, SEQ], R_C)
        qsq = sb("qsq", [P, 2, SEQ], R_C + 4096)
        qsw = sb("qsw", [P, 2, SEQ], R_C + 8192)
        gpre = sb("gpre", [P, 4, SEQ], R_C + 12288)
        gpost = sb("gpost", [P, 4, SEQ], R_C)
        zpad = sb("zpad", [P, 4, SEQ + 2], R_C + 20480)
        pt = sb("pt", [P, 2, 6, SEQ], R_C)
        prob = [sb(f"prob{n}", [P, TOK], R_C + 24576 + 3072 * n) for n in range(2)]
        ytok = sb("ytok", [P, NQB, D], R_C)

        xT = sb("xT", [P, KC, TOK], R_QKV)
        qT = sb("qT", [P, HEADS, SEQ], R_QKV)
        kT = sb("kT", [P, 4, TOK], R_QKV + 24576)
        vv = sb("vv", [P, 6, 512], R_QKV + 36864)
        ktmp = sb("ktmp", [P, 8, TOK], R_QKV)
        xtok2 = sb("xtok2", [P, NQB, D], R_QKV)
        grow = sb("grow", [P, D], R_QKV + 32768)
        h2t = sb("h2t", [P, 3, SEQ], R_QKV + 32768)
        diag = sb("diag", [P, KC, P], R_QKV + 40960)
        facc = sb("facc", [P, KC, SEQ], R_QKV)
        hidhi = sb("hidhi", [P, 4, SEQ], R_QKV + 32768, F32R)
        hidlo = sb("hidlo", [P, 4, SEQ], R_QKV + 40960, F32R)

        stage = sb("stage", [P, RING, UNIT], R_STAGE)
        whi = sb("whi", [P, RING, UNIT], R_WHI, F32R)
        wlo = sb("wlo", [P, RING, UNIT], R_WLO, F32R)
        rows = sb("rows", [P, 2, P], R_ACC)
        acc = sb("acc", [P, 1024], R_ACC)
        sg = sb("sg", [P, 2, SEQ], R_ACC)

        at = [R_SMALL]

        def small(name, shape, dt=F32):
            n = 4
            for s in shape[1:]:
                n *= s
            t = sb(name, shape, at[0], dt)
            at[0] += (n + 31) // 32 * 32
            return t

        ident = small("ident", [P, P])
        ones = small("ones", [P, P])
        prob.append(sb("prob2", [P, TOK], at[0]))
        cosT = small("cosT", [P, SEQ])
        sinT = small("sinT", [P, SEQ])
        maskl = small("maskl", [P, P])
        maskr = small("maskr", [P, P])
        colA = small("colA", [P, 128])
        colB = small("colB", [P, 80])
        sil = small("sil", [P, 32])
        silp = small("silp", [P, 64 + 124], F32R)
        msum = small("msum", [P, 32, 4])
        modc = small("modc", [P, 96])
        adac = small("adac", [P, 8])
        modx = small("modx", [P, 32])
        gain = small("gain", [P, 5, KC])
        xss = small("xss", [P, 4, 6])
        qss = small("qss", [P, 4, 24])
        yss = small("yss", [P, NQB, OUT_JOBS])
        tss = small("tss", [P, 3, 4, NQB])
        ysq = small("ysq", [P, UCOLS])
        sinkc = small("sinkc", [P, A_HEADS])
        mx = small("mx", [P, 48])
        nb = small("nb", [P, 48])
        rsum = small("rsum", [P, 48])
        rinv = small("rinv", [P, 48])
        esink = small("esink", [P, 48])
        assert at[0] <= 229368

        bA = colA[:, 0:96]
        cA = colA[:, 96:128]
        g_mix_pre, g_mix_post = colB[:, 0:16], colB[:, 16:32]
        g_ffn_pre, g_ffn_post = colB[:, 32:48], colB[:, 48:64]

        def tap(t, c):
            return colB[:, 64 + 4 * t + c:65 + 4 * t + c]

        qg, kg, qgs, kgs = (colB[:, n:n + 1] for n in (76, 77, 78, 79))

        v_ada = a["w_ada"].rearrange("(k p) n -> p k n", p=P)
        v_in = a["w_in"].rearrange("(k p) n -> p k n", p=P)
        v_out = a["w_out"].rearrange("(k p) n -> p k n", p=P)
        v_gate = a["w_gate"].rearrange("(k p) n -> p k n", p=P)
        v_up = a["w_up"].rearrange("(k p) n -> p k n", p=P)
        v_down = a["w_down"].rearrange("(k p) n -> p k n", p=P)
        o_tok = out.rearrange("(t p) n -> p t n", p=P)
        facc_tok = facc[:, :, :].rearrange("p (c t) n -> p c t n", c=4)

        const_in = sem("const_in")
        mask_in = sem("mask_in")
        x_in = [sem(f"x_in{t}") for t in range(6)]
        x2_in = sem("x2_in")
        stage_in = [sem(f"stage_in{s}") for s in range(RING)]
        ada_in = [sem(f"ada_in{s}") for s in range(2)]
        setup = sem("setup")
        rows_turned = sem("rows_turned")
        cols_ready = sem("cols_ready")
        silu_ready = sem("silu_ready")
        silp_ready = sem("silp_ready")
        hi_ready = sem("hi_ready")
        lo_ready = sem("lo_ready")
        unit_used = sem("unit_used")
        rms = sem("rms")
        xsq = sem("xsq")
        xhat = sem("xhat")
        x_turned = sem("x_turned")
        x_kept = sem("x_kept")
        row_kept = sem("row_kept")
        row_turned = sem("row_turned")
        mods = sem("mods")
        h_t = sem("h_t")
        h_hi = sem("h_hi")
        h_lo = sem("h_lo")
        ada_used = sem("ada_used")
        ada_sum = sem("ada_sum")
        ada_kept = sem("ada_kept")
        mod_add = sem("mod_add")
        bank_act = sem("bank_act")
        bank_dve = sem("bank_dve")
        ksq = sem("ksq")
        kstat = sem("kstat")
        kswap = sem("kswap")
        kdone = sem("kdone")
        qswap = sem("qswap")
        qsq_made = sem("qsq_made")
        qsum = sem("qsum")
        qdone = sem("qdone")
        zdone = sem("zdone")
        conv_y = sem("conv_y")
        dchain = sem("dchain")
        s_done = sem("s_done")
        nb_done = sem("nb_done")
        p_done = sem("p_done")
        es_done = sem("es_done")
        pn_done = sem("pn_done")
        pt_turned = sem("pt_turned")
        pt_kept = sem("pt_kept")
        o_done = sem("o_done")
        o_hi = sem("o_hi")
        o_lo = sem("o_lo")
        g_diag = sem("g_diag")
        g_row = sem("g_row")
        g_kept = sem("g_kept")
        y_sq = sem("y_sq")
        y_gated = sem("y_gated")
        x1_done = sem("x1_done")
        x1_sq = sem("x1_sq")
        x1_diag = sem("x1_diag")
        facc_zero = sem("facc_zero")
        h2_turned = sem("h2_turned")
        h2_t = sem("h2_t")
        h2_hi = sem("h2_hi")
        h2_lo = sem("h2_lo")
        gate_done = sem("gate_done")
        hid_done = sem("hid_done")
        hid_hi = sem("hid_hi")
        hid_lo = sem("hid_lo")
        facc_done = sem("facc_done")
        f_sq = sem("f_sq")
        f_sqsum = sem("f_sqsum")
        f_stat = sem("f_stat")
        f_scaled = sem("f_scaled")
        f_turned = sem("f_turned")
        f_kept_act = sem("f_kept_act")
        f_kept_dve = sem("f_kept_dve")
        o_made = sem("o_made")
        stored = sem("stored")

        block = ctx.enter_context(nc.Block())
        N_CONST = 3 + 4 + 4 + 3 + 4

        @block.sync
        def _(sp):
            def w_load(slot, src):
                sp.dma_start(stage[:, slot, :].rearrange("p (k n) -> p k n", k=UCH), src).then_inc(stage_in[slot], 16)

            for b in range(4):
                for k in range(KC):
                    u = 16 * b + k
                    if u >= RING:
                        sp.wait_ge(lo_ready, u - RING + 1)
                    sp.dma_start(stage[:, u % RING, :], v_ada[:, k, 1024 * b:1024 * b + 1024])\
                        .then_inc(stage_in[u % RING], 16)
            for q in range(2):
                sp.wait_ge(lo_ready, U_IN - 3 + q)
                w_load(q, v_in[:, 4 * q:4 * q + 4, 0:UCOLS])
            for q in (2, 3):
                sp.wait_ge(lo_ready, U_IN + q - 1)
                w_load(q % 2, v_in[:, 4 * q:4 * q + 4, 0:UCOLS])
            for start, end, job in ((1, KV_JOBS, 1), (KV_JOBS + Q_JOBS, IN_JOBS, KV_JOBS),
                                    (KV_JOBS, KV_JOBS + Q_JOBS, KV_JOBS + CONV_JOBS)):
                with sp.Fori(start, end) as j:
                    for q in range(4):
                        sp.wait_ge(lo_ready, U_IN - 1 + q + 4 * (job - start) + 4 * j)
                        w_load(q % 2, v_in[:, 4 * q:4 * q + 4, bass.ds(j * UCOLS, UCOLS)])
            with sp.Fori(0, OUT_JOBS) as j:
                for q in range(4):
                    k = UCH * OUT_ORDER[q]
                    src = v_out[:, k:k + UCH, bass.ds(j * UCOLS, UCOLS)]
                    sp.wait_ge(lo_ready, U_OUT - 1 + q + 4 * j)
                    w_load(q % 2, src)
            sp.wait_ge(lo_ready, U_FFN)
            sp.wait_ge(ada_used, 128)

            def ffn_loads(g):
                r = 0
                for pair in range(2):
                    for w in (v_gate, v_up):
                        for q in range(4):
                            sp.wait_ge(lo_ready, U_FFN - 3 + r + GROUP_UNITS * g)
                            w_load(r % RING, w[:, 4 * q:4 * q + 4, bass.ds(512 * g + UCOLS * pair, UCOLS)])
                            r += 1
                for d in range(8):
                    sp.wait_ge(lo_ready, U_FFN - 3 + r + GROUP_UNITS * g)
                    w_load(r % RING, v_down[:, bass.ds(4 * g, 4), UCOLS * d:UCOLS * d + UCOLS])
                    r += 1

            with sp.Fori(0, GROUPS) as g:
                ffn_loads(g)
            for t in range(NQB):
                sp.wait_ge(o_made, 2 * t + 2)
                sp.dma_start(o_tok[:, t, :], otok[:, t, :]).then_inc(stored, 16)
            sp.wait_ge(stored, 16 * NQB)

        @block.gpsimd
        def _(pool):
            nc.gpsimd.memset(ones[:], 1.0).then_inc(setup, 1)
            nc.gpsimd.memset(silp[:, :].bitcast(F32), 0.0).then_inc(setup, 1)
            pool.wait_ge(lo_ready, ADA0_UNITS)
            for k in range(KC):
                if k >= 2:
                    pool.wait_ge(ada_used, k - 1)
                pool.dma_start(stage[:, 2 + k % 2, :], v_ada[:, k, 4096:5120]).then_inc(ada_in[k % 2], 16)
            with pool.Fori(1, 8) as b:
                for k in range(KC):
                    pool.wait_ge(ada_used, k - 1 + 16 * b)
                    pool.dma_start(stage[:, 2 + k % 2, :], v_ada[:, k, bass.ds(4096 + 1024 * b, 1024)])\
                        .then_inc(ada_in[k % 2], 16)
            pool.wait_ge(x1_done, NQB)
            nc.gpsimd.memset(facc[:, :, :].rearrange("p c n -> p (c n)"), 0.0).then_inc(facc_zero, 1)

        @block.scalar
        def _(act):
            def copy_(dst, src):
                return nc.scalar.activation(dst, src, ACT.Copy)

            def split_hi(u, slot, count):
                act.wait_ge(stage_in[slot], 16 * count)
                act.wait_ge(unit_used, u - RING + 1)
                copy_(whi[:, u % RING, :], stage[:, slot, :]).then_inc(hi_ready, 1)

            def sqrt_(use, dst, src):
                act.wait_ge(rms, RSQRT_STEPS * use + 1)
                nc.scalar.activation(dst, src, ACT.Sqrt).then_inc(rms, 1)

            ld = lambda dst, src: act.dma_start(dst, src).then_inc(const_in, 16)
            ld(rows[0:96, 0, :], a["b_ada"].rearrange("(r n) -> r n", n=P))
            ld(rows[96:112, 0, :], a["c"].rearrange("o (r n) -> (o r) n", n=P))
            ld(rows[112:128, 0, :], a["c_ctx"].rearrange("(r n) -> r n", n=P))
            for n, name in enumerate(("g_mix_pre", "g_mix_post", "g_ffn_pre", "g_ffn_post")):
                ld(rows[16 * n:16 * n + 16, 1, :], a[name].rearrange("(r n) -> r n", n=P))
            ld(rows[64:76, 1, :], a["conv_w"].rearrange("t (c n) -> (t c) n", n=P))
            ld(rows[76:77, 1, :], a["q_norm"].rearrange("(o n) -> o n", o=1))
            ld(rows[77:78, 1, :], a["k_norm"].rearrange("(o n) -> o n", o=1))
            ld(ident[:], a["ident"])
            for r, name in ((78, "q_norm"), (79, "k_norm")):
                w = a[name].rearrange("(o a h i) -> o a h i", o=1, a=2, h=2)
                d = rows[r:r + 1, 1, :].rearrange("p (a h i) -> p a h i", a=2, h=2)
                for h in range(2):
                    ld(d[:, :, h, :], w[:, :, 1 - h, :])
            ld(cosT[:], a["rope_cos"])
            ld(sinT[:], a["rope_sin"])
            ld(sinkc[:], a["sink"].rearrange("(o h) -> o h", o=1).broadcast_to([P, A_HEADS]))
            for t in range(6):
                src = a["x"][P * t:P * t + P, :] if t < 4 else a["ctx"][P * (t - 4):P * (t - 4) + P, :]
                act.dma_start(xtok[:, t, :], src).then_inc(x_in[t], 16)
            act.dma_start(maskl[:], a["mask_left"]).then_inc(mask_in, 16)
            act.dma_start(maskr[:], a["mask_right"]).then_inc(mask_in, 16)

            act.wait_ge(cols_ready, 1)
            nc.scalar.activation(sil[:], cA, ACT.Silu).then_inc(silu_ready, 1)

            def keep_row(b):
                act.wait_ge(unit_used, 16 * b + 16)
                if b:
                    act.wait_ge(row_turned, b)
                copy_(row4[:, :], psf[0:4, 1024 * (b % 2):1024 * (b % 2) + 1024]).then_inc(row_kept, 1)

            def keep_x(g):
                t, c = g // 4, g % 4
                act.wait_ge(x_turned, g + 1)
                copy_(xT[:, 4 * c:4 * c + 4, P * t:P * t + P],
                      PS[:, 4 + g % 2, :].rearrange("p (c n) -> p c n", c=4)).then_inc(x_kept, 1)

            for u in range(ADA0_UNITS):
                act.wait_ge(stage_in[u % RING], 16 * (u // RING + 1))
                if u >= RING:
                    act.wait_ge(unit_used, u - RING + 1)
                copy_(whi[:, u % RING, :], stage[:, u % RING, :]).then_inc(hi_ready, 1)
                if 4 <= u < 16 and u % 2 == 0:
                    t = (u - 4) // 2
                    act.wait_ge(x_in[t], 16)
                    if t:
                        act.wait_ge(xsq, t)
                    nc.scalar.activation(junk[:], xtok[:, t, :], ACT.Square, accum_out=xss[:, 0, t:t + 1])\
                        .then_inc(xsq, 1)
                if u == 18:
                    sqrt_(0, xss[:, 2, :], xss[:, 1, :])
                if 27 <= u < 51:
                    keep_x(u - 27)
                if u in (19, 35, 51):
                    keep_row((u - 19) // 16)
            keep_row(3)
            for u in range(U_IN, U_IN + 4):
                split_hi(u, *slot_in(u))

            act.wait_ge(x_turned, 24)
            for j in range(KC):
                act.wait_ge(h_t, 2 * j + 1)
                copy_(hhi[:, j, :], xT[:, j, 0:SEQ]).then_inc(h_hi, 1)
                act.wait_ge(h_t, 2 * j + 2)
                copy_(chi[:, j, :], xT[:, j, SEQ:TOK]).then_inc(h_hi, 1)

            def swap(dst, src, done):
                for s in range(4):
                    act.dma_start(dst[32 * (s ^ 1):32 * (s ^ 1) + 32], src[32 * s:32 * s + 32]).then_inc(done, 16)

            def k_job(b):
                act.wait_ge(unit_used, U_IN + 8 * b + 4)
                if b:
                    act.wait_ge(kdone, 2)
                else:
                    act.wait_ge(h_lo, 2 * KC)
                copy_(ktmp[:, 0, 0:SEQ], PS[:, 0, :]).then_inc(bank_act, 1)
                copy_(ktmp[:, 0:2, SEQ:TOK], PS[:, 2, :].rearrange("p (s n) -> p s n", s=2)).then_inc(bank_act, 1)
                act.wait_ge(bank_act, 4 * b + 2)
                swap(ktmp[:, 7, 0:SEQ], ktmp[:, 0, 0:SEQ], kswap)
                if b == 0:
                    nc.scalar.activation(ktmp[:, 2, :], ktmp[:, 0, :], ACT.Square).then_inc(ksq, 1)
                    act.wait_ge(bank_dve, 1)
                    nc.scalar.activation(ktmp[:, 3, :], ktmp[:, 1, :], ACT.Square).then_inc(ksq, 1)

            def k_swap_second(b):
                act.wait_ge(bank_dve, 2 * b + 1)
                act.wait_ge(kdone, 2 * b + 1)
                swap(ktmp[:, 7, 0:SEQ], ktmp[:, 1, 0:SEQ], kswap)

            def v_job(b):
                act.wait_ge(unit_used, U_IN + 8 * b + 8)
                for t in (0, 4):
                    copy_(vv[:, t:t + 2, UCOLS * b:UCOLS * b + UCOLS],
                          PS[:, 3 + t // 2, :].rearrange("p (t n) -> p t n", t=2)).then_inc(bank_act, 1)

            def conv_job(j):
                act.wait_ge(unit_used, U_C + 4 * j + 4)
                if j == 4:
                    act.wait_ge(zdone, 2)
                for s in range(2):
                    c = 2 * (j % 2) + s
                    dst = (gpre[:, c, :], gpost[:, c, :], zpad[:, c, 1:SEQ + 1])[j // 2]
                    copy_(dst, PS[:, 2 * (j % 3) + s, :]).then_inc(bank_act, 1)

            def q_job(j):
                act.wait_ge(unit_used, U_Q + 4 * j + 4)
                if j == 0:
                    act.wait_ge(kdone, 4)
                    act.wait_ge(conv_y, 4)
                else:
                    act.wait_ge(qdone, 2 * j)
                for s in range(2):
                    copy_(qraw[:, s, :], PS[:, 2 * (j % 3) + s, :]).then_inc(bank_act, 1)
                act.wait_ge(bank_act, 20 + 2 * j + 2)
                swap(qsw[:, :, :], qraw[:, :, :], qswap)
                if j < 3:
                    if j:
                        act.wait_ge(qsum, j)
                    for s in range(2):
                        nc.scalar.activation(qsq[:, s, :], qraw[:, s, :], ACT.Square).then_inc(qsq_made, 1)

            for u in range(U_IN + 4, U_OUT + 4):
                e = u - 3
                if e == U_IN + 4:
                    k_job(0)
                if e == U_IN + 6:
                    sqrt_(1, ktmp[:, 5, :], ktmp[:, 4, :])
                if e == U_IN + 7:
                    k_swap_second(0)
                if e == U_IN + 8:
                    v_job(0)
                    sqrt_(2, ktmp[:, 5, :], ktmp[:, 4, :])
                if e == U_IN + 12:
                    k_job(1)
                if e == U_IN + 14:
                    k_swap_second(1)
                if e == U_IN + 16:
                    v_job(1)
                if e > U_C and (e - U_C) % 4 == 0:
                    j = (e - U_C) // 4 - 1
                    if j < CONV_JOBS:
                        conv_job(j)
                    else:
                        q_job(j - CONV_JOBS)
                if e == U_Q + 16:
                    sqrt_(3, qss[:, 1, :], qss[:, 0, :])
                if u < U_OUT + 3:
                    split_hi(u, *slot_in(u))

            def exp_item(i):
                h = i // NQB
                s0 = 1024 * (i % 2)
                lo, w = key_window(i)
                act.wait_ge(nb_done, i + 1)
                if i == 2:
                    act.wait_ge(qdone, HEADS)
                if i >= 3:
                    act.wait_ge(pt_turned, i - 2)
                sc = qss[:, 3, i:i + 1] if h < A_HEADS else SCALE
                nc.scalar.activation(prob[i % 3][:, 512 - w:TOK], psf[:, s0 + 512 - w:s0 + TOK], ACT.Exp,
                                     bias=nb[:, i:i + 1], scale=sc, accum_out=rsum[:, i:i + 1]).then_inc(p_done, 1)
                if h >= A_HEADS:
                    nc.scalar.activation(esink[:, i:i + 1], sinkc[:, h - A_HEADS:h - A_HEADS + 1], ACT.Exp,
                                         bias=nb[:, i:i + 1]).then_inc(es_done, 1)

            def keep_pt(i):
                h, n = divmod(i, NQB)
                lo, w = key_window(i)
                act.wait_ge(pt_turned, i + 1)
                if i == NQB:
                    act.wait_ge(o_lo, 4)
                if h >= 2:
                    act.wait_ge(o_done, h - 1)
                if i == ADA_ITEM + KC - LAG:
                    copy_(adac[:], PS[:, 5, CTX:CTX + 8]).then_inc(ada_kept, 1)
                kept = pt[:, h % 2, :, P * n:P * n + P]
                turned = psf[:, 2048:2048 + TOK].rearrange("p (k n) -> p k n", n=P)
                if w == SEQ:
                    copy_(kept, turned).then_inc(pt_kept, 1)
                else:
                    copy_(kept[:, lo // P:(lo + w) // P], turned[:, lo // P:(lo + w) // P])
                    copy_(kept[:, 4:6], turned[:, 4:6]).then_inc(pt_kept, 1)

            def keep_conv_hi(c):
                act.wait_ge(conv_y, c + 1)
                copy_(hhi[:, 12 + c, :], gpre[:, c, :]).then_inc(o_hi, 1)

            def keep_o_hi(h):
                act.wait_ge(o_done, h + 1)
                copy_(hhi[:, h, :], PS[:, 6 + h % 2, :]).then_inc(o_hi, 1)

            for i in range(4 * HEADS + LAG):
                if i < 4 * HEADS:
                    exp_item(i)
                if i >= LAG:
                    keep_pt(i - LAG)
                if i == 0:
                    split_hi(U_OUT + 3, *slot_in(U_OUT + 3))
                if 1 <= i < 5:
                    keep_conv_hi(i - 1)
                if i % 4 == 1 and i > 8:
                    keep_o_hi(i // 4 - 2)
            keep_o_hi(HEADS - 1)

            for t in range(NQB):
                act.dma_start(xtok2[:, t, :], a["x"][P * t:P * t + P, :]).then_inc(x2_in, 16)

            def y_squares(j):
                for t in range(NQB):
                    act.wait_ge(bank_dve, 4 + 2 * j + t // 2 + 1)
                    if j or t:
                        act.wait_ge(y_sq, NQB * j + t)
                    nc.scalar.activation(ysq[:], ytok[:, t, UCOLS * j:UCOLS * j + UCOLS], ACT.Square,
                                         accum_out=yss[:, t, j:j + 1]).then_inc(y_sq, 1)

            def keep_gate_row(c):
                act.wait_ge(g_row, c + 1)
                copy_(grow[:, 512 * c:512 * c + 512], PS[:, 6 + c % 2, :]).then_inc(g_kept, 1)

            for u in range(U_OUT + 4, U_FFN + 4):
                e = u - 3
                if u < U_FFN:
                    split_hi(u, *slot_in(u))
                else:
                    act.wait_ge(stage_in[u - U_FFN], 16 * (ffn_fills(u - U_FFN) + 1))
                    act.wait_ge(unit_used, e)
                    copy_(whi[:, u % RING, :], stage[:, u - U_FFN, :]).then_inc(hi_ready, 1)
                if e in (U_OUT + 3, U_OUT + 4):
                    keep_gate_row(2 * (e - U_OUT - 3))
                    keep_gate_row(2 * (e - U_OUT - 3) + 1)
                if (e - U_OUT) % 4 == 0:
                    y_squares((e - U_OUT) // 4 - 1)

            sqrt_(4, tss[:, 0, 2, :], tss[:, 0, 1, :])
            for t in range(NQB):
                act.wait_ge(x1_done, t + 1)
                if t:
                    act.wait_ge(x1_sq, t)
                nc.scalar.activation(junk[:], ytok[:, t, :], ACT.Square, accum_out=tss[:, 1, 0, t:t + 1])\
                    .then_inc(x1_sq, 1)
            sqrt_(5, tss[:, 1, 2, :], tss[:, 1, 1, :])
            for j in range(KC):
                act.wait_ge(h2_turned, j + 1)
                if j >= 3:
                    act.wait_ge(h2_lo, j - 2)
                nc.scalar.activation(h2t[:, j % 3, :], PS[:, 4 + j % 2, :], ACT.Identity, bias=modc[:, 48 + j:49 + j],
                                     scale=gain[:, 3, j:j + 1]).then_inc(h2_t, 1)
                act.wait_ge(h2_t, j + 1)
                copy_(hhi[:, j, :], h2t[:, j % 3, :]).then_inc(h2_hi, 1)

            def squares(d):
                act.wait_ge(unit_used, U_END - 8)
                for j in (2 * d, 2 * d + 1):
                    act.wait_ge(facc_done, 16 * (GROUPS - 1) + j + 1)
                    if j >= 2:
                        act.wait_ge(f_sqsum, j - 1)
                    nc.scalar.activation(tsq[:, j % 2, :], facc[:, j, :], ACT.Square).then_inc(f_sq, 1)
                    act.wait_ge(f_sq, j + 1)
                    nc.scalar.activation(facc[:, j, :], facc[:, j, :], ACT.Copy, scale=gain[:, 4, j:j + 1])\
                        .then_inc(f_scaled, 1)

            def keep_f(c):
                act.wait_ge(f_turned, c + 1)
                for t in range(2):
                    copy_(facc_tok[:, c, t, :], PS[:, 4 + t, :]).then_inc(f_kept_act, 1)

            def ffn(g, last):
                for r in range(GROUP_UNITS):
                    def silu(half):
                        act.wait_ge(unit_used, U_FFN + 1 + r + GROUP_UNITS * g)
                        act.wait_ge(hid_lo, 4 * g + 2 * half)
                        for s in range(2):
                            nc.scalar.activation(sg[:, s, :], PS[:, s, :], ACT.Silu).then_inc(gate_done, 1)

                    def upper(half):
                        for s in range(2):
                            act.wait_ge(hid_done, 4 * g + 2 * half + s + 1)
                            copy_(hidhi[:, 2 * half + s, :], sg[:, s, :]).then_inc(hid_hi, 1)

                    if r in (3, 11):
                        silu(r // 8)
                    if r in (7, 15):
                        upper(r // 8)
                    if last and r >= 16:
                        squares(r - 16)
                        if r in (18, 20, 22):
                            keep_f(r // 2 - 9)
                    if not (last and r >= GROUP_UNITS - RING):
                        act.wait_ge(stage_in[r % RING], 16 * (ffn_fills(r % RING) + r // RING + 2) + 96 * g)
                        act.wait_ge(unit_used, U_FFN + 1 + r + GROUP_UNITS * g)
                        copy_(whi[:, r % RING, :], stage[:, r % RING, :]).then_inc(hi_ready, 1)

            with act.Fori(0, GROUPS - 1) as g:
                ffn(g, False)
            ffn(GROUPS - 1, True)

            sqrt_(6, tss[:, 2, 2, :], tss[:, 2, 1, :])

        @block.vector
        def _(dve):
            own = [0]

            def mark(ins):
                own[0] += 1
                ins.then_inc(dchain, 1)
                return own[0]

            def link(ins):
                dve.wait_ge(dchain, mark(ins))

            def split_lo(u, slot):
                dve.wait_ge(hi_ready, u + 1)
                nc.vector.tensor_tensor(wlo[:, u % RING, :], stage[:, slot, :], whi[:, u % RING, :].bitcast(F32),
                                        ALU.subtract).then_inc(lo_ready, 1)

            def rsqrt_head(use, dst, sums, n):
                nc.vector.tensor_scalar(dst, sums, 1.0 / n, EPS, ALU.mult, ALU.add).then_inc(rms, 1)

            def rsqrt_tail(use, mean, root, tmp):
                n = RSQRT_STEPS * use + 2
                steps = (
                    lambda: nc.vector.reciprocal(root, root),
                    lambda: nc.vector.tensor_tensor(tmp, root, root, ALU.mult),
                    lambda: nc.vector.tensor_tensor(tmp, tmp, mean, ALU.mult),
                    lambda: nc.vector.tensor_scalar(tmp, tmp, -0.5, 1.5, ALU.mult, ALU.add),
                    lambda: nc.vector.tensor_tensor(root, root, tmp, ALU.mult),
                )
                for step in steps:
                    dve.wait_ge(rms, n)
                    step().then_inc(rms, 1)
                    n += 1
                dve.wait_ge(rms, n)

            dve.wait_ge(rows_turned, 2)
            nc.vector.tensor_copy(colA[:], PS[:, 7, 0:128]).then_inc(cols_ready, 1)
            nc.vector.tensor_copy(colB[:], PS[:, 7, 128:208]).then_inc(cols_ready, 1)
            dve.wait_ge(cols_ready, 2)
            dve.wait_ge(silu_ready, 1)
            dve.wait_ge(setup, 2)
            silv = sil[:, :].rearrange("p (v k) -> p k v", v=2)
            parts = silp[:, 0:64].rearrange("p (k v) -> p k v", v=4)
            nc.vector.tensor_copy(parts[:, :, 0:2], silv).then_inc(silp_ready, 1)
            dve.wait_ge(silp_ready, 1)
            nc.vector.tensor_tensor(parts[:, :, 2:4], silv, parts[:, :, 0:2].bitcast(F32), ALU.subtract)\
                .then_inc(silp_ready, 1)

            for u in range(ADA0_UNITS):
                split_lo(u, u % RING)
                if u == 16:
                    dve.wait_ge(xsq, 6)
                    rsqrt_head(0, xss[:, 1, :], xss[:, 0, :], D)
                if u == 20:
                    rsqrt_tail(0, xss[:, 1, :], xss[:, 2, :], xss[:, 3, :])
                if 21 <= u < 45 and (u - 21) % 4 == 0:
                    t = (u - 21) // 4
                    nc.vector.tensor_scalar(xtok[:, t, :], xtok[:, t, :], xss[:, 2, t:t + 1], None, ALU.mult)\
                        .then_inc(xhat, 1)
            split_lo(U_IN, 0)
            split_lo(U_IN + 1, 1)
            dve.wait_ge(row_turned, 4)
            link(nc.vector.tensor_copy(msum[:, :, :].rearrange("p c v -> p (c v)"), PS[:, 6, 0:128]))
            link(nc.vector.tensor_tensor(msum[:, :, 0:2], msum[:, :, 0:2], msum[:, :, 2:4], ALU.add))
            nc.vector.tensor_tensor(modc[:, 0:32], msum[:, :, 0], bA[:, 0:32], ALU.add).then_inc(mods, 1)
            nc.vector.tensor_tensor(modx[:, :], msum[:, :, 1], bA[:, 0:32], ALU.add).then_inc(mods, 1)
            dve.wait_ge(mods, 2)
            nc.vector.scalar_tensor_tensor(gain[:, 0, :], modc[:, 16:32], 1.0, g_mix_pre, ALU.add, ALU.mult)\
                .then_inc(mods, 1)
            nc.vector.scalar_tensor_tensor(gain[:, 1, :], modx[:, 16:32], 1.0, g_mix_pre, ALU.add, ALU.mult)\
                .then_inc(mods, 1)
            dve.wait_ge(mods, 4)
            dve.wait_ge(x_kept, 24)

            def h_full(j):
                nc.vector.tensor_scalar(xT[:, j, 0:SEQ], xT[:, j, 0:SEQ], gain[:, 0, j:j + 1], modc[:, j:j + 1],
                                        ALU.mult, ALU.add).then_inc(h_t, 1)
                nc.vector.tensor_scalar(xT[:, j, SEQ:TOK], xT[:, j, SEQ:TOK], gain[:, 1, j:j + 1],
                                        modx[:, j:j + 1], ALU.mult, ALU.add).then_inc(h_t, 1)

            h_full(0)
            h_full(1)
            split_lo(U_IN + 2, 0)
            split_lo(U_IN + 3, 1)
            for j in range(KC):
                if j + 2 < KC:
                    h_full(j + 2)
                dve.wait_ge(h_hi, 2 * j + 1)
                nc.vector.tensor_tensor(hlo[:, j, :], xT[:, j, 0:SEQ], hhi[:, j, :].bitcast(F32), ALU.subtract)\
                    .then_inc(h_lo, 1)
                dve.wait_ge(h_hi, 2 * j + 2)
                nc.vector.tensor_tensor(clo[:, j, :], xT[:, j, SEQ:TOK], chi[:, j, :].bitcast(F32), ALU.subtract)\
                    .then_inc(h_lo, 1)

            seen = [0]

            def ada_step():
                n = seen[0]
                b, k = divmod(n, KC)
                seen[0] += 1
                w = stage[:, 2 + n % 2, :]
                if k == 0 and b not in (0, 5, 6):
                    mod_block(b - 1)
                dve.wait_ge(ada_in[n % 2], 16 * (n // 2 + 1))
                if n:
                    dve.wait_ge(ada_used, n)
                if k == 0:
                    nc.vector.tensor_scalar(acc[:], w, sil[:, k:k + 1], None, ALU.mult).then_inc(ada_used, 1)
                else:
                    nc.vector.scalar_tensor_tensor(acc[:], w, sil[:, k:k + 1], acc[:], ALU.mult, ALU.add)\
                        .then_inc(ada_used, 1)

            def mod_block(b, sums=PS[:, 6, 0:8]):
                dve.wait_ge(ada_sum, b + 1)
                nc.vector.tensor_tensor(modc[:, 32 + 8 * b:40 + 8 * b], sums,
                                        bA[:, 32 + 8 * b:40 + 8 * b], ALU.add).then_inc(mod_add, 1)

            def k_job(b):
                dve.wait_ge(unit_used, U_IN + 8 * b + 4)
                nc.vector.tensor_copy(ktmp[:, 1, 0:SEQ], PS[:, 1, :]).then_inc(bank_dve, 1)

            def k_mean(s):
                dve.wait_ge(kstat, s + 1)
                rsqrt_head(1 + s, ktmp[:, 4, :], psf[:, 3072:3072 + TOK], P)

            def k_finish(b, s):
                raw, part, res = ktmp[:, s, :], ktmp[:, 7, 0:SEQ], kT[:, 2 * b + s, :]
                dve.wait_ge(bank_dve, 2 * b + 1)
                dve.wait_ge(bank_act, 4 * b + 2)
                if b == 0:
                    rsqrt_tail(1 + s, ktmp[:, 4, :], ktmp[:, 5, :], ktmp[:, 6, :])
                    t = ktmp[:, 2 + s, :]
                    dve.wait_ge(kswap, 64 * (s + 1))
                    link(nc.vector.scalar_tensor_tensor(part, part, kgs, sinT[:], ALU.mult, ALU.mult))
                    link(nc.vector.scalar_tensor_tensor(t[:, 0:SEQ], raw[:, 0:SEQ], kg, cosT[:], ALU.mult, ALU.mult))
                    link(nc.vector.tensor_scalar(t[:, SEQ:TOK], raw[:, SEQ:TOK], kg, None, ALU.mult))
                    link(nc.vector.tensor_tensor(t[:, 0:SEQ], t[:, 0:SEQ], part, ALU.add))
                    nc.vector.tensor_tensor(res, t, ktmp[:, 5, :], ALU.mult).then_inc(kdone, 1)
                else:
                    dve.wait_ge(kswap, 64 * (s + 3))
                    link(nc.vector.tensor_tensor(part, part, sinT[:], ALU.mult))
                    link(nc.vector.tensor_tensor(res[:, 0:SEQ], raw[:, 0:SEQ], cosT[:], ALU.mult))
                    link(nc.vector.tensor_copy(res[:, SEQ:TOK], raw[:, SEQ:TOK]))
                    nc.vector.tensor_tensor(res[:, 0:SEQ], res[:, 0:SEQ], part, ALU.add).then_inc(kdone, 1)

            def v_job(b):
                dve.wait_ge(unit_used, U_IN + 8 * b + 8)
                nc.vector.tensor_copy(vv[:, 2:4, UCOLS * b:UCOLS * b + UCOLS],
                                      PS[:, 4, :].rearrange("p (t n) -> p t n", t=2)).then_inc(bank_dve, 1)

            def q_finish(j, heads=(0, 1)):
                for s in heads:
                    h = 2 * j + s
                    dve.wait_ge(bank_act, 20 + 2 * j + 2)
                    dve.wait_ge(qswap, 64 * j + 64)
                    part, res, raw = qsw[:, s, :], qT[:, h, :], qraw[:, s, :]
                    if h < A_HEADS:
                        link(nc.vector.scalar_tensor_tensor(part, part, qgs, sinT[:], ALU.mult, ALU.mult))
                        link(nc.vector.scalar_tensor_tensor(res, raw, qg, cosT[:], ALU.mult, ALU.mult))
                    else:
                        link(nc.vector.tensor_tensor(part, part, sinT[:], ALU.mult))
                        link(nc.vector.tensor_tensor(res, raw, cosT[:], ALU.mult))
                    nc.vector.tensor_tensor(res, res, part, ALU.add).then_inc(qdone, 1)

            def z_job(j):
                for s in range(2):
                    c = 2 * (j - 4) + s
                    dve.wait_ge(bank_act, 8 + 2 * j + s + 1)
                    z = zpad[:, c, 1:SEQ + 1]
                    nc.vector.tensor_tensor(z, z, gpre[:, c, :], ALU.mult).then_inc(zdone, 1)

            def conv(c):
                dve.wait_ge(zdone, 3 + c)
                y = gpre[:, c, :]
                link(nc.vector.tensor_scalar(y, zpad[:, c, 0:SEQ], tap(0, c), None, ALU.mult))
                link(nc.vector.scalar_tensor_tensor(y, zpad[:, c, 1:SEQ + 1], tap(1, c), y, ALU.mult, ALU.add))
                link(nc.vector.scalar_tensor_tensor(y, zpad[:, c, 2:SEQ + 2], tap(2, c), y, ALU.mult, ALU.add))
                nc.vector.tensor_tensor(y, y, gpost[:, c, :], ALU.mult).then_inc(conv_y, 1)

            for u in range(U_IN + 4, U_OUT + 4):
                e = u - 3
                if e == U_IN + 4:
                    k_job(0)
                if e == U_IN + 6:
                    k_mean(0)
                if e == U_IN + 7:
                    k_finish(0, 0)
                    k_mean(1)
                if e == U_IN + 8:
                    v_job(0)
                if e == U_IN + 9:
                    k_finish(0, 1)
                if e == U_IN + 12:
                    k_job(1)
                if e == U_IN + 14:
                    k_finish(1, 0)
                if e == U_IN + 15:
                    k_finish(1, 1)
                if e == U_IN + 16:
                    v_job(1)
                if e == U_C:
                    dve.wait_ge(unit_used, U_C)
                    for s in (0, SEQ + 1):
                        nc.vector.memset(zpad[:, :, s:s + 1], 0.0).then_inc(zdone, 1)
                if e > U_Q + 1 and (e - U_Q) % 4 == 1:
                    q_finish((e - U_Q) // 4 - 1)
                if e == U_Q + 15:
                    dve.wait_ge(qsum, 3)
                    rsqrt_head(3, qss[:, 0, :], PS[:, 7, 0:24], P)
                if e == U_Q + 18:
                    rsqrt_tail(3, qss[:, 0, :], qss[:, 1, :], qss[:, 2, :])
                    link(nc.vector.tensor_scalar(qss[:, 3, :], qss[:, 1, :], SCALE, None, ALU.mult))
                if e == U_C + 20:
                    z_job(4)
                if e == U_C + 21:
                    conv(0)
                if e == U_C + 22:
                    conv(1)
                if e == U_C + 24:
                    z_job(5)
                if e == U_C + 25:
                    conv(2)
                if e == U_C + 26:
                    conv(3)
                for _ in range(ada_steps(u)):
                    ada_step()
                if u == U_OUT + 2:
                    mod_block(4)
                if u < U_OUT + 3:
                    split_lo(u, slot_in(u)[0])
            dve.wait_ge(mask_in, 32)

            def item(i):
                h, n = divmod(i, NQB)
                s0 = 1024 * (i % 2)
                w = key_window(i)[1]
                new, old = i < 4 * HEADS, i >= 1
                o = slice(i - 1, i)
                if new:
                    dve.wait_ge(s_done, i + 1)
                masked = False
                if new and h >= A_HEADS and n > 0:
                    left = psf[:, s0 + 512 - w:s0 + 512 - w + P]
                    masked = mark(nc.vector.tensor_tensor(left, left, maskl[:], ALU.add))
                summed = False
                if old:
                    dve.wait_ge(p_done, i)
                if old and i - 1 >= NQB * A_HEADS:
                    dve.wait_ge(es_done, i - NQB * A_HEADS)
                    summed = mark(nc.vector.tensor_tensor(rsum[:, o], rsum[:, o], esink[:, o], ALU.add))
                if new and h >= A_HEADS and n < NQB - 1:
                    if masked:
                        dve.wait_ge(dchain, masked)
                    right = psf[:, s0 + 512 - P:s0 + 512]
                    masked = mark(nc.vector.tensor_tensor(right, right, maskr[:], ALU.add))
                if old:
                    if summed:
                        dve.wait_ge(dchain, summed)
                    turned = mark(nc.vector.reciprocal(rinv[:, o], rsum[:, o]))
                if new:
                    if masked:
                        dve.wait_ge(dchain, masked)
                    link(nc.vector.tensor_reduce(mx[:, i:i + 1], psf[:, s0 + 512 - w:s0 + TOK], AX.X, ALU.max))
                    if h < A_HEADS:
                        nc.vector.tensor_scalar(nb[:, i:i + 1], mx[:, i:i + 1], qss[:, 3, i:i + 1], -1.0,
                                                ALU.mult, ALU.mult).then_inc(nb_done, 1)
                    else:
                        link(nc.vector.tensor_scalar(mx[:, i:i + 1], mx[:, i:i + 1], SCALE,
                                                     sinkc[:, h - A_HEADS:h - A_HEADS + 1], ALU.mult, ALU.max))
                        nc.vector.tensor_scalar(nb[:, i:i + 1], mx[:, i:i + 1], -1.0, None, ALU.mult)\
                            .then_inc(nb_done, 1)
                if old:
                    dve.wait_ge(dchain, turned)
                    p = prob[(i - 1) % 3][:, 512 - key_window(i - 1)[1]:TOK]
                    nc.vector.tensor_scalar(p, p, rinv[:, o], None, ALU.mult).then_inc(pn_done, 1)

            def keep_o_lo(h):
                dve.wait_ge(o_hi, 4 + h + 1)
                nc.vector.tensor_tensor(hlo[:, h, :], PS[:, 6 + h % 2, :], hhi[:, h, :].bitcast(F32), ALU.subtract)\
                    .then_inc(o_lo, 1)

            def keep_conv_lo(c):
                dve.wait_ge(o_hi, c + 1)
                dve.wait_ge(conv_y, c + 1)
                nc.vector.tensor_tensor(hlo[:, 12 + c, :], gpre[:, c, :], hhi[:, 12 + c, :].bitcast(F32),
                                        ALU.subtract).then_inc(o_lo, 1)

            for i in range(4 * HEADS + 1):
                item(i)
                if i < 2:
                    q_finish(Q_JOBS - 1, (i,))
                if i == 1:
                    split_lo(U_OUT + 3, slot_in(U_OUT + 3)[0])
                if 2 <= i < 6:
                    keep_conv_lo(i - 2)
                if ADA_ITEM <= i < ADA_ITEM + KC:
                    ada_step()
                if i == ADA_ITEM + KC + 1:
                    dve.wait_ge(ada_kept, 1)
                    mod_block(5, adac[:])
                if i % 4 == 2 and i > 8:
                    keep_o_lo(i // 4 - 2)
            keep_o_lo(HEADS - 2)
            keep_o_lo(HEADS - 1)

            def gate_diag():
                dve.wait_ge(mod_add, 2)
                nc.vector.tensor_tensor(gain[:, 2, :], modc[:, 32:48], g_mix_post, ALU.mult).then_inc(mods, 1)
                dve.wait_ge(mods, 5)
                for k in range(KC):
                    ins = nc.vector.tensor_scalar(diag[:, k, :], ident[:], gain[:, 2, k:k + 1], None, ALU.mult)
                    if k % 4 == 3:
                        ins.then_inc(g_diag, 1)

            def y_job(j):
                dve.wait_ge(unit_used, U_OUT + 4 * j + 4)
                for s in range(2):
                    nc.vector.tensor_copy(ytok[:, 2 * s:2 * s + 2, UCOLS * j:UCOLS * j + UCOLS],
                                          PS[:, 2 * (j % 3) + s, :].rearrange("p (t n) -> p t n", t=2))\
                        .then_inc(bank_dve, 1)

            def y_gate(j):
                dve.wait_ge(y_sq, NQB * j + NQB)
                dve.wait_ge(g_kept, j // 2 + 1)
                y = ytok[:, :, UCOLS * j:UCOLS * j + UCOLS]
                g = grow[:, UCOLS * j:UCOLS * j + UCOLS].unsqueeze(1).broadcast_to([P, NQB, UCOLS])
                nc.vector.tensor_tensor(y, y, g, ALU.mult).then_inc(y_gated, 1)

            gate_diag()
            for u in range(U_OUT + 4, U_FFN + 4):
                e = u - 3
                if (e - U_OUT) % 4 == 0:
                    y_job((e - U_OUT) // 4 - 1)
                if (e - U_OUT) % 4 == 2 and e > U_OUT + 4:
                    y_gate((e - U_OUT) // 4 - 1)
                for _ in range(ada_steps(u)):
                    ada_step()
                if u == U_OUT + 29:
                    mod_block(7)
                split_lo(u, slot_in(u)[0] if u < U_FFN else u - U_FFN)
            dve.wait_ge(mod_add, 8)
            nc.vector.scalar_tensor_tensor(gain[:, 3, :], modc[:, 64:80], 1.0, g_ffn_pre, ALU.add, ALU.mult)\
                .then_inc(mods, 1)
            nc.vector.tensor_tensor(gain[:, 4, :], modc[:, 80:96], g_ffn_post, ALU.mult).then_inc(mods, 1)

            y_gate(OUT_JOBS - 1)
            link(nc.vector.tensor_reduce(tss[:, 0, 0, :], yss[:, :, :], AX.X, ALU.add))
            rsqrt_head(4, tss[:, 0, 1, :], tss[:, 0, 0, :], D)
            rsqrt_tail(4, tss[:, 0, 1, :], tss[:, 0, 2, :], tss[:, 0, 3, :])
            dve.wait_ge(y_gated, OUT_JOBS)
            dve.wait_ge(x2_in, 16 * NQB)
            for t in range(NQB):
                nc.vector.scalar_tensor_tensor(ytok[:, t, :], ytok[:, t, :], tss[:, 0, 2, t:t + 1], xtok2[:, t, :],
                                               ALU.mult, ALU.add).then_inc(x1_done, 1)
            dve.wait_ge(x1_sq, NQB)
            rsqrt_head(5, tss[:, 1, 1, :], tss[:, 1, 0, :], D)
            rsqrt_tail(5, tss[:, 1, 1, :], tss[:, 1, 2, :], tss[:, 1, 3, :])
            for t in range(NQB):
                nc.vector.tensor_scalar(diag[:, t, :], ident[:], tss[:, 1, 2, t:t + 1], None, ALU.mult)\
                    .then_inc(x1_diag, 1)
            for j in range(KC):
                dve.wait_ge(h2_hi, j + 1)
                nc.vector.tensor_tensor(hlo[:, j, :], h2t[:, j % 3, :], hhi[:, j, :].bitcast(F32), ALU.subtract)\
                    .then_inc(h2_lo, 1)
            dve.wait_ge(facc_zero, 1)

            def f_sums(d):
                for s in range(2):
                    n = 2 * d + s
                    dve.wait_ge(f_sq, n + 1)
                    if n == 0:
                        nc.vector.tensor_copy(fsum[:], tsq[:, 0, :]).then_inc(f_sqsum, 1)
                    else:
                        dve.wait_ge(f_sqsum, n)
                        nc.vector.tensor_tensor(fsum[:], fsum[:], tsq[:, s, :], ALU.add)\
                            .then_inc(f_sqsum, 1)

            def keep_f(c):
                dve.wait_ge(f_turned, c + 1)
                for t in (2, 3):
                    nc.vector.tensor_copy(facc_tok[:, c, t, :], PS[:, 4 + t, :]).then_inc(f_kept_dve, 1)

            def ffn(g, last):
                for r in range(GROUP_UNITS):
                    if r in (7, 15):
                        half = r // 8
                        dve.wait_ge(unit_used, U_FFN + 1 + r + GROUP_UNITS * g)
                        for s in range(2):
                            dve.wait_ge(gate_done, 4 * g + 2 * half + s + 1)
                            nc.vector.tensor_tensor(sg[:, s, :], PS[:, 2 + s, :], sg[:, s, :], ALU.mult)\
                                .then_inc(hid_done, 1)
                        for s in range(2):
                            dve.wait_ge(hid_hi, 4 * g + 2 * half + s + 1)
                            nc.vector.tensor_tensor(hidlo[:, 2 * half + s, :], sg[:, s, :],
                                                    hidhi[:, 2 * half + s, :].bitcast(F32), ALU.subtract)\
                                .then_inc(hid_lo, 1)
                    if r >= 16:
                        d = r - 16
                        dve.wait_ge(unit_used, U_FFN + 1 + r + GROUP_UNITS * g)
                        for s in range(2):
                            y = facc[:, 2 * d + s, :]
                            nc.vector.tensor_tensor(y, PS[:, 2 * (d % 2) + s, :], y, ALU.add)\
                                .then_inc(facc_done, 1)
                        if last and d:
                            f_sums(d - 1)
                        if last and d in (2, 4, 6):
                            keep_f(d // 2 - 1)
                    if not (last and r >= GROUP_UNITS - RING):
                        dve.wait_ge(hi_ready, U_FFN + RING + 1 + r + GROUP_UNITS * g)
                        nc.vector.tensor_tensor(wlo[:, r % RING, :], stage[:, r % RING, :],
                                                whi[:, r % RING, :].bitcast(F32), ALU.subtract).then_inc(lo_ready, 1)

            with dve.Fori(0, GROUPS - 1) as g:
                ffn(g, False)
            ffn(GROUPS - 1, True)

            f_sums(7)
            dve.wait_ge(f_stat, 1)
            rsqrt_head(6, tss[:, 2, 1, :], PS[:, 0, 0:NQB], D)
            rsqrt_tail(6, tss[:, 2, 1, :], tss[:, 2, 2, :], tss[:, 2, 3, :])
            dve.wait_ge(f_kept_act, 6)
            dve.wait_ge(f_kept_dve, 6)
            dve.wait_ge(f_turned, 4)
            for t in range(NQB):
                r1 = tss[:, 2, 2, t:t + 1]
                x1 = ytok[:, t, :]
                nc.vector.scalar_tensor_tensor(otok[:, t, 0:1536].rearrange("p (c n) -> p c n", c=3),
                                               facc_tok[:, 0:3, t, :], r1,
                                               x1[:, 0:1536].rearrange("p (c n) -> p c n", c=3),
                                               ALU.mult, ALU.add).then_inc(o_made, 1)
                nc.vector.scalar_tensor_tensor(otok[:, t, 1536:D], PS[:, 4 + t, :], r1, x1[:, 1536:D],
                                               ALU.mult, ALU.add).then_inc(o_made, 1)

        @block.tensor
        def _(pe):
            mm = nc.tensor.matmul

            def three(dst, w, x, start, stop):
                (w_hi, w_lo), (x_hi, x_lo) = w, x
                mm(dst, w_hi, x_hi, start=start, stop=False)
                mm(dst, w_hi, x_lo, start=False, stop=False)
                return mm(dst, w_lo, x_hi, start=False, stop=stop)

            def wt(slot, k, s):
                n = slot * UNIT + k * UCOLS + s * P
                return (whi[:, :, :].rearrange("p r n -> p (r n)")[:, n:n + P],
                        wlo[:, :, :].rearrange("p r n -> p (r n)")[:, n:n + P])

            pe.wait_ge(const_in, 16 * N_CONST)
            nc.tensor.transpose(PS[:, 7, 0:128], rows[:, 0, :], ident[:]).then_inc(rows_turned, 1)
            nc.tensor.transpose(PS[:, 7, 128:208], rows[0:80, 1, :], ident[0:80, 0:80]).then_inc(rows_turned, 1)

            def turn_rows(b):
                pe.wait_ge(row_kept, b + 1)
                for q in range(8):
                    n = 4 * (8 * b + q)
                    last = nc.tensor.transpose(PS[:, 6, n:n + 4], row4[:, P * q:P * q + P], ident[0:4, 0:4])
                last.then_inc(row_turned, 1)

            pe.wait_ge(silp_ready, 2)
            for u in range(ADA0_UNITS):
                b, k = divmod(u, KC)
                if k == 0 and b >= 2:
                    pe.wait_ge(row_kept, b - 1)
                pe.wait_ge(lo_ready, u + 1)
                c4 = silp[:, 4 * k:4 * k + P]
                for s in range(2):
                    mm(PS[:, 2 * (b % 2) + s, :], c4, whi[:, u % RING, 512 * s:512 * s + 512],
                       start=(k == 0), stop=False)
                    last = mm(PS[:, 2 * (b % 2) + s, :], c4, wlo[:, u % RING, 512 * s:512 * s + 512],
                              start=False, stop=(k == KC - 1))
                last.then_inc(unit_used, 1)
                if 24 <= u < 48:
                    g = u - 24
                    t, c = g // 4, g % 4
                    pe.wait_ge(xhat, t + 1)
                    if g >= 2:
                        pe.wait_ge(x_kept, g - 1)
                    for i in range(4):
                        n = P * (4 * c + i)
                        last = nc.tensor.transpose(PS[:, 4 + g % 2, P * i:P * i + P], xtok[:, t, n:n + P], ident[:])
                    last.then_inc(x_turned, 1)
                if u in (21, 37, 53):
                    turn_rows((u - 21) // 16)
            turn_rows(3)

            def ada_reduce(b, bank=6, col=0):
                pe.wait_ge(ada_used, 16 * b + 16)
                pe.wait_ge(mod_add, b)
                for q in range(8):
                    last = mm(PS[:, bank, col + q:col + q + 1], acc[:, P * q:P * q + P], ones[:, 0:1], start=True, stop=True)
                last.then_inc(ada_sum, 1)

            def k_units(b, first):
                for q in range(4):
                    u = U_IN + 8 * b + q
                    pe.wait_ge(lo_ready, u + 1)
                    for i in range(UCH):
                        k = UCH * q + i
                        if first:
                            pe.wait_ge(h_lo, 2 * k + 2)
                        for s in range(2):
                            w = wt(u % RING, i, s)
                            three(PS[:, s, :], w, (hhi[:, k, :], hlo[:, k, :]), k == 0, k == KC - 1)
                            last = three(PS[:, 2, CTX * s:CTX * s + CTX], w, (chi[:, k, :], clo[:, k, :]),
                                         (k, s) == (0, 0), (k, s) == (KC - 1, 1))
                    last.then_inc(unit_used, 1)

            def k_sum(s):
                pe.wait_ge(ksq, s + 1)
                if s:
                    pe.wait_ge(rms, RSQRT_STEPS + 1)
                mm(PS[:, 6, :], ones[:], ktmp[:, 2 + s, 0:SEQ], start=True, stop=True)
                mm(PS[:, 7, 0:CTX], ones[:], ktmp[:, 2 + s, SEQ:TOK], start=True, stop=True).then_inc(kstat, 1)

            def v_units(b):
                for q in range(4):
                    u = U_IN + 8 * b + 4 + q
                    pe.wait_ge(lo_ready, u + 1)
                    for i in range(UCH):
                        k = UCH * q + i
                        w = (whi[:, u % RING, UCOLS * i:UCOLS * i + UCOLS],
                             wlo[:, u % RING, UCOLS * i:UCOLS * i + UCOLS])
                        for t in range(6):
                            if t < 4:
                                x = (hhi[:, k, P * t:P * t + P], hlo[:, k, P * t:P * t + P])
                            else:
                                x = (chi[:, k, P * (t - 4):P * (t - 3)], clo[:, k, P * (t - 4):P * (t - 3)])
                            last = three(PS[:, 3 + t // 2, UCOLS * (t % 2):UCOLS * (t % 2) + UCOLS], x, w,
                                         k == 0 and t % 2 == 0, k == KC - 1 and t % 2 == 1)
                    last.then_inc(unit_used, 1)
                    if b == 0 and q in (1, 2):
                        k_sum(q - 1)
                    if (b, q) == (1, 1):
                        pe.wait_ge(rms, 2 * RSQRT_STEPS + 1)
                        ada_reduce(0)

            def banks_empty(n_act, n_dve):
                pe.wait_ge(bank_act, n_act)
                pe.wait_ge(bank_dve, n_dve)

            k_units(0, True)
            v_units(0)
            banks_empty(2, 1)
            k_units(1, False)
            banks_empty(4, 2)
            v_units(1)
            banks_empty(8, 4)

            def product(banks, slot, q, first, last_, x=(hhi, hlo), chunk_ready=None):
                for i in range(UCH):
                    k = UCH * q + i
                    if chunk_ready:
                        chunk_ready(k)
                    for s in range(2):
                        last = three(PS[:, banks + s, :], wt(slot, i, s), (x[0][:, k, :], x[1][:, k, :]),
                                     first and i == 0, last_ and i == UCH - 1)
                return last

            def q_sum(j):
                pe.wait_ge(qsq_made, 2 * j + 2)
                for s in range(2):
                    for n in range(NQB):
                        c = NQB * (2 * j + s) + n
                        last = mm(PS[:, 7, c:c + 1], qsq[:, s, P * n:P * n + P], ones[:, 0:1], start=True, stop=True)
                last.then_inc(qsum, 1)

            def q_units(i3, sums):
                for r in range(3):
                    pe.wait_ge(bank_act, 4 + 2 * r + 6 * i3)
                    for q in range(4):
                        n = 4 * r + q
                        pe.wait_ge(lo_ready, U_C + 1 + n + 12 * i3)
                        product(2 * r, n % RING, q, q == 0, q == 3).then_inc(unit_used, 1)
                        if n == 9:
                            ada_reduce(1 + i3)
                        if n in sums:
                            q_sum(sums[n])

            with pe.Fori(0, 2) as i3:
                q_units(i3, {})
            q_units(2, {6: 0, 10: 1})
            q_units(3, {2: 2})

            pe.wait_ge(bank_act, 8 + 2 * (CONV_JOBS + Q_JOBS - 1))
            pe.wait_ge(rms, 3 * RSQRT_STEPS + 1)

            def scores(i):
                h, n = divmod(i, NQB)
                kv = h // GROUP
                lo, w = key_window(i)
                if n == 0:
                    pe.wait_ge(qdone, h + 1)
                if i >= 2:
                    pe.wait_ge(p_done, i - 1)
                s0 = 1024 * (i % 2)
                qb = qT[:, h, P * n:P * n + P]
                mm(psf[:, s0 + 512 - w:s0 + 512], qb, kT[:, kv, lo:lo + w], start=True, stop=True)
                mm(psf[:, s0 + 512:s0 + TOK], qb, kT[:, kv, SEQ:TOK], start=True, stop=True).then_inc(s_done, 1)

            def turn(i):
                lo, w = key_window(i)
                pe.wait_ge(pn_done, i + 1)
                if i:
                    pe.wait_ge(pt_kept, i)
                else:
                    pe.wait_ge(bank_act, 8 + 2 * (CONV_JOBS + Q_JOBS))
                if i == ADA_ITEM + KC - LAG:
                    ada_reduce(5, 5, CTX)
                for k in range(w // P):
                    s = 512 - w + P * k
                    nc.tensor.transpose(psf[:, 2048 + lo + P * k:2048 + lo + P * k + P], prob[i % 3][:, s:s + P], ident[:])
                for k in range(2):
                    last = nc.tensor.transpose(PS[:, 5, P * k:P * k + P], prob[i % 3][:, 512 + P * k:640 + P * k], ident[:])
                last.then_inc(pt_turned, 1)

            def values(h, keys):
                kv = h // GROUP
                if 4 in keys:
                    pe.wait_ge(pt_kept, 4 * h + 4)
                    if h == 0:
                        pe.wait_ge(mod_add, 5)
                    if h >= 2:
                        pe.wait_ge(o_lo, 4 + h - 1)
                o = PS[:, 6 + h % 2, :]
                for k in keys:
                    every = h < A_HEADS or k >= 4
                    q0, q1 = (0, SEQ) if every else (P * max(k - 1, 0), P * min(k + 2, NQB))
                    last = mm(o[:, q0:q1], vv[:, k, P * kv:P * kv + P], pt[:, h % 2, k, q0:q1], start=(k == 4),
                              stop=(k == 3))
                if 3 in keys:
                    last.then_inc(o_done, 1)

            def out_unit(banks, q):
                k0 = UCH * OUT_ORDER[q]
                for i in range(UCH):
                    k = k0 + i
                    w = (whi[:, q, UCOLS * i:UCOLS * i + UCOLS], wlo[:, q, UCOLS * i:UCOLS * i + UCOLS])
                    for t in range(NQB):
                        o = (hhi[:, k, P * t:P * t + P], hlo[:, k, P * t:P * t + P])
                        last = three(PS[:, banks + t // 2, UCOLS * (t % 2):UCOLS * (t % 2) + UCOLS], o, w,
                                     (q, i, t % 2) == (0, 0, 0), (q, i, t % 2) == (3, UCH - 1, 1))
                last.then_inc(unit_used, 1)

            def first_out_unit(q, chunks):
                pe.wait_ge(lo_ready, U_OUT + 1 + q)
                pe.wait_ge(o_lo, chunks)
                out_unit(0, q)

            def gate_row(c):
                pe.wait_ge(g_diag, c + 1)
                if c >= 2:
                    pe.wait_ge(g_kept, c - 1)
                for i in range(4):
                    last = mm(PS[:, 6 + c % 2, P * i:P * i + P], ones[:], diag[:, 4 * c + i, :], start=True, stop=True)
                last.then_inc(g_row, 1)

            for i in range(4 * HEADS + LAG):
                if i < 4 * HEADS:
                    scores(i)
                if i >= 6 and i % 4 != 1:
                    h, part = divmod(i - 6, 4)
                    values(h, ((4, 5), (0, 1), (2, 3))[part])
                if i == 4 * HEADS + 1:
                    pe.wait_ge(p_done, 4 * HEADS)
                    first_out_unit(0, 4 + 4)
                if i >= LAG:
                    turn(i - LAG)
            first_out_unit(1, 4 + 4)
            values(HEADS - 1, (4, 5, 0, 1, 2, 3))
            first_out_unit(2, 4 + 8)
            gate_row(0)
            gate_row(1)
            first_out_unit(3, 4 + HEADS)
            gate_row(2)
            gate_row(3)
            pe.wait_ge(g_kept, 4)
            pe.wait_ge(pt_kept, 4 * HEADS)
            with pe.Fori(0, 2) as i3:
                for r in range(3):
                    if r == 2:
                        pe.wait_ge(bank_dve, 4 + 2 + 6 * i3)
                    for q in range(4):
                        pe.wait_ge(lo_ready, U_OUT + 5 + 4 * r + q + 12 * i3)
                        out_unit(2 * ((r + 1) % 3), q)
                    if r == 2:
                        ada_reduce(6 + i3)
            for q in range(4):
                pe.wait_ge(lo_ready, U_FFN - 3 + q)
                out_unit(2, q)

            def turn_x1(j):
                if j >= 2:
                    pe.wait_ge(h2_t, j - 1)
                for t in range(NQB):
                    last = mm(PS[:, 4 + j % 2, P * t:P * t + P], ytok[:, t, P * j:P * j + P], diag[:, t, :],
                              start=True, stop=True)
                last.then_inc(h2_turned, 1)

            def h2_chunk(j):
                if j + 2 < KC:
                    turn_x1(j + 2)
                pe.wait_ge(h2_lo, j + 1)

            pe.wait_ge(x1_diag, NQB)
            turn_x1(0)
            turn_x1(1)

            def turn_f(c):
                pe.wait_ge(f_scaled, 4 * c + 4)
                if c:
                    pe.wait_ge(f_kept_act, 2 * c)
                    pe.wait_ge(f_kept_dve, 2 * c)
                for t in range(NQB):
                    for i in range(4):
                        last = nc.tensor.transpose(PS[:, 4 + t, P * i:P * i + P],
                                                   facc[:, 4 * c + i, P * t:P * t + P], ident[:])
                last.then_inc(f_turned, 1)

            def ffn(g, first=False, last=False):
                r = 0
                for job in range(4):
                    if job < 2:
                        if not first:
                            pe.wait_ge(facc_done, 16 * g - 2 + 2 * job)
                    elif job == 2:
                        pe.wait_ge(gate_done, 2 + 4 * g)
                    else:
                        pe.wait_ge(hid_done, 2 + 4 * g)
                    for q in range(4):
                        pe.wait_ge(lo_ready, U_FFN + 1 + r + GROUP_UNITS * g)
                        product(2 * (job % 2), r % RING, q, q == 0, q == 3, (hhi, hlo),
                                h2_chunk if first and job == 0 else None).then_inc(unit_used, 1)
                        r += 1
                for d in range(8):
                    if d == 0:
                        pe.wait_ge(gate_done, 4 + 4 * g)
                    elif d >= 2:
                        pe.wait_ge(facc_done, 2 * (d - 1) + 16 * g)
                    pe.wait_ge(lo_ready, U_FFN + 1 + r + GROUP_UNITS * g)
                    product(2 * (d % 2), r % RING, 0, True, True, (hidhi, hidlo),
                            (lambda i: pe.wait_ge(hid_lo, 1 + i + 4 * g)) if d == 0 else None).then_inc(unit_used, 1)
                    r += 1
                    if last and d in (2, 4, 6):
                        turn_f(d // 2 - 1)

            pe.wait_ge(bank_dve, 4 + 2 * OUT_JOBS)
            ffn(0, first=True)
            with pe.Fori(1, GROUPS - 1) as g:
                ffn(g)
            ffn(GROUPS - 1, last=True)

            turn_f(3)
            pe.wait_ge(f_sqsum, KC)
            for t in range(NQB):
                last = mm(PS[:, 0, t:t + 1], fsum[:, P * t:P * t + P], ones[:, 0:1], start=True, stop=True)
            last.then_inc(f_stat, 1)


def shape_constants():
    import numpy as np

    grid_w, pairs = 64, P // 4
    inv = np.power(10000.0, -np.arange(pairs) / pairs).astype(np.float32)
    t = np.arange(SEQ)
    place = (t // grid_w, t % grid_w)
    cos, sin = np.zeros((P, SEQ), np.float32), np.zeros((P, SEQ), np.float32)
    for p in range(P):
        axis, half, i = p // 64, (p // 32) % 2, p % 32
        angle = place[axis].astype(np.float32) * inv[i]
        cos[p] = np.cos(angle.astype(np.float64))
        sin[p] = np.sin(angle.astype(np.float64)) * (1 if half else -1)
    q, k = np.arange(P)[:, None], np.arange(P)[None, :]
    return {
        "ident": np.eye(P, dtype=np.float32), "rope_cos": cos, "rope_sin": sin,
        "mask_left": np.where(k >= q, 0, NEG).astype(np.float32),
        "mask_right": np.where(k <= q, 0, NEG).astype(np.float32),
    }


_INS = ["x", "c", "ctx", "c_ctx", "w_ada", "b_ada", "g_mix_pre", "g_mix_post", "g_ffn_pre", "g_ffn_post",
        "w_in", "q_norm", "k_norm", "sink", "conv_w", "w_out", "w_gate", "w_up", "w_down"]


def kernel(**inputs):
    import concourse.bacc as bacc
    import numpy as np
    from concourse.bass_utils import run_bass_kernel_spmd

    nc = bacc.Bacc("TRN2", target_bir_lowering=False, num_devices=1)
    arrays, args = {}, {}
    given = {name: np.ascontiguousarray(inputs[name]) for name in _INS}
    given.update(shape_constants())
    for name, v in given.items():
        arrays[f"in_{name}"] = v
        ap = nc.dram_tensor(f"in_{name}", v.shape, mybir.dt.from_np(v.dtype), kind="ExternalInput").ap()
        if name in _INS and name not in ("c", "c_ctx"):
            ap = ap[0]
        args[name] = ap
    out = nc.dram_tensor("out", (1, SEQ, D), F32, kind="ExternalOutput").ap()
    hybrid_block(nc, args, out[0])
    r = run_bass_kernel_spmd(nc, [arrays], core_ids=[0])
    return r.results[0]["out"]
```

```python
from contextlib import ExitStack

import concourse.bass as bass
from concourse import mybir

ALU = mybir.AluOpType
ACT = mybir.ActivationFunctionType
AX = mybir.AxisListType
F32 = mybir.dt.float32
F32R = mybir.dt.float32r

P = 128
D = 2048
KC = D // P
SEQ = 512
CTX = 256
TOK = SEQ + CTX
NQB = SEQ // P
HEADS = 12
A_HEADS = 6
GROUP = 3
FFN = 5632
EPS = 1e-6
NEG = -1e30
SCALE = float(P) ** -0.5

UCOLS = 256
UCH = 4
UNIT = UCH * UCOLS
RING = 4
ADA0_UNITS = 64
KV_JOBS = 4
CONV_JOBS = 6
Q_JOBS = 6
IN_JOBS = KV_JOBS + CONV_JOBS + Q_JOBS
OUT_JOBS = 8
GROUPS = FFN // (4 * P)
GROUP_UNITS = 24
U_IN = ADA0_UNITS - 2
U_OUT = U_IN + 4 * IN_JOBS
U_FFN = U_OUT + 4 * OUT_JOBS
U_END = U_FFN + GROUPS * GROUP_UNITS
U_C = U_IN + 4 * KV_JOBS
U_Q = U_C + 4 * CONV_JOBS
RSQRT_STEPS = 7

ADA0_BLOCKS = (0, 2, 1, 3)
ADA0_BANK = (0, 2, 0, 4)
FIRST = ADA0_UNITS
FIRST_RING = 8
X_TURN = 20
EARLY_LOAD = 40
EARLY_PIECES = (54, 56, 58, 60, 62)
TURN_F = (2, 5, 6)
ADA_ITEM = 8
LAG = 2
OUT_ORDER = (0, 3, 1, 2)

BASE = 16512
R_H = BASE
R_C = R_H + 65536
R_QKV = R_C + 32768
R_STAGE = R_QKV + 49152
R_WHI = R_STAGE + 16384
R_WLO = R_WHI + 16384
R_ACC = R_WLO + 16384
R_SMALL = R_ACC + 4096


def ring(u):
    return (u - U_IN) % RING


def first_fills(slot):
    return len(range(slot, FIRST, FIRST_RING))


def slot_in(u):
    v = u - FIRST
    return v % 2, first_fills(v % 2) + v // 2 + 1


def ada_steps(u):
    if u < U_C:
        return (1, 1, 2)[(u - U_IN - RING) % 3]
    if u < U_OUT:
        return (2, 1, 1, 1, 2, 1, 1, 1, 2, 1, 1, 2)[(u - U_C) % 12]
    if U_OUT + 5 <= u < U_OUT + 29:
        return (2, 1, 1)[(u - U_OUT - 5) % 3]
    return 0


def ffn_fills(slot):
    return first_fills(slot) + ((U_FFN - FIRST) // 2 if slot < 2 else 0)


def key_window(i):
    h, n = divmod(i, NQB)
    if h < A_HEADS:
        return 0, SEQ
    lo, hi = max(n - 1, 0), min(n + 2, NQB)
    return P * lo, P * (hi - lo)


def hybrid_block(nc, a, out):
    ctx = ExitStack()

    def sb(name, shape, at, dt=F32):
        return nc.alloc_sbuf_tensor_at(name, shape, dt, offset=at)

    def sem(name):
        return ctx.enter_context(nc.semaphore(name))

    with ctx:
        PS = ctx.enter_context(nc.psum_tensor("PS", [P, 8, 512], F32))
        psf = PS[:, :, :].rearrange("p b n -> p (b n)")

        xtok = sb("xtok", [P, 6, D], R_H)
        junk = sb("junk", [P, D], R_H + 49152)
        row4 = sb("row4", [4, 1024], R_H + 57344)
        hhi = sb("hhi", [P, KC, SEQ], R_H, F32R)
        hlo = sb("hlo", [P, KC, SEQ], R_H + 32768, F32R)
        tsq = sb("tsq", [P, 2, SEQ], R_H)
        fsum = sb("fsum", [P, SEQ], R_H + 4096)
        otok = sb("otok", [P, NQB, D], R_H + 32768)

        chi = sb("chi", [P, KC, CTX], R_C, F32R)
        clo = sb("clo", [P, KC, CTX], R_C + 16384, F32R)
        qraw = sb("qraw", [P, 2, SEQ], R_C)
        qsq = sb("qsq", [P, 2, SEQ], R_C + 4096)
        qsw = sb("qsw", [P, 2, SEQ], R_C + 8192)
        gpre = sb("gpre", [P, 4, SEQ], R_C + 12288)
        gpost = sb("gpost", [P, 4, SEQ], R_C)
        zpad = sb("zpad", [P, 4, SEQ + 2], R_C + 20480)
        pt = sb("pt", [P, 2, 6, SEQ], R_C)
        prob = [sb(f"prob{n}", [P, TOK], R_C + 24576 + 3072 * n) for n in range(2)]
        prob.append(sb("prob2", [P, TOK], R_H + 20480))
        qraw_last = sb("qraw_last", [P, 2, SEQ], R_H + 16384)
        qsw_last = sb("qsw_last", [P, 2, SEQ], R_H + 49152)
        ytok = sb("ytok", [P, NQB, D], R_C)

        kstage = sb("kstage", [P, 2, UNIT], R_H + 49152)
        khi = sb("khi", [P, 2, UNIT], R_H + 16384, F32R)
        klo = sb("klo", [P, 2, UNIT], R_H + 24576, F32R)

        xT = sb("xT", [P, KC, TOK], R_QKV)
        qT = sb("qT", [P, HEADS, SEQ], R_QKV)
        kT = sb("kT", [P, 4, TOK], R_QKV + 24576)
        vv = sb("vv", [P, 6, 512], R_QKV + 36864)
        ktmp = sb("ktmp", [P, 8, TOK], R_QKV)
        xtok2 = sb("xtok2", [P, NQB, D], R_QKV)
        grow = sb("grow", [P, D], R_QKV + 32768)
        h2t = sb("h2t", [P, 3, SEQ], R_QKV + 32768)
        diag = sb("diag", [P, KC, P], R_QKV + 40960)
        xh = sb("xh", [P, NQB, D], R_QKV)
        facc = sb("facc", [P, KC, SEQ], R_QKV)
        hidhi = sb("hidhi", [P, 4, SEQ], R_QKV + 32768, F32R)
        hidlo = sb("hidlo", [P, 4, SEQ], R_QKV + 40960, F32R)

        stage = sb("stage", [P, RING, UNIT], R_STAGE)
        early = [sb(f"early{n}", [P, UNIT], R_C + o) for n, o in enumerate((8192, 12288, 24576, 28672))]
        whi = sb("whi", [P, RING, UNIT], R_WHI, F32R)
        wlo = sb("wlo", [P, RING, UNIT], R_WLO, F32R)
        rows = sb("rows", [P, 2, P], R_ACC)
        acc = sb("acc", [P, 1024], R_ACC)
        sg = sb("sg", [P, 2, SEQ], R_ACC)

        at = [R_SMALL]

        def small(name, shape, dt=F32):
            n = 4
            for s in shape[1:]:
                n *= s
            t = sb(name, shape, at[0], dt)
            at[0] += (n + 31) // 32 * 32
            return t

        ident = small("ident", [P, P])
        ones = small("ones", [P, P])
        cosT = small("cosT", [P, SEQ])
        sinT = small("sinT", [P, SEQ])
        maskl = small("maskl", [P, P])
        maskr = small("maskr", [P, P])
        colA = small("colA", [P, 128])
        colB = small("colB", [P, 80])
        sil = small("sil", [P, 32])
        silp = small("silp", [P, 64 + 124], F32R)
        msum = small("msum", [P, 32, 4])
        modc = small("modc", [P, 96])
        adac = small("adac", [P, 8])
        modx = small("modx", [P, 32])
        gain = small("gain", [P, 5, KC])
        xss = small("xss", [P, 4, 6])
        qss = small("qss", [P, 4, 24])
        yss = small("yss", [P, NQB, OUT_JOBS])
        tss = small("tss", [P, 3, 4, NQB])
        ysq = small("ysq", [P, UCOLS])
        sinkc = small("sinkc", [P, A_HEADS])
        sinkn = small("sinkn", [P, A_HEADS])
        mx = small("mx", [P, 48])
        nb = small("nb", [P, 48])
        rsum = small("rsum", [P, 48])
        rinv = small("rinv", [P, 48])
        esink = small("esink", [P, 48])
        assert at[0] <= 229368

        bA = colA[:, 0:96]
        cA = colA[:, 96:128]
        g_mix_pre, g_mix_post = colB[:, 0:16], colB[:, 16:32]
        g_ffn_pre, g_ffn_post = colB[:, 32:48], colB[:, 48:64]

        def tap(t, c):
            return colB[:, 64 + 4 * t + c:65 + 4 * t + c]

        qg, kg, qgs, kgs = (colB[:, n:n + 1] for n in (76, 77, 78, 79))

        v_ada = a["w_ada"].rearrange("(k p) n -> p k n", p=P)
        v_in = a["w_in"].rearrange("(k p) n -> p k n", p=P)
        v_out = a["w_out"].rearrange("(k p) n -> p k n", p=P)
        v_gate = a["w_gate"].rearrange("(k p) n -> p k n", p=P)
        v_up = a["w_up"].rearrange("(k p) n -> p k n", p=P)
        v_down = a["w_down"].rearrange("(k p) n -> p k n", p=P)
        o_tok = out.rearrange("(t p) n -> p t n", p=P)
        facc_tok = facc[:, :, :].rearrange("p (c t) n -> p c t n", c=4)

        first_in = sem("first_in")
        const_in = sem("const_in")
        mask_in = sem("mask_in")
        x_in = [sem(f"x_in{t}") for t in range(6)]
        x2_in = sem("x2_in")
        stage_in = [sem(f"stage_in{s}") for s in range(FIRST_RING)]
        early_in = sem("early_in")
        early_hi = sem("early_hi")
        early_lo = sem("early_lo")
        early_used = sem("early_used")
        ada_in = [sem(f"ada_in{s}") for s in range(2)]
        setup = sem("setup")
        rows_turned = sem("rows_turned")
        cols_ready = sem("cols_ready")
        silu_ready = sem("silu_ready")
        silp_ready = sem("silp_ready")
        hi_ready = sem("hi_ready")
        lo_ready = sem("lo_ready")
        unit_used = sem("unit_used")
        rms = sem("rms")
        xsq = sem("xsq")
        xhat = sem("xhat")
        x_turned = sem("x_turned")
        x_kept = sem("x_kept")
        row_kept = sem("row_kept")
        row_turned = sem("row_turned")
        mods = sem("mods")
        h_t = sem("h_t")
        h_hi = sem("h_hi")
        h_hi_pool = sem("h_hi_pool")
        h_lo_pool = sem("h_lo_pool")
        h_lo = sem("h_lo")
        ada_used = sem("ada_used")
        ada_sum = sem("ada_sum")
        ada_kept = sem("ada_kept")
        mod_add = sem("mod_add")
        bank_act = sem("bank_act")
        bank_dve = sem("bank_dve")
        ksq = sem("ksq")
        kstat = sem("kstat")
        kswap = sem("kswap")
        kdone = sem("kdone")
        qswap = sem("qswap")
        qsq_made = sem("qsq_made")
        qsum = sem("qsum")
        qdone = sem("qdone")
        zdone = sem("zdone")
        conv_y = sem("conv_y")
        dchain = sem("dchain")
        s_done = sem("s_done")
        nb_done = sem("nb_done")
        p_done = sem("p_done")
        es_done = sem("es_done")
        pn_done = sem("pn_done")
        pt_turned = sem("pt_turned")
        pt_kept = sem("pt_kept")
        o_done = sem("o_done")
        o_hi = sem("o_hi")
        o_lo = sem("o_lo")
        g_diag = sem("g_diag")
        g_row = sem("g_row")
        g_kept = sem("g_kept")
        y_sq = sem("y_sq")
        y_gated = sem("y_gated")
        x1_done = sem("x1_done")
        x1_sq = sem("x1_sq")
        xh_act = sem("xh_act")
        xh_dve = sem("xh_dve")
        facc_zero = sem("facc_zero")
        h2_turned = sem("h2_turned")
        h2_t = sem("h2_t")
        h2_hi = sem("h2_hi")
        h2_lo = sem("h2_lo")
        gate_done = sem("gate_done")
        hid_done = sem("hid_done")
        hid_hi = sem("hid_hi")
        hid_lo = sem("hid_lo")
        facc_done = sem("facc_done")
        f_sq = sem("f_sq")
        f_sqsum = sem("f_sqsum")
        f_stat = sem("f_stat")
        f_scaled = sem("f_scaled")
        f_turned = sem("f_turned")
        f_kept_act = sem("f_kept_act")
        f_kept_dve = sem("f_kept_dve")
        o_made = sem("o_made")
        o_scaled = sem("o_scaled")
        o_pool = sem("o_pool")
        table = sem("table")
        stored = sem("stored")

        block = ctx.enter_context(nc.Block())
        N_FIRST = 4
        N_CONST = 4 + 1 + 2 + 4 + 3

        def first_slot(u):
            n = u % FIRST_RING
            return stage[:, n, :] if n < RING else early[n - RING][:, :]

        @block.sync
        def _(sp):
            def w_load(slot, src):
                sp.dma_start(stage[:, slot, :].rearrange("p (k n) -> p k n", k=UCH), src).then_inc(stage_in[slot], 16)

            for u in range(FIRST):
                if u >= FIRST_RING:
                    sp.wait_ge(lo_ready, u - FIRST_RING + 1)
                b, k = divmod(u, KC)
                n = 1024 * ADA0_BLOCKS[b]
                sp.dma_start(first_slot(u), v_ada[:, k, n:n + 1024]).then_inc(stage_in[u % FIRST_RING], 16)
                if u == EARLY_LOAD:
                    sp.wait_ge(xsq, 6)
                    for q in range(2):
                        sp.dma_start(kstage[:, q, :].rearrange("p (k n) -> p k n", k=UCH),
                                     v_in[:, UCH * q:UCH * q + UCH, 0:UCOLS]).then_inc(early_in, 16)
            for q in (2, 3):
                sp.wait_ge(lo_ready, FIRST - FIRST_RING + q - 1)
                w_load(q % 2, v_in[:, 4 * q:4 * q + 4, 0:UCOLS])
            for start, end, job in ((1, KV_JOBS, 1), (KV_JOBS + Q_JOBS, IN_JOBS, KV_JOBS),
                                    (KV_JOBS, KV_JOBS + Q_JOBS, KV_JOBS + CONV_JOBS)):
                with sp.Fori(start, end) as j:
                    for q in range(4):
                        sp.wait_ge(lo_ready, U_IN - 1 + q + 4 * (job - start) + 4 * j)
                        w_load(q % 2, v_in[:, 4 * q:4 * q + 4, bass.ds(j * UCOLS, UCOLS)])
            with sp.Fori(0, OUT_JOBS) as j:
                for q in range(4):
                    k = UCH * OUT_ORDER[q]
                    src = v_out[:, k:k + UCH, bass.ds(j * UCOLS, UCOLS)]
                    sp.wait_ge(lo_ready, U_OUT - 1 + q + 4 * j)
                    w_load(q % 2, src)
            sp.wait_ge(lo_ready, U_FFN)
            sp.wait_ge(ada_used, 128)

            def ffn_loads(g):
                r = 0
                for pair in range(2):
                    for w in (v_gate, v_up):
                        for q in range(4):
                            sp.wait_ge(lo_ready, U_FFN - 3 + r + GROUP_UNITS * g)
                            w_load(r % RING, w[:, 4 * q:4 * q + 4, bass.ds(512 * g + UCOLS * pair, UCOLS)])
                            r += 1
                for d in range(8):
                    sp.wait_ge(lo_ready, U_FFN - 3 + r + GROUP_UNITS * g)
                    w_load(r % RING, v_down[:, bass.ds(4 * g, 4), UCOLS * d:UCOLS * d + UCOLS])
                    r += 1

            with sp.Fori(0, GROUPS) as g:
                ffn_loads(g)
            for t in range(NQB):
                for part, (n, end) in enumerate(((0, 1536), (1536, D))):
                    if t < 3 or part:
                        sp.wait_ge(o_made, 2 * t + part + (t < 3))
                    else:
                        sp.wait_ge(o_pool, 1)
                    sp.dma_start(o_tok[:, t, n:end], otok[:, t, n:end]).then_inc(stored, 16)
            sp.wait_ge(stored, 32 * NQB)

        @block.gpsimd
        def _(pool):
            nc.gpsimd.memset(ones[:], 1.0).then_inc(setup, 1)
            nc.gpsimd.memset(silp[:, :].bitcast(F32), 0.0).then_inc(setup, 1)
            ld = lambda dst, src: pool.dma_start(dst, src).then_inc(const_in, 16)
            for n, name in enumerate(("g_mix_pre", "g_mix_post", "g_ffn_pre", "g_ffn_post")):
                ld(rows[16 * n:16 * n + 16, 1, :], a[name].rearrange("(r n) -> r n", n=P))
            ld(rows[64:76, 1, :], a["conv_w"].rearrange("t (c n) -> (t c) n", n=P))
            ld(rows[76:77, 1, :], a["q_norm"].rearrange("(o n) -> o n", o=1))
            ld(rows[77:78, 1, :], a["k_norm"].rearrange("(o n) -> o n", o=1))
            for r, name in ((78, "q_norm"), (79, "k_norm")):
                w = a[name].rearrange("(o a h i) -> o a h i", o=1, a=2, h=2)
                d = rows[r:r + 1, 1, :].rearrange("p (a h i) -> p a h i", a=2, h=2)
                for h in range(2):
                    ld(d[:, :, h, :], w[:, :, 1 - h, :])
            ld(cosT[:], a["rope_cos"])
            ld(sinT[:], a["rope_sin"])
            ld(sinkc[:], a["sink"].rearrange("(o h) -> o h", o=1).broadcast_to([P, A_HEADS]))
            pool.dma_start(maskl[:], a["mask_left"]).then_inc(mask_in, 16)
            pool.dma_start(maskr[:], a["mask_right"]).then_inc(mask_in, 16)
            pool.wait_ge(x_turned, 24)
            for j in range(8):
                pool.wait_ge(h_t, 2 * j + 2)
                nc.gpsimd.tensor_copy(hhi[:, j, :], xT[:, j, 0:SEQ]).then_inc(h_hi_pool, 1)
                nc.gpsimd.tensor_copy(chi[:, j, :], xT[:, j, SEQ:TOK]).then_inc(h_hi_pool, 1)
                pool.wait_ge(h_hi_pool, 2 * j + 1)
                nc.gpsimd.tensor_tensor(hlo[:, j, :], xT[:, j, 0:SEQ], hhi[:, j, :].bitcast(F32), ALU.subtract)\
                    .then_inc(h_lo_pool, 1)
                pool.wait_ge(h_hi_pool, 2 * j + 2)
                nc.gpsimd.tensor_tensor(clo[:, j, :], xT[:, j, SEQ:TOK], chi[:, j, :].bitcast(F32), ALU.subtract)\
                    .then_inc(h_lo_pool, 1)
            pool.wait_ge(lo_ready, FIRST - 4)
            for k in range(KC):
                if k >= 2:
                    pool.wait_ge(ada_used, k - 1)
                pool.dma_start(stage[:, 2 + k % 2, :], v_ada[:, k, 4096:5120]).then_inc(ada_in[k % 2], 16)
            with pool.Fori(1, 8) as b:
                for k in range(KC):
                    pool.wait_ge(ada_used, k - 1 + 16 * b)
                    pool.dma_start(stage[:, 2 + k % 2, :], v_ada[:, k, bass.ds(4096 + 1024 * b, 1024)])\
                        .then_inc(ada_in[k % 2], 16)
            pool.wait_ge(h2_turned, KC)
            nc.gpsimd.memset(facc[:, :, :].rearrange("p c n -> p (c n)"), 0.0).then_inc(facc_zero, 1)
            pool.wait_ge(o_scaled, 1)
            o3 = otok[:, 3, 0:1536]
            nc.gpsimd.tensor_tensor(o3, o3, ytok[:, 3, 0:1536], ALU.add).then_inc(o_pool, 1)

        @block.scalar
        def _(act):
            def copy_(dst, src):
                return nc.scalar.activation(dst, src, ACT.Copy)

            def split_hi(u, slot, count):
                act.wait_ge(stage_in[slot], 16 * count)
                act.wait_ge(unit_used, u - RING + 1)
                copy_(whi[:, ring(u), :], stage[:, slot, :]).then_inc(hi_ready, 1)

            def sqrt_(use, dst, src):
                act.wait_ge(rms, RSQRT_STEPS * use + 1)
                nc.scalar.activation(dst, src, ACT.Sqrt).then_inc(rms, 1)

            ld = lambda dst, src: act.dma_start(dst, src).then_inc(first_in, 16)
            ld(rows[96:112, 0, :], a["c"].rearrange("o (r n) -> (o r) n", n=P))
            ld(rows[112:128, 0, :], a["c_ctx"].rearrange("(r n) -> r n", n=P))
            ld(rows[0:96, 0, :], a["b_ada"].rearrange("(r n) -> r n", n=P))
            ld(ident[:], a["ident"])
            for t in range(6):
                src = a["x"][P * t:P * t + P, :] if t < 4 else a["ctx"][P * (t - 4):P * (t - 4) + P, :]
                act.dma_start(xtok[:, t, :], src).then_inc(x_in[t], 16)

            act.wait_ge(cols_ready, 1)
            nc.scalar.activation(sil[:], cA, ACT.Silu).then_inc(silu_ready, 1)

            def keep_row(b):
                n = 512 * ADA0_BANK[b]
                act.wait_ge(unit_used, KC * b + KC)
                if b:
                    act.wait_ge(row_turned, b)
                copy_(row4[:, :], psf[0:4, n:n + 1024]).then_inc(row_kept, 1)

            def keep_x(g):
                c, t = divmod(g, 6)
                act.wait_ge(x_turned, g + 1)
                copy_(xT[:, 4 * c:4 * c + 4, P * t:P * t + P],
                      PS[:, 4 + g % 2, :].rearrange("p (c n) -> p c n", c=4)).then_inc(x_kept, 1)

            def h_upper(j):
                act.wait_ge(h_t, 2 * j + 1)
                copy_(hhi[:, j, :], xT[:, j, 0:SEQ]).then_inc(h_hi, 1)
                act.wait_ge(h_t, 2 * j + 2)
                copy_(chi[:, j, :], xT[:, j, SEQ:TOK]).then_inc(h_hi, 1)

            for u in range(FIRST):
                act.wait_ge(stage_in[u % FIRST_RING], 16 * (u // FIRST_RING + 1))
                if u >= RING:
                    act.wait_ge(unit_used, u - RING + 1)
                copy_(whi[:, ring(u), :], first_slot(u)).then_inc(hi_ready, 1)
                if 3 <= u < 15 and u % 2 == 1:
                    t = (u - 3) // 2
                    act.wait_ge(x_in[t], 16)
                    if t:
                        act.wait_ge(xsq, t)
                    nc.scalar.activation(junk[:], xtok[:, t, :], ACT.Square, accum_out=xss[:, 0, t:t + 1])\
                        .then_inc(xsq, 1)
                if u == X_TURN - 4:
                    sqrt_(0, xss[:, 2, :], xss[:, 1, :])
                if X_TURN + 3 <= u < X_TURN + 27:
                    keep_x(u - X_TURN - 3)
                if u in (19, 35, 51):
                    keep_row((u - 19) // 16)
                if u in (50, 52):
                    act.wait_ge(early_in, 32)
                    q = (u - 50) // 2
                    copy_(khi[:, q, :], kstage[:, q, :]).then_inc(early_hi, 1)
            keep_row(3)
            for u in (FIRST, FIRST + 1):
                split_hi(u, *slot_in(u))
            act.wait_ge(early_used, 1)
            for j in range(8, KC):
                h_upper(j)

            def swap(dst, src, done):
                for s in range(4):
                    act.dma_start(dst[32 * (s ^ 1):32 * (s ^ 1) + 32], src[32 * s:32 * s + 32]).then_inc(done, 16)

            def k_job(b):
                act.wait_ge(unit_used, U_IN + 8 * b + 4)
                if b:
                    act.wait_ge(kdone, 2)
                else:
                    act.wait_ge(h_lo, 16)
                copy_(ktmp[:, 0, 0:SEQ], PS[:, 0, :]).then_inc(bank_act, 1)
                copy_(ktmp[:, 0:2, SEQ:TOK], PS[:, 2, :].rearrange("p (s n) -> p s n", s=2)).then_inc(bank_act, 1)
                act.wait_ge(bank_act, 4 * b + 2)
                swap(ktmp[:, 7, 0:SEQ], ktmp[:, 0, 0:SEQ], kswap)
                if b == 0:
                    nc.scalar.activation(ktmp[:, 2, :], ktmp[:, 0, :], ACT.Square).then_inc(ksq, 1)
                    act.wait_ge(bank_dve, 1)
                    nc.scalar.activation(ktmp[:, 3, :], ktmp[:, 1, :], ACT.Square).then_inc(ksq, 1)

            def k_swap_second(b):
                act.wait_ge(bank_dve, 2 * b + 1)
                act.wait_ge(kdone, 2 * b + 1)
                swap(ktmp[:, 7, 0:SEQ], ktmp[:, 1, 0:SEQ], kswap)

            def v_job(b):
                act.wait_ge(unit_used, U_IN + 8 * b + 8)
                for t in (0, 4):
                    copy_(vv[:, t:t + 2, UCOLS * b:UCOLS * b + UCOLS],
                          PS[:, 3 + t // 2, :].rearrange("p (t n) -> p t n", t=2)).then_inc(bank_act, 1)

            def conv_job(j):
                act.wait_ge(unit_used, U_C + 4 * j + 4)
                if j == 4:
                    act.wait_ge(zdone, 2)
                for s in range(2):
                    c = 2 * (j % 2) + s
                    dst = (gpre[:, c, :], gpost[:, c, :], zpad[:, c, 1:SEQ + 1])[j // 2]
                    copy_(dst, PS[:, 2 * (j % 3) + s, :]).then_inc(bank_act, 1)

            def q_job(j):
                act.wait_ge(unit_used, U_Q + 4 * j + 4)
                if j == 0:
                    act.wait_ge(kdone, 4)
                    act.wait_ge(conv_y, 4)
                else:
                    act.wait_ge(qdone, 2 * j)
                raw, part = (qraw, qsw) if j < Q_JOBS - 1 else (qraw_last, qsw_last)
                for s in range(2):
                    copy_(raw[:, s, :], PS[:, 2 * (j % 3) + s, :]).then_inc(bank_act, 1)
                act.wait_ge(bank_act, 20 + 2 * j + 2)
                swap(part[:, :, :], raw[:, :, :], qswap)
                if j < 3:
                    if j:
                        act.wait_ge(qsum, j)
                    for s in range(2):
                        nc.scalar.activation(qsq[:, s, :], qraw[:, s, :], ACT.Square).then_inc(qsq_made, 1)

            def exp_item(i):
                h = i // NQB
                s0 = 1024 * (i % 2)
                lo, w = key_window(i)
                act.wait_ge(nb_done, i + 1)
                if i == 2:
                    act.wait_ge(unit_used, U_OUT - 1)
                if i >= 3:
                    act.wait_ge(pt_turned, i - 2)
                sc = qss[:, 3, i:i + 1] if h < A_HEADS else SCALE
                nc.scalar.activation(prob[i % 3][:, 512 - w:TOK], psf[:, s0 + 512 - w:s0 + TOK], ACT.Exp,
                                     bias=nb[:, i:i + 1], scale=sc, accum_out=rsum[:, i:i + 1]).then_inc(p_done, 1)
                if h >= A_HEADS:
                    nc.scalar.activation(esink[:, i:i + 1], sinkc[:, h - A_HEADS:h - A_HEADS + 1], ACT.Exp,
                                         bias=nb[:, i:i + 1]).then_inc(es_done, 1)

            for u in range(U_IN + 4, U_OUT + 4):
                e = u - 3
                if e == U_IN + 4:
                    k_job(0)
                if e == U_IN + 6:
                    sqrt_(1, ktmp[:, 5, :], ktmp[:, 4, :])
                if e == U_IN + 7:
                    k_swap_second(0)
                if e == U_IN + 8:
                    v_job(0)
                    sqrt_(2, ktmp[:, 5, :], ktmp[:, 4, :])
                if e == U_IN + 12:
                    k_job(1)
                if e == U_IN + 14:
                    k_swap_second(1)
                if e == U_IN + 16:
                    v_job(1)
                if e > U_C and (e - U_C) % 4 == 0:
                    j = (e - U_C) // 4 - 1
                    if e == U_OUT:
                        nc.scalar.activation(esink[:, 0:1], ones[:, 0:1], ACT.Exp).then_inc(table, 1)
                        exp_item(0)
                        exp_item(1)
                    if j < CONV_JOBS:
                        conv_job(j)
                    else:
                        q_job(j - CONV_JOBS)
                if e == U_Q + 16:
                    sqrt_(3, qss[:, 1, :], qss[:, 0, :])
                if u < U_OUT + 3:
                    split_hi(u, *slot_in(u))

            def keep_pt(i):
                h, n = divmod(i, NQB)
                lo, w = key_window(i)
                act.wait_ge(pt_turned, i + 1)
                if i == 0:
                    act.wait_ge(qdone, HEADS - 2)
                if i == NQB:
                    act.wait_ge(o_lo, 4)
                if h >= 2:
                    act.wait_ge(o_done, h - 1)
                if i == ADA_ITEM + KC - LAG:
                    copy_(adac[:], PS[:, 5, CTX:CTX + 8]).then_inc(ada_kept, 1)
                kept = pt[:, h % 2, :, P * n:P * n + P]
                turned = psf[:, 2048:2048 + TOK].rearrange("p (k n) -> p k n", n=P)
                if w == SEQ:
                    copy_(kept, turned).then_inc(pt_kept, 1)
                else:
                    copy_(kept[:, lo // P:(lo + w) // P], turned[:, lo // P:(lo + w) // P])
                    copy_(kept[:, 4:6], turned[:, 4:6]).then_inc(pt_kept, 1)

            def keep_conv_hi(c):
                act.wait_ge(conv_y, c + 1)
                copy_(hhi[:, 12 + c, :], gpre[:, c, :]).then_inc(o_hi, 1)

            def keep_o_hi(h):
                act.wait_ge(o_done, h + 1)
                copy_(hhi[:, h, :], PS[:, 6 + h % 2, :]).then_inc(o_hi, 1)

            for i in range(4 * HEADS + LAG):
                if 2 <= i < 4 * HEADS:
                    exp_item(i)
                if i >= LAG:
                    keep_pt(i - LAG)
                if 2 <= i < 6:
                    keep_conv_hi(i - 2)
                if i == 6:
                    split_hi(U_OUT + 3, *slot_in(U_OUT + 3))
                if i % 4 == 2 and i > 9:
                    keep_o_hi(i // 4 - 2)
            act.wait_ge(pt_turned, 4 * HEADS)
            keep_o_hi(HEADS - 2)
            keep_o_hi(HEADS - 1)

            def y_squares(j):
                for t in range(NQB):
                    act.wait_ge(bank_dve, 4 + 2 * j + t // 2 + 1)
                    if j or t:
                        act.wait_ge(y_sq, NQB * j + t)
                    nc.scalar.activation(ysq[:], ytok[:, t, UCOLS * j:UCOLS * j + UCOLS], ACT.Square,
                                         accum_out=yss[:, t, j:j + 1]).then_inc(y_sq, 1)

            def keep_gate_row(c):
                act.wait_ge(g_row, c + 1)
                copy_(grow[:, 512 * c:512 * c + 512], PS[:, 6 + c % 2, :]).then_inc(g_kept, 1)

            def split_ffn_hi(u):
                slot = u - U_FFN
                act.wait_ge(stage_in[slot], 16 * (ffn_fills(slot) + 1))
                act.wait_ge(unit_used, u - RING + 1)
                copy_(whi[:, ring(u), :], stage[:, slot, :]).then_inc(hi_ready, 1)

            for u in range(U_OUT + 4, U_FFN + 3):
                e = u - 3
                if e == U_OUT + 4:
                    for c in range(4):
                        keep_gate_row(c)
                if e in (U_OUT + 6, U_OUT + 10, U_OUT + 14, U_OUT + 18):
                    t = (e - U_OUT - 6) // 4
                    act.dma_start(xtok2[:, t, :], a["x"][P * t:P * t + P, :]).then_inc(x2_in, 16)
                if u < U_FFN:
                    split_hi(u, *slot_in(u))
                else:
                    split_ffn_hi(u)
                if (e - U_OUT) % 4 == 0:
                    y_squares((e - U_OUT) // 4 - 1)
            nc.scalar.activation(esink[:, 0:1], ones[:, 0:1], ACT.Sqrt).then_inc(table, 1)
            y_squares(OUT_JOBS - 1)

            sqrt_(4, tss[:, 0, 2, :], tss[:, 0, 1, :])
            split_ffn_hi(U_FFN + 3)
            for t in range(NQB):
                act.wait_ge(x1_done, t + 1)
                if t:
                    act.wait_ge(x1_sq, t)
                nc.scalar.activation(junk[:], ytok[:, t, :], ACT.Square, accum_out=tss[:, 1, 0, t:t + 1])\
                    .then_inc(x1_sq, 1)
            sqrt_(5, tss[:, 1, 2, :], tss[:, 1, 1, :])
            act.wait_ge(rms, RSQRT_STEPS * 6)
            for f in (slice(0, D // 2), slice(D // 2, D)):
                nc.scalar.activation(xh[:, 3, f], ytok[:, 3, f], ACT.Copy, scale=tss[:, 1, 2, 3:4]).then_inc(xh_act, 1)
            for j in range(KC):
                act.wait_ge(h2_turned, j + 1)
                if j >= 3:
                    act.wait_ge(h2_lo, j - 2)
                nc.scalar.activation(h2t[:, j % 3, :], PS[:, 4 + j % 2, :], ACT.Identity, bias=modc[:, 48 + j:49 + j],
                                     scale=gain[:, 3, j:j + 1]).then_inc(h2_t, 1)
                act.wait_ge(h2_t, j + 1)
                copy_(hhi[:, j, :], h2t[:, j % 3, :]).then_inc(h2_hi, 1)

            def squares(d):
                act.wait_ge(unit_used, U_END - 8)
                for j in (2 * d, 2 * d + 1):
                    act.wait_ge(facc_done, 16 * (GROUPS - 1) + j + 1)
                    if j >= 2:
                        act.wait_ge(f_sqsum, j - 1)
                    nc.scalar.activation(tsq[:, j % 2, :], facc[:, j, :], ACT.Square).then_inc(f_sq, 1)
                    act.wait_ge(f_sq, j + 1)
                    nc.scalar.activation(facc[:, j, :], facc[:, j, :], ACT.Copy, scale=gain[:, 4, j:j + 1])\
                        .then_inc(f_scaled, 1)

            def keep_f(c):
                act.wait_ge(f_turned, c + 1)
                for t in range(2):
                    copy_(facc_tok[:, c, t, :], PS[:, 4 + t, :]).then_inc(f_kept_act, 1)

            def ffn(g, last):
                for r in range(GROUP_UNITS):
                    def silu(half):
                        act.wait_ge(unit_used, U_FFN + 1 + r + GROUP_UNITS * g)
                        act.wait_ge(hid_lo, 4 * g + 2 * half)
                        for s in range(2):
                            nc.scalar.activation(sg[:, s, :], PS[:, s, :], ACT.Silu).then_inc(gate_done, 1)

                    def upper(half):
                        for s in range(2):
                            act.wait_ge(hid_done, 4 * g + 2 * half + s + 1)
                            copy_(hidhi[:, 2 * half + s, :], sg[:, s, :]).then_inc(hid_hi, 1)

                    if r in (3, 11):
                        silu(r // 8)
                    if r in (7, 15):
                        upper(r // 8)
                    if last and r >= 16:
                        squares(r - 16)
                        if r - 16 in TURN_F:
                            keep_f(TURN_F.index(r - 16))
                    if not (last and r >= GROUP_UNITS - RING):
                        act.wait_ge(stage_in[r % RING], 16 * (ffn_fills(r % RING) + r // RING + 2) + 96 * g)
                        act.wait_ge(unit_used, U_FFN + 1 + r + GROUP_UNITS * g)
                        copy_(whi[:, r % RING, :], stage[:, r % RING, :]).then_inc(hi_ready, 1)

            with act.Fori(0, GROUPS - 1) as g:
                ffn(g, False)
            ffn(GROUPS - 1, True)

            sqrt_(6, tss[:, 2, 2, :], tss[:, 2, 1, :])
            act.wait_ge(f_kept_act, 6)
            act.wait_ge(f_kept_dve, 6)
            act.wait_ge(rms, RSQRT_STEPS * 7)
            nc.scalar.activation(otok[:, 3, 0:1536].rearrange("p (c n) -> p c n", c=3), facc_tok[:, 0:3, 3, :],
                                 ACT.Copy, scale=tss[:, 2, 2, 3:4]).then_inc(o_scaled, 1)

        @block.vector
        def _(dve):
            own = [0]

            def mark(ins):
                own[0] += 1
                ins.then_inc(dchain, 1)
                return own[0]

            def link(ins):
                dve.wait_ge(dchain, mark(ins))

            def split_lo(u, slot):
                dve.wait_ge(hi_ready, u + 1)
                nc.vector.tensor_tensor(wlo[:, ring(u), :], stage[:, slot, :], whi[:, ring(u), :].bitcast(F32),
                                        ALU.subtract).then_inc(lo_ready, 1)

            def rsqrt_head(use, dst, sums, n):
                nc.vector.tensor_scalar(dst, sums, 1.0 / n, EPS, ALU.mult, ALU.add).then_inc(rms, 1)

            def rsqrt_tail(use, mean, root, tmp):
                n = RSQRT_STEPS * use + 2
                steps = (
                    lambda: nc.vector.reciprocal(root, root),
                    lambda: nc.vector.tensor_tensor(tmp, root, root, ALU.mult),
                    lambda: nc.vector.tensor_tensor(tmp, tmp, mean, ALU.mult),
                    lambda: nc.vector.tensor_scalar(tmp, tmp, -0.5, 1.5, ALU.mult, ALU.add),
                    lambda: nc.vector.tensor_tensor(root, root, tmp, ALU.mult),
                )
                for step in steps:
                    dve.wait_ge(rms, n)
                    step().then_inc(rms, 1)
                    n += 1
                dve.wait_ge(rms, n)

            dve.wait_ge(rows_turned, 1)
            nc.vector.tensor_copy(colA[:], PS[:, 7, 0:128]).then_inc(cols_ready, 1)
            dve.wait_ge(silu_ready, 1)
            dve.wait_ge(setup, 2)
            silv = sil[:, :].rearrange("p (v k) -> p k v", v=2)
            parts = silp[:, 0:64].rearrange("p (k v) -> p k v", v=4)
            nc.vector.tensor_copy(parts[:, :, 0:2], silv).then_inc(silp_ready, 1)
            dve.wait_ge(silp_ready, 1)
            nc.vector.tensor_tensor(parts[:, :, 2:4], silv, parts[:, :, 0:2].bitcast(F32), ALU.subtract)\
                .then_inc(silp_ready, 1)

            def split_first(u):
                dve.wait_ge(hi_ready, u + 1)
                nc.vector.tensor_tensor(wlo[:, ring(u), :], first_slot(u), whi[:, ring(u), :].bitcast(F32),
                                        ALU.subtract).then_inc(lo_ready, 1)

            def first_mods(f):
                sums = PS[:, 6, 0:128].rearrange("p (k f c v) -> p k f c v", k=2, f=2, v=4)[:, :, f]
                m = msum[:, :, :].rearrange("p (k f c) v -> p k f c v", k=2, f=2)[:, :, f]
                part = lambda t: t.rearrange("p (k f c) -> p k f c", k=2, f=2)[:, :, f]
                dve.wait_ge(row_turned, 2 * f + 2)
                link(nc.vector.tensor_copy(m, sums))
                link(nc.vector.tensor_tensor(m[:, :, :, 0:2], m[:, :, :, 0:2], m[:, :, :, 2:4], ALU.add))
                nc.vector.tensor_tensor(part(modc[:, 0:32]), m[:, :, :, 0], part(bA[:, 0:32]), ALU.add)\
                    .then_inc(mods, 1)
                nc.vector.tensor_tensor(part(modx[:, :]), m[:, :, :, 1], part(bA[:, 0:32]), ALU.add).then_inc(mods, 1)
                dve.wait_ge(mods, 4 * f + 2)
                c = slice(8 * f, 8 * f + 8)
                for n, m in enumerate((modc, modx)):
                    nc.vector.scalar_tensor_tensor(gain[:, n, c], m[:, 16 + 8 * f:24 + 8 * f], 1.0, g_mix_pre[:, c],
                                                   ALU.add, ALU.mult).then_inc(mods, 1)

            def h_full(j):
                dve.wait_ge(x_kept, 6 * (j // 4) + 6)
                dve.wait_ge(mods, 4 * (j // 8) + 4)
                nc.vector.tensor_scalar(xT[:, j, 0:SEQ], xT[:, j, 0:SEQ], gain[:, 0, j:j + 1], modc[:, j:j + 1],
                                        ALU.mult, ALU.add).then_inc(h_t, 1)
                nc.vector.tensor_scalar(xT[:, j, SEQ:TOK], xT[:, j, SEQ:TOK], gain[:, 1, j:j + 1],
                                        modx[:, j:j + 1], ALU.mult, ALU.add).then_inc(h_t, 1)

            def h_lower(j):
                dve.wait_ge(h_hi, 2 * (j - 8) + 1)
                nc.vector.tensor_tensor(hlo[:, j, :], xT[:, j, 0:SEQ], hhi[:, j, :].bitcast(F32), ALU.subtract)\
                    .then_inc(h_lo, 1)
                dve.wait_ge(h_hi, 2 * (j - 8) + 2)
                nc.vector.tensor_tensor(clo[:, j, :], xT[:, j, SEQ:TOK], chi[:, j, :].bitcast(F32), ALU.subtract)\
                    .then_inc(h_lo, 1)

            for u in range(FIRST):
                split_first(u)
                if u == X_TURN:
                    dve.wait_ge(rows_turned, 2)
                    nc.vector.tensor_copy(colB[:], PS[:, 7, 128:208]).then_inc(cols_ready, 1)
                    dve.wait_ge(cols_ready, 2)
                if u == X_TURN - 5:
                    dve.wait_ge(xsq, 6)
                    rsqrt_head(0, xss[:, 1, :], xss[:, 0, :], D)
                if u == X_TURN - 3:
                    rsqrt_tail(0, xss[:, 1, :], xss[:, 2, :], xss[:, 3, :])
                if X_TURN - 3 <= u < X_TURN + 3:
                    t = u - X_TURN + 3
                    nc.vector.tensor_scalar(xtok[:, t, :], xtok[:, t, :], xss[:, 2, t:t + 1], None, ALU.mult)\
                        .then_inc(xhat, 1)
                if u == 39:
                    first_mods(0)
                if 40 <= u < 48:
                    h_full(u - 40)
                if u in (50, 52):
                    q = (u - 50) // 2
                    dve.wait_ge(early_hi, q + 1)
                    nc.vector.tensor_tensor(klo[:, q, :], kstage[:, q, :], khi[:, q, :].bitcast(F32), ALU.subtract)\
                        .then_inc(early_lo, 1)
            first_mods(1)
            h_full(8)
            h_full(9)
            split_lo(FIRST, 0)
            split_lo(FIRST + 1, 1)
            for j in range(8, KC):
                if j + 2 < KC:
                    h_full(j + 2)
                h_lower(j)

            seen = [0]

            def ada_step():
                n = seen[0]
                b, k = divmod(n, KC)
                seen[0] += 1
                w = stage[:, 2 + n % 2, :]
                if k == 0 and b not in (0, 5, 6):
                    mod_block(b - 1)
                dve.wait_ge(ada_in[n % 2], 16 * (n // 2 + 1))
                if n:
                    dve.wait_ge(ada_used, n)
                if k == 0:
                    nc.vector.tensor_scalar(acc[:], w, sil[:, k:k + 1], None, ALU.mult).then_inc(ada_used, 1)
                else:
                    nc.vector.scalar_tensor_tensor(acc[:], w, sil[:, k:k + 1], acc[:], ALU.mult, ALU.add)\
                        .then_inc(ada_used, 1)

            def mod_block(b, sums=PS[:, 6, 0:8]):
                dve.wait_ge(ada_sum, b + 1)
                nc.vector.tensor_tensor(modc[:, 32 + 8 * b:40 + 8 * b], sums,
                                        bA[:, 32 + 8 * b:40 + 8 * b], ALU.add).then_inc(mod_add, 1)

            def k_job(b):
                dve.wait_ge(unit_used, U_IN + 8 * b + 4)
                nc.vector.tensor_copy(ktmp[:, 1, 0:SEQ], PS[:, 1, :]).then_inc(bank_dve, 1)

            def k_mean(s):
                dve.wait_ge(kstat, s + 1)
                rsqrt_head(1 + s, ktmp[:, 4, :], psf[:, 3072:3072 + TOK], P)

            def k_finish(b, s):
                raw, part, res = ktmp[:, s, :], ktmp[:, 7, 0:SEQ], kT[:, 2 * b + s, :]
                dve.wait_ge(bank_dve, 2 * b + 1)
                dve.wait_ge(bank_act, 4 * b + 2)
                if b == 0:
                    rsqrt_tail(1 + s, ktmp[:, 4, :], ktmp[:, 5, :], ktmp[:, 6, :])
                    t = ktmp[:, 2 + s, :]
                    dve.wait_ge(kswap, 64 * (s + 1))
                    link(nc.vector.scalar_tensor_tensor(part, part, kgs, sinT[:], ALU.mult, ALU.mult))
                    link(nc.vector.scalar_tensor_tensor(t[:, 0:SEQ], raw[:, 0:SEQ], kg, cosT[:], ALU.mult, ALU.mult))
                    link(nc.vector.tensor_scalar(t[:, SEQ:TOK], raw[:, SEQ:TOK], kg, None, ALU.mult))
                    link(nc.vector.tensor_tensor(t[:, 0:SEQ], t[:, 0:SEQ], part, ALU.add))
                    nc.vector.tensor_tensor(res, t, ktmp[:, 5, :], ALU.mult).then_inc(kdone, 1)
                else:
                    dve.wait_ge(kswap, 64 * (s + 3))
                    link(nc.vector.tensor_tensor(part, part, sinT[:], ALU.mult))
                    link(nc.vector.tensor_tensor(res[:, 0:SEQ], raw[:, 0:SEQ], cosT[:], ALU.mult))
                    link(nc.vector.tensor_copy(res[:, SEQ:TOK], raw[:, SEQ:TOK]))
                    nc.vector.tensor_tensor(res[:, 0:SEQ], res[:, 0:SEQ], part, ALU.add).then_inc(kdone, 1)

            def v_job(b):
                dve.wait_ge(unit_used, U_IN + 8 * b + 8)
                nc.vector.tensor_copy(vv[:, 2:4, UCOLS * b:UCOLS * b + UCOLS],
                                      PS[:, 4, :].rearrange("p (t n) -> p t n", t=2)).then_inc(bank_dve, 1)

            def q_finish(j, heads=(0, 1)):
                for s in heads:
                    h = 2 * j + s
                    dve.wait_ge(bank_act, 20 + 2 * j + 2)
                    dve.wait_ge(qswap, 64 * j + 64)
                    if j < Q_JOBS - 1:
                        part, res, raw = qsw[:, s, :], qT[:, h, :], qraw[:, s, :]
                    else:
                        part, res, raw = qsw_last[:, s, :], qT[:, h, :], qraw_last[:, s, :]
                    if h < A_HEADS:
                        link(nc.vector.scalar_tensor_tensor(part, part, qgs, sinT[:], ALU.mult, ALU.mult))
                        link(nc.vector.scalar_tensor_tensor(res, raw, qg, cosT[:], ALU.mult, ALU.mult))
                    else:
                        link(nc.vector.tensor_tensor(part, part, sinT[:], ALU.mult))
                        link(nc.vector.tensor_tensor(res, raw, cosT[:], ALU.mult))
                    nc.vector.tensor_tensor(res, res, part, ALU.add).then_inc(qdone, 1)

            def z_job(j):
                for s in range(2):
                    c = 2 * (j - 4) + s
                    dve.wait_ge(bank_act, 8 + 2 * j + s + 1)
                    z = zpad[:, c, 1:SEQ + 1]
                    nc.vector.tensor_tensor(z, z, gpre[:, c, :], ALU.mult).then_inc(zdone, 1)

            def conv(c):
                dve.wait_ge(zdone, 3 + c)
                y = gpre[:, c, :]
                link(nc.vector.tensor_scalar(y, zpad[:, c, 0:SEQ], tap(0, c), None, ALU.mult))
                link(nc.vector.scalar_tensor_tensor(y, zpad[:, c, 1:SEQ + 1], tap(1, c), y, ALU.mult, ALU.add))
                link(nc.vector.scalar_tensor_tensor(y, zpad[:, c, 2:SEQ + 2], tap(2, c), y, ALU.mult, ALU.add))
                nc.vector.tensor_tensor(y, y, gpost[:, c, :], ALU.mult).then_inc(conv_y, 1)

            for u in range(U_IN + 4, U_OUT + 4):
                e = u - 3
                if e == U_IN + 4:
                    k_job(0)
                if e == U_IN + 6:
                    k_mean(0)
                if e == U_IN + 7:
                    k_finish(0, 0)
                    k_mean(1)
                if e == U_IN + 8:
                    v_job(0)
                if e == U_IN + 9:
                    k_finish(0, 1)
                if e == U_IN + 12:
                    k_job(1)
                if e == U_IN + 14:
                    k_finish(1, 0)
                if e == U_IN + 15:
                    k_finish(1, 1)
                if e == U_IN + 16:
                    v_job(1)
                if e == U_C:
                    dve.wait_ge(unit_used, U_C)
                    for s in (0, SEQ + 1):
                        nc.vector.memset(zpad[:, :, s:s + 1], 0.0).then_inc(zdone, 1)
                if e > U_Q + 1 and (e - U_Q) % 4 == 1:
                    q_finish((e - U_Q) // 4 - 1)
                if e == U_Q + 15:
                    dve.wait_ge(qsum, 3)
                    rsqrt_head(3, qss[:, 0, :], PS[:, 7, 0:24], P)
                if e == U_Q + 18:
                    rsqrt_tail(3, qss[:, 0, :], qss[:, 1, :], qss[:, 2, :])
                    link(nc.vector.tensor_scalar(qss[:, 3, :], qss[:, 1, :], SCALE, None, ALU.mult))
                if e == U_C + 20:
                    z_job(4)
                if e == U_C + 21:
                    conv(0)
                if e == U_C + 22:
                    conv(1)
                if e == U_C + 24:
                    z_job(5)
                if e == U_C + 25:
                    conv(2)
                if e == U_C + 26:
                    conv(3)
                for _ in range(ada_steps(u)):
                    ada_step()
                if u == U_OUT + 2:
                    mod_block(4)
                if u < U_OUT + 3:
                    split_lo(u, slot_in(u)[0])
            dve.wait_ge(mask_in, 32)

            def item(i, new=True, old=True):
                h, n = divmod(i, NQB)
                s0 = 1024 * (i % 2)
                w = key_window(i)[1]
                o = slice(i - 1, i)
                if new:
                    dve.wait_ge(s_done, i + 1)
                masked = False
                if new and h >= A_HEADS and n > 0:
                    left = psf[:, s0 + 512 - w:s0 + 512 - w + P]
                    masked = mark(nc.vector.tensor_tensor(left, left, maskl[:], ALU.add))
                summed = False
                if old:
                    dve.wait_ge(p_done, i)
                if old and i - 1 >= NQB * A_HEADS:
                    dve.wait_ge(es_done, i - NQB * A_HEADS)
                    summed = mark(nc.vector.tensor_tensor(rsum[:, o], rsum[:, o], esink[:, o], ALU.add))
                if new and h >= A_HEADS and n < NQB - 1:
                    if masked:
                        dve.wait_ge(dchain, masked)
                    right = psf[:, s0 + 512 - P:s0 + 512]
                    masked = mark(nc.vector.tensor_tensor(right, right, maskr[:], ALU.add))
                if old:
                    if summed:
                        dve.wait_ge(dchain, summed)
                    turned = mark(nc.vector.reciprocal(rinv[:, o], rsum[:, o]))
                if new:
                    if masked:
                        dve.wait_ge(dchain, masked)
                    link(nc.vector.tensor_reduce(mx[:, i:i + 1], psf[:, s0 + 512 - w:s0 + TOK], AX.X, ALU.max))
                    if h < A_HEADS:
                        nc.vector.tensor_scalar(nb[:, i:i + 1], mx[:, i:i + 1], qss[:, 3, i:i + 1], -1.0,
                                                ALU.mult, ALU.mult).then_inc(nb_done, 1)
                    else:
                        nc.vector.tensor_scalar(nb[:, i:i + 1], mx[:, i:i + 1], -SCALE,
                                                sinkn[:, h - A_HEADS:h - A_HEADS + 1], ALU.mult, ALU.min)\
                            .then_inc(nb_done, 1)
                if old:
                    dve.wait_ge(dchain, turned)
                    p = prob[(i - 1) % 3][:, 512 - key_window(i - 1)[1]:TOK]
                    nc.vector.tensor_scalar(p, p, rinv[:, o], None, ALU.mult).then_inc(pn_done, 1)

            def keep_o_lo(h):
                dve.wait_ge(o_hi, 4 + h + 1)
                nc.vector.tensor_tensor(hlo[:, h, :], PS[:, 6 + h % 2, :], hhi[:, h, :].bitcast(F32), ALU.subtract)\
                    .then_inc(o_lo, 1)

            def keep_conv_lo(c):
                dve.wait_ge(o_hi, c + 1)
                dve.wait_ge(conv_y, c + 1)
                nc.vector.tensor_tensor(hlo[:, 12 + c, :], gpre[:, c, :], hhi[:, 12 + c, :].bitcast(F32),
                                        ALU.subtract).then_inc(o_lo, 1)

            link(nc.vector.tensor_scalar(sinkn[:], sinkc[:], -1.0, None, ALU.mult))
            item(0, old=False)
            item(1)
            item(2, new=False)
            for i in range(2, 4 * HEADS + 1):
                item(i, i < 4 * HEADS, i > 2)
                if 3 <= i < 7:
                    keep_conv_lo(i - 3)
                if i in (7, 8):
                    q_finish(Q_JOBS - 1, (i - 7,))
                if i == 9:
                    split_lo(U_OUT + 3, slot_in(U_OUT + 3)[0])
                if ADA_ITEM <= i < ADA_ITEM + KC:
                    ada_step()
                if i == ADA_ITEM + KC + 1:
                    dve.wait_ge(ada_kept, 1)
                    mod_block(5, adac[:])
                if i % 4 == 3 and i > 10:
                    keep_o_lo(i // 4 - 2)
            keep_o_lo(HEADS - 2)
            keep_o_lo(HEADS - 1)

            def gate_diag():
                dve.wait_ge(mod_add, 2)
                nc.vector.tensor_tensor(gain[:, 2, :], modc[:, 32:48], g_mix_post, ALU.mult).then_inc(mods, 1)
                dve.wait_ge(mods, 9)
                for k in range(KC):
                    ins = nc.vector.tensor_scalar(diag[:, k, :], ident[:], gain[:, 2, k:k + 1], None, ALU.mult)
                    if k % 4 == 3:
                        ins.then_inc(g_diag, 1)

            def y_job(j):
                dve.wait_ge(unit_used, U_OUT + 4 * j + 4)
                for s in range(2):
                    nc.vector.tensor_copy(ytok[:, 2 * s:2 * s + 2, UCOLS * j:UCOLS * j + UCOLS],
                                          PS[:, 2 * (j % 3) + s, :].rearrange("p (t n) -> p t n", t=2))\
                        .then_inc(bank_dve, 1)

            def y_gate(j):
                dve.wait_ge(y_sq, NQB * j + NQB)
                dve.wait_ge(g_kept, j // 2 + 1)
                y = ytok[:, :, UCOLS * j:UCOLS * j + UCOLS]
                g = grow[:, UCOLS * j:UCOLS * j + UCOLS].unsqueeze(1).broadcast_to([P, NQB, UCOLS])
                nc.vector.tensor_tensor(y, y, g, ALU.mult).then_inc(y_gated, 1)

            gate_diag()
            for u in range(U_OUT + 4, U_FFN + 4):
                e = u - 3
                if (e - U_OUT) % 4 == 0:
                    y_job((e - U_OUT) // 4 - 1)
                if (e - U_OUT) % 4 == 2 and e > U_OUT + 4:
                    y_gate((e - U_OUT) // 4 - 1)
                for _ in range(ada_steps(u)):
                    ada_step()
                if u == U_OUT + 29:
                    mod_block(7)
                if u < U_FFN + 3:
                    split_lo(u, slot_in(u)[0] if u < U_FFN else u - U_FFN)
            dve.wait_ge(mod_add, 8)
            nc.vector.scalar_tensor_tensor(gain[:, 3, :], modc[:, 64:80], 1.0, g_ffn_pre, ALU.add, ALU.mult)\
                .then_inc(mods, 1)
            nc.vector.tensor_tensor(gain[:, 4, :], modc[:, 80:96], g_ffn_post, ALU.mult).then_inc(mods, 1)

            dve.wait_ge(y_sq, NQB * OUT_JOBS)
            link(nc.vector.tensor_reduce(tss[:, 0, 0, :], yss[:, :, :], AX.X, ALU.add))
            rsqrt_head(4, tss[:, 0, 1, :], tss[:, 0, 0, :], D)
            y_gate(OUT_JOBS - 1)
            rsqrt_tail(4, tss[:, 0, 1, :], tss[:, 0, 2, :], tss[:, 0, 3, :])
            dve.wait_ge(y_gated, OUT_JOBS)
            dve.wait_ge(x2_in, 16 * NQB)
            for t in range(NQB):
                nc.vector.scalar_tensor_tensor(ytok[:, t, :], ytok[:, t, :], tss[:, 0, 2, t:t + 1], xtok2[:, t, :],
                                               ALU.mult, ALU.add).then_inc(x1_done, 1)
            split_lo(U_FFN + 3, 3)
            dve.wait_ge(x1_sq, NQB)
            rsqrt_head(5, tss[:, 1, 1, :], tss[:, 1, 0, :], D)
            rsqrt_tail(5, tss[:, 1, 1, :], tss[:, 1, 2, :], tss[:, 1, 3, :])
            for f in (slice(0, D // 2), slice(D // 2, D)):
                for t in range(3):
                    nc.vector.tensor_scalar(xh[:, t, f], ytok[:, t, f], tss[:, 1, 2, t:t + 1], None, ALU.mult)\
                        .then_inc(xh_dve, 1)
            for j in range(KC):
                dve.wait_ge(h2_hi, j + 1)
                nc.vector.tensor_tensor(hlo[:, j, :], h2t[:, j % 3, :], hhi[:, j, :].bitcast(F32), ALU.subtract)\
                    .then_inc(h2_lo, 1)

            def f_sums(d):
                for s in range(2):
                    n = 2 * d + s
                    dve.wait_ge(f_sq, n + 1)
                    if n == 0:
                        nc.vector.tensor_copy(fsum[:], tsq[:, 0, :]).then_inc(f_sqsum, 1)
                    else:
                        dve.wait_ge(f_sqsum, n)
                        nc.vector.tensor_tensor(fsum[:], fsum[:], tsq[:, s, :], ALU.add)\
                            .then_inc(f_sqsum, 1)

            def keep_f(c):
                dve.wait_ge(f_turned, c + 1)
                for t in (2, 3):
                    nc.vector.tensor_copy(facc_tok[:, c, t, :], PS[:, 4 + t, :]).then_inc(f_kept_dve, 1)

            def ffn(g, last):
                for r in range(GROUP_UNITS):
                    if r in (7, 15):
                        half = r // 8
                        dve.wait_ge(unit_used, U_FFN + 1 + r + GROUP_UNITS * g)
                        for s in range(2):
                            dve.wait_ge(gate_done, 4 * g + 2 * half + s + 1)
                            nc.vector.tensor_tensor(sg[:, s, :], PS[:, 2 + s, :], sg[:, s, :], ALU.mult)\
                                .then_inc(hid_done, 1)
                        for s in range(2):
                            dve.wait_ge(hid_hi, 4 * g + 2 * half + s + 1)
                            nc.vector.tensor_tensor(hidlo[:, 2 * half + s, :], sg[:, s, :],
                                                    hidhi[:, 2 * half + s, :].bitcast(F32), ALU.subtract)\
                                .then_inc(hid_lo, 1)
                    if r >= 16:
                        d = r - 16
                        if d == 0:
                            dve.wait_ge(facc_zero, 1)
                        dve.wait_ge(unit_used, U_FFN + 1 + r + GROUP_UNITS * g)
                        for s in range(2):
                            y = facc[:, 2 * d + s, :]
                            nc.vector.tensor_tensor(y, PS[:, 2 * (d % 2) + s, :], y, ALU.add)\
                                .then_inc(facc_done, 1)
                        if last and d:
                            f_sums(d - 1)
                        if last and d in TURN_F:
                            keep_f(TURN_F.index(d))
                    if not (last and r >= GROUP_UNITS - RING):
                        dve.wait_ge(hi_ready, U_FFN + RING + 1 + r + GROUP_UNITS * g)
                        nc.vector.tensor_tensor(wlo[:, r % RING, :], stage[:, r % RING, :],
                                                whi[:, r % RING, :].bitcast(F32), ALU.subtract).then_inc(lo_ready, 1)

            with dve.Fori(0, GROUPS - 1) as g:
                ffn(g, False)
            ffn(GROUPS - 1, True)

            f_sums(7)
            dve.wait_ge(f_stat, 1)
            rsqrt_head(6, tss[:, 2, 1, :], PS[:, 0, 0:NQB], D)
            rsqrt_tail(6, tss[:, 2, 1, :], tss[:, 2, 2, :], tss[:, 2, 3, :])
            dve.wait_ge(f_kept_act, 6)
            dve.wait_ge(f_kept_dve, 6)
            for t in range(NQB):
                r1 = tss[:, 2, 2, t:t + 1]
                x1 = ytok[:, t, :]
                if t < 3:
                    nc.vector.scalar_tensor_tensor(otok[:, t, 0:1536].rearrange("p (c n) -> p c n", c=3),
                                                   facc_tok[:, 0:3, t, :], r1,
                                                   x1[:, 0:1536].rearrange("p (c n) -> p c n", c=3),
                                                   ALU.mult, ALU.add).then_inc(o_made, 1)
                if t == 0:
                    dve.wait_ge(f_turned, 4)
                nc.vector.scalar_tensor_tensor(otok[:, t, 1536:D], PS[:, 4 + t, :], r1, x1[:, 1536:D],
                                               ALU.mult, ALU.add).then_inc(o_made, 1)

        @block.tensor
        def _(pe):
            mm = nc.tensor.matmul

            def three(dst, w, x, start, stop):
                (w_hi, w_lo), (x_hi, x_lo) = w, x
                mm(dst, w_hi, x_hi, start=start, stop=False)
                mm(dst, w_hi, x_lo, start=False, stop=False)
                return mm(dst, w_lo, x_hi, start=False, stop=stop)

            def wt(slot, k, s):
                n = slot * UNIT + k * UCOLS + s * P
                return (whi[:, :, :].rearrange("p r n -> p (r n)")[:, n:n + P],
                        wlo[:, :, :].rearrange("p r n -> p (r n)")[:, n:n + P])

            pe.wait_ge(first_in, 16 * N_FIRST)
            nc.tensor.transpose(PS[:, 7, 0:128], rows[:, 0, :], ident[:]).then_inc(rows_turned, 1)

            def turn_rows(b):
                pe.wait_ge(row_kept, b + 1)
                if b == 2:
                    pe.wait_ge(mods, 2)
                for q in range(8):
                    n = 4 * (8 * ADA0_BLOCKS[b] + q)
                    last = nc.tensor.transpose(PS[:, 6, n:n + 4], row4[:, P * q:P * q + P], ident[0:4, 0:4])
                last.then_inc(row_turned, 1)

            def turn_x(g):
                c, t = divmod(g, 6)
                pe.wait_ge(xhat, t + 1)
                if g >= 2:
                    pe.wait_ge(x_kept, g - 1)
                for i in range(4):
                    n = P * (4 * c + i)
                    last = nc.tensor.transpose(PS[:, 4 + g % 2, P * i:P * i + P], xtok[:, t, n:n + P], ident[:])
                last.then_inc(x_turned, 1)

            def k_chunk(k, w, first):
                if first and k < 8:
                    pe.wait_ge(h_lo_pool, 2 * k + 2)
                elif first:
                    pe.wait_ge(h_lo, 2 * (k - 8) + 2)
                for s in range(2):
                    three(PS[:, s, :], w(s), (hhi[:, k, :], hlo[:, k, :]), k == 0, k == KC - 1)
                    last = three(PS[:, 2, CTX * s:CTX * s + CTX], w(s), (chi[:, k, :], clo[:, k, :]),
                                 (k, s) == (0, 0), (k, s) == (KC - 1, 1))
                return last

            def k_unit(b, q, first):
                u = U_IN + 8 * b + q
                pe.wait_ge(lo_ready, u + 1)
                for i in range(UCH):
                    last = k_chunk(UCH * q + i, lambda s: wt(ring(u), i, s), first)
                last.then_inc(unit_used, 1)

            def early_chunk(k):
                q, i = divmod(k, UCH)
                if i == 0:
                    pe.wait_ge(early_lo, q + 1)
                    pe.wait_ge(row_kept, 3)

                def w(s):
                    n = UCOLS * i + P * s
                    return khi[:, q, n:n + P], klo[:, q, n:n + P]

                last = k_chunk(k, w, True)
                if k == 7:
                    last.then_inc(early_used, 1)

            pe.wait_ge(silp_ready, 2)
            for u in range(FIRST):
                b, k = divmod(u, KC)
                bank = ADA0_BANK[b]
                if (b, k) == (2, 0):
                    pe.wait_ge(row_kept, 1)
                if (b, k) == (3, 0):
                    pe.wait_ge(x_kept, 24)
                pe.wait_ge(lo_ready, u + 1)
                c4 = silp[:, 4 * k:4 * k + P]
                for s in range(2):
                    mm(PS[:, bank + s, :], c4, whi[:, ring(u), 512 * s:512 * s + 512], start=(k == 0), stop=False)
                    last = mm(PS[:, bank + s, :], c4, wlo[:, ring(u), 512 * s:512 * s + 512],
                              start=False, stop=(k == KC - 1))
                last.then_inc(unit_used, 1)
                if u in EARLY_PIECES:
                    early_chunk(EARLY_PIECES.index(u))
                if u == X_TURN - 2:
                    pe.wait_ge(const_in, 16 * N_CONST)
                    pe.wait_ge(cols_ready, 1)
                    nc.tensor.transpose(PS[:, 7, 128:208], rows[0:80, 1, :], ident[0:80, 0:80]).then_inc(rows_turned, 1)
                if X_TURN <= u < X_TURN + 24:
                    turn_x(u - X_TURN)
                if u in (21, 37, 53):
                    turn_rows((u - 21) // 16)
            early_chunk(5)
            turn_rows(3)
            early_chunk(6)
            early_chunk(7)

            def ada_reduce(b, bank=6, col=0):
                pe.wait_ge(ada_used, 16 * b + 16)
                pe.wait_ge(mod_add, b)
                for q in range(8):
                    last = mm(PS[:, bank, col + q:col + q + 1], acc[:, P * q:P * q + P], ones[:, 0:1],
                              start=True, stop=True)
                last.then_inc(ada_sum, 1)

            def k_sum(s):
                pe.wait_ge(ksq, s + 1)
                if s:
                    pe.wait_ge(rms, RSQRT_STEPS + 1)
                mm(PS[:, 6, :], ones[:], ktmp[:, 2 + s, 0:SEQ], start=True, stop=True)
                mm(PS[:, 7, 0:CTX], ones[:], ktmp[:, 2 + s, SEQ:TOK], start=True, stop=True).then_inc(kstat, 1)

            def v_units(b):
                for q in range(4):
                    u = U_IN + 8 * b + 4 + q
                    pe.wait_ge(lo_ready, u + 1)
                    for i in range(UCH):
                        k = UCH * q + i
                        w = (whi[:, ring(u), UCOLS * i:UCOLS * i + UCOLS],
                             wlo[:, ring(u), UCOLS * i:UCOLS * i + UCOLS])
                        for t in range(6):
                            if t < 4:
                                x = (hhi[:, k, P * t:P * t + P], hlo[:, k, P * t:P * t + P])
                            else:
                                x = (chi[:, k, P * (t - 4):P * (t - 3)], clo[:, k, P * (t - 4):P * (t - 3)])
                            last = three(PS[:, 3 + t // 2, UCOLS * (t % 2):UCOLS * (t % 2) + UCOLS], x, w,
                                         k == 0 and t % 2 == 0, k == KC - 1 and t % 2 == 1)
                    last.then_inc(unit_used, 1)
                    if b == 0 and q in (1, 2):
                        k_sum(q - 1)
                    if (b, q) == (1, 1):
                        pe.wait_ge(rms, 2 * RSQRT_STEPS + 1)
                        ada_reduce(0)

            def banks_empty(n_act, n_dve):
                pe.wait_ge(bank_act, n_act)
                pe.wait_ge(bank_dve, n_dve)

            for q in (2, 3):
                k_unit(0, q, True)
            v_units(0)
            banks_empty(2, 1)
            for q in range(4):
                k_unit(1, q, False)
            banks_empty(4, 2)
            v_units(1)
            banks_empty(8, 4)

            def product(banks, slot, q, first, last_, x=(hhi, hlo), chunk_ready=None):
                for i in range(UCH):
                    k = UCH * q + i
                    if chunk_ready:
                        chunk_ready(k)
                    for s in range(2):
                        last = three(PS[:, banks + s, :], wt(slot, i, s), (x[0][:, k, :], x[1][:, k, :]),
                                     first and i == 0, last_ and i == UCH - 1)
                return last

            def q_sum(j):
                pe.wait_ge(qsq_made, 2 * j + 2)
                for s in range(2):
                    for n in range(NQB):
                        c = NQB * (2 * j + s) + n
                        last = mm(PS[:, 7, c:c + 1], qsq[:, s, P * n:P * n + P], ones[:, 0:1], start=True, stop=True)
                last.then_inc(qsum, 1)

            def scores(i):
                h, n = divmod(i, NQB)
                kv = h // GROUP
                lo, w = key_window(i)
                if n == 0:
                    pe.wait_ge(qdone, h + 1)
                if i >= 2:
                    pe.wait_ge(p_done, i - 1)
                s0 = 1024 * (i % 2)
                qb = qT[:, h, P * n:P * n + P]
                mm(psf[:, s0 + 512 - w:s0 + 512], qb, kT[:, kv, lo:lo + w], start=True, stop=True)
                mm(psf[:, s0 + 512:s0 + TOK], qb, kT[:, kv, SEQ:TOK], start=True, stop=True).then_inc(s_done, 1)

            def turn(i):
                lo, w = key_window(i)
                pe.wait_ge(pn_done, i + 1)
                if i:
                    pe.wait_ge(pt_kept, i)
                else:
                    pe.wait_ge(bank_act, 8 + 2 * (CONV_JOBS + Q_JOBS))
                if i == ADA_ITEM + KC - LAG:
                    ada_reduce(5, 5, CTX)
                for k in range(w // P):
                    s = 512 - w + P * k
                    n = 2048 + lo + P * k
                    nc.tensor.transpose(psf[:, n:n + P], prob[i % 3][:, s:s + P], ident[:])
                for k in range(2):
                    s = SEQ + P * k
                    last = nc.tensor.transpose(PS[:, 5, P * k:P * k + P], prob[i % 3][:, s:s + P], ident[:])
                last.then_inc(pt_turned, 1)

            def values(h, keys):
                kv = h // GROUP
                if 4 in keys:
                    pe.wait_ge(pt_kept, 4 * h + 4)
                    if h == 0:
                        pe.wait_ge(mod_add, 5)
                    if h >= 2:
                        pe.wait_ge(o_lo, 4 + h - 1)
                o = PS[:, 6 + h % 2, :]
                for k in keys:
                    every = h < A_HEADS or k >= 4
                    q0, q1 = (0, SEQ) if every else (P * max(k - 1, 0), P * min(k + 2, NQB))
                    last = mm(o[:, q0:q1], vv[:, k, P * kv:P * kv + P], pt[:, h % 2, k, q0:q1], start=(k == 4),
                              stop=(k == 3))
                if 3 in keys:
                    last.then_inc(o_done, 1)

            def q_units(i3, sums, attend=False):
                for r in range(3):
                    pe.wait_ge(bank_act, 4 + 2 * r + 6 * i3)
                    for q in range(4):
                        n = 4 * r + q
                        pe.wait_ge(lo_ready, U_C + 1 + n + 12 * i3)
                        if attend and n == 11:
                            pe.wait_ge(bank_act, 8 + 2 * (CONV_JOBS + Q_JOBS - 1))
                            pe.wait_ge(rms, 3 * RSQRT_STEPS + 1)
                            scores(0)
                            scores(1)
                        product(2 * r, n % RING, q, q == 0, q == 3).then_inc(unit_used, 1)
                        if n == 9:
                            ada_reduce(1 + i3)
                        if n in sums:
                            q_sum(sums[n])

            with pe.Fori(0, 2) as i3:
                q_units(i3, {})
            q_units(2, {6: 0, 10: 1})
            q_units(3, {2: 2}, True)

            pe.wait_ge(bank_act, 8 + 2 * (CONV_JOBS + Q_JOBS - 1))
            pe.wait_ge(rms, 3 * RSQRT_STEPS + 1)

            def out_unit(banks, q):
                k0 = UCH * OUT_ORDER[q]
                for i in range(UCH):
                    k = k0 + i
                    w = (whi[:, q, UCOLS * i:UCOLS * i + UCOLS], wlo[:, q, UCOLS * i:UCOLS * i + UCOLS])
                    for t in range(NQB):
                        o = (hhi[:, k, P * t:P * t + P], hlo[:, k, P * t:P * t + P])
                        last = three(PS[:, banks + t // 2, UCOLS * (t % 2):UCOLS * (t % 2) + UCOLS], o, w,
                                     (q, i, t % 2) == (0, 0, 0), (q, i, t % 2) == (3, UCH - 1, 1))
                last.then_inc(unit_used, 1)

            def first_out_unit(q, chunks):
                pe.wait_ge(lo_ready, U_OUT + 1 + q)
                pe.wait_ge(o_lo, chunks)
                out_unit(0, q)

            def gate_row(c):
                pe.wait_ge(g_diag, c + 1)
                if c >= 2:
                    pe.wait_ge(g_kept, c - 1)
                for i in range(4):
                    last = mm(PS[:, 6 + c % 2, P * i:P * i + P], ones[:], diag[:, 4 * c + i, :], start=True, stop=True)
                last.then_inc(g_row, 1)

            for i in range(4 * HEADS + LAG):
                if 2 <= i < 4 * HEADS:
                    scores(i)
                if i >= 7 and i % 4 != 2:
                    h, part = divmod(i - 7, 4)
                    values(h, ((4, 5), (0, 1), (2, 3))[part])
                if i == 4 * HEADS + 1:
                    pe.wait_ge(p_done, 4 * HEADS)
                    first_out_unit(0, 4 + 4)
                if i >= LAG:
                    turn(i - LAG)
            first_out_unit(1, 4 + 4)
            values(HEADS - 1, (4, 5, 0, 1, 2, 3))
            first_out_unit(2, 4 + 8)
            first_out_unit(3, 4 + HEADS)
            gate_row(0)
            gate_row(1)
            gate_row(2)
            gate_row(3)
            pe.wait_ge(g_kept, 4)
            pe.wait_ge(pt_kept, 4 * HEADS)
            with pe.Fori(0, 2) as i3:
                for r in range(3):
                    if r == 2:
                        pe.wait_ge(bank_dve, 4 + 2 + 6 * i3)
                    for q in range(4):
                        pe.wait_ge(lo_ready, U_OUT + 5 + 4 * r + q + 12 * i3)
                        out_unit(2 * ((r + 1) % 3), q)
                    if r == 2:
                        ada_reduce(6 + i3)
            for q in range(4):
                pe.wait_ge(lo_ready, U_FFN - 3 + q)
                out_unit(2, q)

            def turn_x1(j):
                if j % 8 == 0:
                    pe.wait_ge(xh_dve, 3 * (j // 8) + 3)
                    pe.wait_ge(xh_act, j // 8 + 1)
                if j >= 2:
                    pe.wait_ge(h2_t, j - 1)
                for t in range(NQB):
                    last = nc.tensor.transpose(PS[:, 4 + j % 2, P * t:P * t + P], xh[:, t, P * j:P * j + P], ident[:])
                last.then_inc(h2_turned, 1)

            def h2_chunk(j):
                if j + 2 < KC:
                    turn_x1(j + 2)
                pe.wait_ge(h2_lo, j + 1)

            turn_x1(0)
            turn_x1(1)

            def turn_f(c):
                pe.wait_ge(f_scaled, 4 * c + 4)
                if c:
                    pe.wait_ge(f_kept_act, 2 * c)
                    pe.wait_ge(f_kept_dve, 2 * c)
                for t in range(NQB):
                    for i in range(4):
                        last = nc.tensor.transpose(PS[:, 4 + t, P * i:P * i + P],
                                                   facc[:, 4 * c + i, P * t:P * t + P], ident[:])
                last.then_inc(f_turned, 1)

            def ffn(g, first=False, last=False):
                r = 0
                for job in range(4):
                    if job < 2:
                        if not first:
                            pe.wait_ge(facc_done, 16 * g - 2 + 2 * job)
                    elif job == 2:
                        pe.wait_ge(gate_done, 2 + 4 * g)
                    else:
                        pe.wait_ge(hid_done, 2 + 4 * g)
                    for q in range(4):
                        pe.wait_ge(lo_ready, U_FFN + 1 + r + GROUP_UNITS * g)
                        product(2 * (job % 2), r % RING, q, q == 0, q == 3, (hhi, hlo),
                                h2_chunk if first and job == 0 else None).then_inc(unit_used, 1)
                        r += 1
                for d in range(8):
                    if d == 0:
                        pe.wait_ge(gate_done, 4 + 4 * g)
                    elif d >= 2:
                        pe.wait_ge(facc_done, 2 * (d - 1) + 16 * g)
                    pe.wait_ge(lo_ready, U_FFN + 1 + r + GROUP_UNITS * g)
                    product(2 * (d % 2), r % RING, 0, True, True, (hidhi, hidlo),
                            (lambda i: pe.wait_ge(hid_lo, 1 + i + 4 * g)) if d == 0 else None).then_inc(unit_used, 1)
                    r += 1
                    if last and d in TURN_F:
                        turn_f(TURN_F.index(d))

            pe.wait_ge(bank_dve, 4 + 2 * OUT_JOBS)
            ffn(0, first=True)
            with pe.Fori(1, GROUPS - 1) as g:
                ffn(g)
            ffn(GROUPS - 1, last=True)

            pe.wait_ge(f_sqsum, KC)
            for t in range(NQB):
                last = mm(PS[:, 0, t:t + 1], fsum[:, P * t:P * t + P], ones[:, 0:1], start=True, stop=True)
            last.then_inc(f_stat, 1)
            turn_f(3)


def shape_constants():
    import numpy as np

    grid_w, pairs = 64, P // 4
    inv = np.power(10000.0, -np.arange(pairs) / pairs).astype(np.float32)
    t = np.arange(SEQ)
    place = (t // grid_w, t % grid_w)
    cos, sin = np.zeros((P, SEQ), np.float32), np.zeros((P, SEQ), np.float32)
    for p in range(P):
        axis, half, i = p // 64, (p // 32) % 2, p % 32
        angle = place[axis].astype(np.float32) * inv[i]
        cos[p] = np.cos(angle.astype(np.float64))
        sin[p] = np.sin(angle.astype(np.float64)) * (1 if half else -1)
    q, k = np.arange(P)[:, None], np.arange(P)[None, :]
    return {
        "ident": np.eye(P, dtype=np.float32), "rope_cos": cos, "rope_sin": sin,
        "mask_left": np.where(k >= q, 0, NEG).astype(np.float32),
        "mask_right": np.where(k <= q, 0, NEG).astype(np.float32),
    }


_INS = ["x", "c", "ctx", "c_ctx", "w_ada", "b_ada", "g_mix_pre", "g_mix_post", "g_ffn_pre", "g_ffn_post",
        "w_in", "q_norm", "k_norm", "sink", "conv_w", "w_out", "w_gate", "w_up", "w_down"]


def kernel(**inputs):
    import concourse.bacc as bacc
    import numpy as np
    from concourse.bass_utils import run_bass_kernel_spmd

    nc = bacc.Bacc("TRN2", target_bir_lowering=False, num_devices=1)
    arrays, args = {}, {}
    given = {name: np.ascontiguousarray(inputs[name]) for name in _INS}
    given.update(shape_constants())
    for name, v in given.items():
        arrays[f"in_{name}"] = v
        ap = nc.dram_tensor(f"in_{name}", v.shape, mybir.dt.from_np(v.dtype), kind="ExternalInput").ap()
        if name in _INS and name not in ("c", "c_ctx"):
            ap = ap[0]
        args[name] = ap
    out = nc.dram_tensor("out", (1, SEQ, D), F32, kind="ExternalOutput").ap()
    hybrid_block(nc, args, out[0])
    r = run_bass_kernel_spmd(nc, [arrays], core_ids=[0])
    return r.results[0]["out"]
```
